# Optimizing a Trainium2 kernel written in Bass

```python
import jax, jax.numpy as jnp
from jax import lax
import numpy as np

D_MODEL = 1024
BATCH = 1
SEQ = 512
DEPTH = 1

CHUNK = 64
D_MIX = D_MODEL
HEAD_DIM = 64
ATT_WIDTH = 3 * D_MIX // 8
ATT_HEADS = ATT_WIDTH // HEAD_DIM
ATT_PAST_CHUNKS = 8
ATT_BAND = (ATT_PAST_CHUNKS + 1) * CHUNK
REL_CLIP = 128
ML_WIDTH = 3 * D_MIX // 8
ML_HEADS = ML_WIDTH // HEAD_DIM
CONV_WIDTH = 4
GLA_WIDTH = D_MIX - ATT_WIDTH - ML_WIDTH
GLA_HEADS = 4
GLA_DV = GLA_WIDTH // GLA_HEADS
GLA_DK = GLA_DV // 2
GLA_KW = GLA_HEADS * GLA_DK
GLA_RANK = 16
GLA_TAU = 16.0
IN_SPLITS = (ATT_WIDTH, ATT_WIDTH, ATT_WIDTH, ATT_WIDTH,
             ML_WIDTH, ML_WIDTH, ML_WIDTH, ML_WIDTH, ML_HEADS, ML_HEADS, ML_WIDTH,
             GLA_KW, GLA_KW, GLA_WIDTH, GLA_RANK, GLA_WIDTH)
D_IN = sum(IN_SPLITS)
EPS = 1e-6
NEG = -1e30


def rmsnorm(x, g):
    xf = x.astype(jnp.float32)
    y = xf * lax.rsqrt(jnp.mean(xf * xf, axis=-1, keepdims=True) + EPS)
    return (y * g.astype(jnp.float32)).astype(x.dtype)

def head_rmsnorm(x, g, n_heads):
    b, s, w = x.shape
    y = rmsnorm(x.reshape(b, s, n_heads, w // n_heads), g.reshape(n_heads, w // n_heads))
    return y.reshape(b, s, w)

def causal_conv(x, w):
    k_w = w.shape[0]
    s = x.shape[1]
    xp = jnp.pad(x, ((0, 0), (k_w - 1, 0), (0, 0)))
    return sum(xp[:, j:j + s] * w[j] for j in range(k_w))

def band_chunk_attention(q, k, v, rel_bias):
    bsz, s, h, d = q.shape
    nc = s // CHUNK
    pad = ATT_PAST_CHUNKS * CHUNK
    qc = q.reshape(bsz, nc, CHUNK, h, d)
    kp = jnp.pad(k, ((0, 0), (pad, 0), (0, 0), (0, 0))).reshape(bsz, nc + ATT_PAST_CHUNKS, CHUNK, h, d)
    vp = jnp.pad(v, ((0, 0), (pad, 0), (0, 0), (0, 0))).reshape(bsz, nc + ATT_PAST_CHUNKS, CHUNK, h, d)
    kb = jnp.concatenate([kp[:, m:m + nc] for m in range(ATT_PAST_CHUNKS + 1)], axis=2)
    vb = jnp.concatenate([vp[:, m:m + nc] for m in range(ATT_PAST_CHUNKS + 1)], axis=2)
    scores = jnp.einsum('bnqhd,bnkhd->bnhqk', qc, kb).astype(jnp.float32) * (d ** -0.5)
    rel = jnp.arange(CHUNK)[:, None] + pad - jnp.arange(ATT_BAND)[None, :]
    bias = rel_bias[:, jnp.clip(rel, -REL_CLIP, REL_CLIP) + REL_CLIP].astype(jnp.float32)
    kpos = (jnp.arange(nc)[:, None] - ATT_PAST_CHUNKS) * CHUNK + jnp.arange(ATT_BAND)[None, :]
    valid = kpos >= 0
    scores = jnp.where(valid[None, :, None, None, :], scores + bias[None, None], NEG)
    p = jax.nn.softmax(scores, axis=-1).astype(v.dtype)
    o = jnp.einsum('bnhqk,bnkhd->bnqhd', p, vb)
    return o.reshape(bsz, s, h * d)

def mlstm_chunkwise(q, k, v, i_pre, f_pre):
    bsz, s, h, d = q.shape
    nc = s // CHUNK
    L = CHUNK
    dt = q.dtype
    qc = q.astype(jnp.float32).reshape(bsz, nc, L, h, d)
    kc = (k.astype(jnp.float32) * (d ** -0.5)).reshape(bsz, nc, L, h, d)
    vc = v.astype(jnp.float32).reshape(bsz, nc, L, h, d)
    ig = i_pre.astype(jnp.float32).reshape(bsz, nc, L, h).transpose(0, 1, 3, 2)
    lf = jax.nn.log_sigmoid(f_pre.astype(jnp.float32)).reshape(bsz, nc, L, h).transpose(0, 1, 3, 2)
    bcum = jnp.cumsum(lf, axis=-1)
    g = bcum[..., -1]
    a = g[..., None] - bcum + ig
    m_loc = jnp.max(a, axis=-1)
    w = jnp.exp(a - m_loc[..., None])
    c_loc = jnp.einsum('bnhj,bnjhv,bnjhk->bnhvk', w, vc, kc)
    n_loc = jnp.einsum('bnhj,bnjhk->bnhk', w, kc)

    def step(carry, xs):
        c_st, n_st, m_st = carry
        g_c, m_l, c_l, n_l = xs
        m_new = jnp.maximum(g_c + m_st, m_l)
        s_old = jnp.exp(g_c + m_st - m_new)
        s_new = jnp.exp(m_l - m_new)
        c_new = s_old[..., None, None] * c_st + s_new[..., None, None] * c_l
        n_new = s_old[..., None] * n_st + s_new[..., None] * n_l
        return (c_new, n_new, m_new), (c_st, n_st, m_st)

    init = (jnp.zeros((bsz, h, d, d), jnp.float32), jnp.zeros((bsz, h, d), jnp.float32),
            jnp.zeros((bsz, h), jnp.float32))
    xs = (jnp.moveaxis(g, 1, 0), jnp.moveaxis(m_loc, 1, 0), jnp.moveaxis(c_loc, 1, 0), jnp.moveaxis(n_loc, 1, 0))
    _, (c_prev, n_prev, m_prev) = lax.scan(step, init, xs)
    c_prev = jnp.moveaxis(c_prev, 0, 1)
    n_prev = jnp.moveaxis(n_prev, 0, 1)
    m_prev = jnp.moveaxis(m_prev, 0, 1)

    causal = jnp.tril(jnp.ones((L, L), dtype=bool))
    log_d = jnp.where(causal, bcum[..., :, None] - bcum[..., None, :] + ig[..., None, :], NEG)
    inter_log = bcum + m_prev[..., None]
    m_row = jnp.maximum(inter_log, jnp.max(log_d, axis=-1))
    d_mat = jnp.exp(log_d - m_row[..., None])
    inter_w = jnp.exp(inter_log - m_row)
    sc = jnp.einsum('bnthd,bnjhd->bnhtj', qc, kc) * d_mat
    num = jnp.einsum('bnhtj,bnjhv->bnthv', sc, vc) + \
        inter_w.transpose(0, 1, 3, 2)[..., None] * jnp.einsum('bnhvk,bnthk->bnthv', c_prev, qc)
    den = jnp.sum(sc, axis=-1) + inter_w * jnp.einsum('bnhk,bnthk->bnht', n_prev, qc)
    den = jnp.maximum(jnp.abs(den), jnp.exp(-m_row))
    out = num / den.transpose(0, 1, 3, 2)[..., None]
    return out.reshape(bsz, s, h * d).astype(dt)

def gla_chunkwise(q, k, v, log_alpha):
    bsz, s, h, dk = q.shape
    dv = v.shape[-1]
    nc = s // CHUNK
    L = CHUNK
    dt = q.dtype

    def to_chunks(t):
        return jnp.moveaxis(t.astype(jnp.float32).reshape(bsz, nc, L, h, t.shape[-1]), 1, 0)

    xs = (to_chunks(q * (dk ** -0.5)), to_chunks(k), to_chunks(v), to_chunks(log_alpha))
    causal = jnp.tril(jnp.ones((L, L), dtype=bool))

    def step(state, chunk):
        qx, kx, vx, la = chunk
        bcum = jnp.cumsum(la, axis=1)
        diff = bcum[:, :, None] - bcum[:, None, :]
        decay = jnp.where(causal[None, :, :, None, None], jnp.exp(jnp.minimum(diff, 0.0)), 0.0)
        att = jnp.einsum('bthd,bjhd,btjhd->bhtj', qx, kx, decay)
        o_intra = jnp.einsum('bhtj,bjhv->bthv', att, vx)
        o_inter = jnp.einsum('bthd,bhdv->bthv', qx * jnp.exp(bcum), state)
        btot = bcum[:, -1]
        k_dec = kx * jnp.exp(btot[:, None] - bcum)
        state_new = jnp.exp(btot)[..., None] * state + jnp.einsum('bjhd,bjhv->bhdv', k_dec, vx)
        return state_new, o_intra + o_inter

    _, o = lax.scan(step, jnp.zeros((bsz, h, dk, dv), jnp.float32), xs)
    return jnp.moveaxis(o, 0, 1).reshape(bsz, s, h * dv).astype(dt)

def hybrid_layer(x, norm_g, w_in, b_gates, conv_w, w_alpha, b_alpha, rel_bias, ml_norm_g, gla_norm_g, w_out):
    bsz, s, _ = x.shape
    hn = rmsnorm(x, norm_g)
    z = jnp.einsum('bsd,de->bse', hn, w_in)
    split_idx = [int(i) for i in np.cumsum(IN_SPLITS)[:-1]]
    (aq, ak, av, ag, mq, mk, mv, mo, mi, mf, mg, gq, gk, gv, ga, gg) = jnp.split(z, split_idx, axis=-1)

    att = band_chunk_attention(aq.reshape(bsz, s, ATT_HEADS, HEAD_DIM), ak.reshape(bsz, s, ATT_HEADS, HEAD_DIM),
                               av.reshape(bsz, s, ATT_HEADS, HEAD_DIM), rel_bias)
    y_a = att * jax.nn.silu(ag)

    qk = jax.nn.silu(causal_conv(jnp.concatenate([mq, mk], axis=-1), conv_w))
    mq_c, mk_c = qk[..., :ML_WIDTH], qk[..., ML_WIDTH:]
    h_ml = mlstm_chunkwise(mq_c.reshape(bsz, s, ML_HEADS, HEAD_DIM), mk_c.reshape(bsz, s, ML_HEADS, HEAD_DIM),
                           mv.reshape(bsz, s, ML_HEADS, HEAD_DIM),
                           mi + b_gates[:ML_HEADS], mf + b_gates[ML_HEADS:])
    y_b = jax.nn.sigmoid(mo) * head_rmsnorm(h_ml, ml_norm_g, ML_HEADS) * jax.nn.silu(mg)

    log_alpha = jax.nn.log_sigmoid((jnp.einsum('bsr,rk->bsk', ga, w_alpha) + b_alpha).astype(jnp.float32)) / GLA_TAU
    h_gla = gla_chunkwise(gq.reshape(bsz, s, GLA_HEADS, GLA_DK), gk.reshape(bsz, s, GLA_HEADS, GLA_DK),
                          gv.reshape(bsz, s, GLA_HEADS, GLA_DV), log_alpha.reshape(bsz, s, GLA_HEADS, GLA_DK))
    y_c = head_rmsnorm(h_gla, gla_norm_g, GLA_HEADS) * jax.nn.silu(gg)

    y = jnp.concatenate([y_a, y_b, y_c], axis=-1)
    return x + jnp.einsum('bse,ed->bsd', y, w_out)

def first_inputs(seed: int = 0) -> dict:
    key = jax.random.key(seed)
    ks = jax.random.split(key, 12)
    f32 = jnp.float32
    x = jax.random.normal(ks[0], (BATCH, SEQ, D_MODEL), f32)
    norm_g = 1.0 + 0.1 * jax.random.normal(ks[1], (DEPTH, D_MODEL), f32)
    w_in = jax.random.normal(ks[2], (DEPTH, D_MODEL, D_IN), f32) * D_MODEL ** -0.5
    f_bias = jnp.broadcast_to(jnp.linspace(3.0, 6.0, ML_HEADS, dtype=f32), (DEPTH, ML_HEADS))
    i_bias = 0.1 * jax.random.normal(ks[3], (DEPTH, ML_HEADS), f32)
    b_gates = jnp.concatenate([i_bias, f_bias + 0.1 * jax.random.normal(ks[4], (DEPTH, ML_HEADS), f32)], axis=-1)
    conv_w = jax.random.normal(ks[5], (DEPTH, CONV_WIDTH, 2 * ML_WIDTH), f32) * CONV_WIDTH ** -0.5
    w_alpha = jax.random.normal(ks[6], (DEPTH, GLA_RANK, GLA_KW), f32) * GLA_RANK ** -0.5
    b_alpha = 0.1 * jax.random.normal(ks[7], (DEPTH, GLA_KW), f32)
    rel_bias = 0.1 * jax.random.normal(ks[8], (DEPTH, ATT_HEADS, 2 * REL_CLIP + 1), f32)
    ml_norm_g = 1.0 + 0.1 * jax.random.normal(ks[9], (DEPTH, ML_WIDTH), f32)
    gla_norm_g = 1.0 + 0.1 * jax.random.normal(ks[10], (DEPTH, GLA_WIDTH), f32)
    k_out, k_fin = jax.random.split(ks[11])
    w_out = jax.random.normal(k_out, (DEPTH, D_MIX, D_MODEL), f32) * D_MIX ** -0.5
    final_g = 1.0 + 0.1 * jax.random.normal(k_fin, (D_MODEL,), f32)
    return {"x": x, "norm_g": norm_g, "w_in": w_in, "b_gates": b_gates, "conv_w": conv_w,
            "w_alpha": w_alpha, "b_alpha": b_alpha, "rel_bias": rel_bias, "ml_norm_g": ml_norm_g,
            "gla_norm_g": gla_norm_g, "w_out": w_out, "final_g": final_g}

def first_block(x, norm_g, w_in, b_gates, conv_w, w_alpha, b_alpha, rel_bias, ml_norm_g, gla_norm_g, w_out, final_g):
    for l in range(DEPTH):
        x = hybrid_layer(x, norm_g[l], w_in[l], b_gates[l], conv_w[l], w_alpha[l], b_alpha[l], rel_bias[l],
                         ml_norm_g[l], gla_norm_g[l], w_out[l])
    return rmsnorm(x, final_g)


MLA_HEADS = 8
QK_NOPE_DIM = 64
QK_ROPE_DIM = 32
QK_HEAD_DIM = QK_NOPE_DIM + QK_ROPE_DIM
V_HEAD_DIM = 64
Q_LORA_RANK = 256
KV_LORA_RANK = 128
ROPE_THETA = 10000.0
Q_BLOCK = 128
MLA_OUT = MLA_HEADS * V_HEAD_DIM
MLA_IN = Q_LORA_RANK + KV_LORA_RANK + QK_ROPE_DIM

RWKV_HEADS = 8
RWKV_HEAD_DIM = 64
RWKV_DIM = RWKV_HEADS * RWKV_HEAD_DIM
DECAY_LORA = 64
ICLR_LORA = 64
VRES_LORA = 32
GATE_LORA = 128
RWKV_GN_EPS = 64e-5
RWKV_IN = 3 * RWKV_DIM + DECAY_LORA + ICLR_LORA + GATE_LORA

N_IN = MLA_IN + RWKV_IN
MIX_DIM = MLA_OUT + RWKV_DIM

N_EXPERTS = 32
TOP_K = 4
D_FF_EXPERT = D_MODEL
SWIGLU_LIMIT = 7.0
SWIGLU_ALPHA = 1.702
EXPERT_BLOCK = 128

DEEPNORM_ALPHA = (2 * DEPTH) ** 0.25
DEEPNORM_BETA = (8 * DEPTH) ** -0.25
LN_EPS = 1e-5
RMS_EPS = 1e-6


def layer_norm(x, g, b):
    xf = x.astype(jnp.float32)
    mu = xf.mean(-1, keepdims=True)
    var = jnp.square(xf - mu).mean(-1, keepdims=True)
    return ((xf - mu) * lax.rsqrt(var + LN_EPS) * g + b).astype(x.dtype)

def rms_norm(x, g):
    xf = x.astype(jnp.float32)
    return (xf * lax.rsqrt(jnp.square(xf).mean(-1, keepdims=True) + RMS_EPS) * g).astype(x.dtype)

def rope(x, cos, sin):
    xp = x.astype(jnp.float32).reshape(x.shape[:-1] + (x.shape[-1] // 2, 2))
    x0, x1 = xp[..., 0], xp[..., 1]
    out = jnp.stack([x0 * cos - x1 * sin, x0 * sin + x1 * cos], axis=-1)
    return out.reshape(x.shape).astype(x.dtype)

def causal_attention(q, k, v):
    b, s, h, dq = q.shape
    nb = s // Q_BLOCK
    scale = QK_HEAD_DIM ** -0.5
    q_blocks = jnp.moveaxis(q.reshape(b, nb, Q_BLOCK, h, dq), 1, 0)
    k_pos = jnp.arange(s)

    def one_block(args):
        qb, bi = args
        scores = jnp.einsum('bqhd,bkhd->bhqk', qb, k, preferred_element_type=jnp.float32) * scale
        q_pos = bi * Q_BLOCK + jnp.arange(Q_BLOCK)
        scores = jnp.where(k_pos[None, :] <= q_pos[:, None], scores, -jnp.inf)
        probs = jax.nn.softmax(scores, axis=-1).astype(v.dtype)
        return jnp.einsum('bhqk,bkhd->bqhd', probs, v)

    out = lax.map(one_block, (q_blocks, jnp.arange(nb)))
    return jnp.moveaxis(out, 0, 1).reshape(b, s, h, v.shape[-1])

def mla_group(p, cos, sin, q_norm_g, w_uq, kv_norm_g, w_uk, w_uv, out_g):
    b, s, _ = p.shape
    q_lat = p[..., :Q_LORA_RANK]
    kv_lat = p[..., Q_LORA_RANK:Q_LORA_RANK + KV_LORA_RANK]
    k_rot = p[..., Q_LORA_RANK + KV_LORA_RANK:]
    q = (rms_norm(q_lat, q_norm_g) @ w_uq).reshape(b, s, MLA_HEADS, QK_HEAD_DIM)
    q = jnp.concatenate([q[..., :QK_NOPE_DIM],
                         rope(q[..., QK_NOPE_DIM:], cos[:, :, None, :], sin[:, :, None, :])], axis=-1)
    c_kv = rms_norm(kv_lat, kv_norm_g)
    k_nope = (c_kv @ w_uk).reshape(b, s, MLA_HEADS, QK_NOPE_DIM)
    v = (c_kv @ w_uv).reshape(b, s, MLA_HEADS, V_HEAD_DIM)
    k_rot = rope(k_rot, cos, sin)
    k = jnp.concatenate([k_nope, jnp.broadcast_to(k_rot[:, :, None, :], (b, s, MLA_HEADS, QK_ROPE_DIM))], axis=-1)
    o = causal_attention(q, k, v)
    return rms_norm(o.reshape(b, s, MLA_OUT), out_g)

def rwkv7_recurrence(r, decay, k, v, kk, a):
    b, s, h, n = r.shape

    def step(state, inp):
        r_t, w_t, k_t, v_t, kk_t, a_t = inp
        sa = jnp.einsum('bhij,bhj->bhi', state, -kk_t)
        state = (state * w_t[:, :, None, :]
                 + sa[..., :, None] * (kk_t * a_t)[..., None, :]
                 + v_t[..., :, None] * k_t[..., None, :])
        return state, jnp.einsum('bhij,bhj->bhi', state, r_t)

    xs = tuple(jnp.moveaxis(z, 1, 0) for z in (r, decay, k, v, kk, a))
    _, out = lax.scan(step, jnp.zeros((b, h, n, n), jnp.float32), xs)
    return jnp.moveaxis(out, 0, 1)

def rwkv7_group(p, mu, w0, w2, a0, a2, g2, k_k, k_a, r_k, gn_g, gn_b, v_first, vres):
    b, s, _ = p.shape
    h_, n_ = RWKV_HEADS, RWKV_HEAD_DIM
    p_prev = jnp.pad(p[:, :-1], ((0, 0), (1, 0), (0, 0)))
    p = p + mu * (p_prev - p)
    c3 = 3 * RWKV_DIM
    r = p[..., :RWKV_DIM]
    k = p[..., RWKV_DIM:2 * RWKV_DIM]
    v = p[..., 2 * RWKV_DIM:c3]
    wd = p[..., c3:c3 + DECAY_LORA]
    ad = p[..., c3 + DECAY_LORA:c3 + DECAY_LORA + ICLR_LORA]
    gd = p[..., c3 + DECAY_LORA + ICLR_LORA:]
    w = -jax.nn.softplus(-(w0 + jnp.tanh(wd) @ w2).astype(jnp.float32)) - 0.5
    decay = jnp.exp(-jnp.exp(w))
    a = jax.nn.sigmoid(a0 + ad @ a2)
    g = jax.nn.sigmoid(gd) @ g2
    if vres is not None:
        v0, v1, v2 = vres
        v = v + (v_first - v) * jax.nn.sigmoid(v0 + (v @ v1) @ v2)
    heads = lambda z: z.reshape(b, s, h_, n_).astype(jnp.float32)
    r_h, k_h, v_h, a_h, d_h = heads(r), heads(k), heads(v), heads(a), heads(decay)
    kk = k_h * k_k.reshape(h_, n_)
    kk = kk / jnp.maximum(jnp.linalg.norm(kk, axis=-1, keepdims=True), 1e-12)
    k_h = k_h * (1.0 + (a_h - 1.0) * k_a.reshape(h_, n_))
    o = rwkv7_recurrence(r_h, d_h, k_h, v_h, kk, a_h)
    mean = o.mean(-1, keepdims=True)
    var = jnp.square(o - mean).mean(-1, keepdims=True)
    o = ((o - mean) * lax.rsqrt(var + RWKV_GN_EPS)).reshape(b, s, RWKV_DIM) * gn_g + gn_b
    bonus = jnp.sum(r_h * k_h * r_k, axis=-1, keepdims=True) * v_h
    o = (o + bonus.reshape(b, s, RWKV_DIM)) * g
    return o.astype(p.dtype), v

def clamped_swiglu(hh):
    x_glu = jnp.minimum(hh[..., ::2], SWIGLU_LIMIT)
    x_lin = jnp.clip(hh[..., 1::2], -SWIGLU_LIMIT, SWIGLU_LIMIT)
    return x_glu * jax.nn.sigmoid(SWIGLU_ALPHA * x_glu) * (x_lin + 1.0)

def moe_ffn(h, router_w, router_b, w1, b1, w2, b2):
    b, s, d = h.shape
    t = b * s
    ht = h.reshape(t, d)
    logits = (ht @ router_w + router_b).astype(jnp.float32)
    top_val, top_idx = lax.top_k(logits, TOP_K)
    gates = jax.nn.softmax(top_val, axis=-1)
    n_assign = t * TOP_K
    e_flat = top_idx.reshape(n_assign)
    tok_flat = jnp.arange(n_assign, dtype=jnp.int32) // TOP_K
    order = jnp.argsort(e_flat)
    e_sorted = e_flat[order]
    counts = jnp.bincount(e_flat, length=N_EXPERTS)
    starts = jnp.cumsum(counts) - counts
    padded = (counts + EXPERT_BLOCK - 1) // EXPERT_BLOCK * EXPERT_BLOCK
    pad_ends = jnp.cumsum(padded)
    pad_starts = pad_ends - padded
    dest = pad_starts[e_sorted] + (jnp.arange(n_assign) - starts[e_sorted])
    n_blocks = -(-n_assign // EXPERT_BLOCK) + N_EXPERTS
    n_slots = n_blocks * EXPERT_BLOCK
    slot_tok = jnp.full((n_slots,), t, jnp.int32).at[dest].set(tok_flat[order])
    slot_gate = jnp.zeros((n_slots,), jnp.float32).at[dest].set(gates.reshape(n_assign)[order])
    block_expert = jnp.minimum(
        jnp.searchsorted(pad_ends, jnp.arange(n_blocks) * EXPERT_BLOCK, side='right'), N_EXPERTS - 1)
    h_pad = jnp.concatenate([ht, jnp.zeros((1, d), ht.dtype)], axis=0)

    def expert_block(args):
        idx, e = args
        u = clamped_swiglu(h_pad[idx] @ w1[e] + b1[e])
        return u @ w2[e] + b2[e]

    y_slots = lax.map(expert_block, (slot_tok.reshape(n_blocks, EXPERT_BLOCK), block_expert))
    y = jnp.zeros((t + 1, d), jnp.float32).at[slot_tok].add(
        y_slots.reshape(n_slots, d).astype(jnp.float32) * slot_gate[:, None])
    return y[:t].reshape(b, s, d).astype(h.dtype)

def second_inputs(seed: int = 0) -> dict:
    key = jax.random.key(seed)
    keys = iter(jax.random.split(key, 64))

    def nrm(shape, scale):
        return jax.random.normal(next(keys), shape, jnp.float32) * scale

    L, D, C, E, F = DEPTH, D_MODEL, RWKV_DIM, N_EXPERTS, D_FF_EXPERT
    fan = D ** -0.5
    x = nrm((BATCH, SEQ, D), 1.0)
    c = nrm((BATCH, D), 1.0)
    positions = (jnp.arange(SEQ, dtype=jnp.int32)[None, :]
                 + jax.random.randint(next(keys), (BATCH, 1), 0, 2048, dtype=jnp.int32))
    emb_ln_g = 1.0 + nrm((D,), 0.02)
    emb_ln_b = nrm((D,), 0.02)
    ada_w = nrm((L, D, 6 * D), 0.1 * fan)
    ada_b = nrm((L, 6 * D), 0.02)
    w_in = jnp.concatenate([
        nrm((L, D, MLA_IN), fan),
        nrm((L, D, 2 * C), fan),
        nrm((L, D, C), fan * DEEPNORM_BETA),
        nrm((L, D, DECAY_LORA + ICLR_LORA + GATE_LORA), fan)], axis=-1)
    q_norm_g = 1.0 + nrm((L, Q_LORA_RANK), 0.02)
    w_uq = nrm((L, Q_LORA_RANK, MLA_HEADS * QK_HEAD_DIM), Q_LORA_RANK ** -0.5)
    kv_norm_g = 1.0 + nrm((L, KV_LORA_RANK), 0.02)
    w_uk = nrm((L, KV_LORA_RANK, MLA_HEADS * QK_NOPE_DIM), KV_LORA_RANK ** -0.5)
    w_uv = nrm((L, KV_LORA_RANK, MLA_HEADS * V_HEAD_DIM), KV_LORA_RANK ** -0.5 * DEEPNORM_BETA)
    mla_out_g = 1.0 + nrm((L, MLA_OUT), 0.02)
    rwkv_mu = jax.random.uniform(next(keys), (L, RWKV_IN), jnp.float32)
    ramp = jnp.linspace(0.0, 1.0, C) ** 0.85
    rwkv_w0 = -6.5 + 5.0 * ramp[None, :] + nrm((L, C), 0.1)
    rwkv_w2 = nrm((L, DECAY_LORA, C), 0.1 * DECAY_LORA ** -0.5)
    rwkv_a0 = nrm((L, C), 0.1)
    rwkv_a2 = nrm((L, ICLR_LORA, C), 0.1 * ICLR_LORA ** -0.5)
    rwkv_g2 = nrm((L, GATE_LORA, C), GATE_LORA ** -0.5)
    rwkv_k_k = 0.85 + nrm((L, C), 0.02)
    rwkv_k_a = 1.0 + nrm((L, C), 0.02)
    rwkv_r_k = nrm((L, RWKV_HEADS, RWKV_HEAD_DIM), 0.1)
    rwkv_gn_g = 1.0 + nrm((L, C), 0.02)
    rwkv_gn_b = nrm((L, C), 0.02)
    vres_v0 = 1.0 + nrm((L - 1, C), 0.1)
    vres_v1 = nrm((L - 1, C, VRES_LORA), C ** -0.5)
    vres_v2 = nrm((L - 1, VRES_LORA, C), 0.1 * VRES_LORA ** -0.5)
    w_o = nrm((L, MIX_DIM, D), MIX_DIM ** -0.5 * DEEPNORM_BETA)
    ln1_g = 1.0 + nrm((L, D), 0.02)
    ln1_b = nrm((L, D), 0.02)
    router_w = nrm((L, D, E), fan)
    router_b = nrm((L, E), 0.01)
    exp_w1 = nrm((L, E, D, 2 * F), fan)
    exp_b1 = nrm((L, E, 2 * F), 0.02)
    exp_w2 = nrm((L, E, F, D), F ** -0.5 * DEEPNORM_BETA)
    exp_b2 = nrm((L, E, D), 0.02)
    ln2_g = 1.0 + nrm((L, D), 0.02)
    ln2_b = nrm((L, D), 0.02)
    return {'x': x, 'c': c, 'positions': positions, 'emb_ln_g': emb_ln_g, 'emb_ln_b': emb_ln_b,
            'ada_w': ada_w, 'ada_b': ada_b, 'w_in': w_in,
            'q_norm_g': q_norm_g, 'w_uq': w_uq, 'kv_norm_g': kv_norm_g, 'w_uk': w_uk, 'w_uv': w_uv,
            'mla_out_g': mla_out_g, 'rwkv_mu': rwkv_mu, 'rwkv_w0': rwkv_w0, 'rwkv_w2': rwkv_w2,
            'rwkv_a0': rwkv_a0, 'rwkv_a2': rwkv_a2, 'rwkv_g2': rwkv_g2, 'rwkv_k_k': rwkv_k_k,
            'rwkv_k_a': rwkv_k_a, 'rwkv_r_k': rwkv_r_k, 'rwkv_gn_g': rwkv_gn_g, 'rwkv_gn_b': rwkv_gn_b,
            'vres_v0': vres_v0, 'vres_v1': vres_v1, 'vres_v2': vres_v2, 'w_o': w_o,
            'ln1_g': ln1_g, 'ln1_b': ln1_b, 'router_w': router_w, 'router_b': router_b,
            'exp_w1': exp_w1, 'exp_b1': exp_b1, 'exp_w2': exp_w2, 'exp_b2': exp_b2,
            'ln2_g': ln2_g, 'ln2_b': ln2_b}

def second_block(x, c, positions, emb_ln_g, emb_ln_b, ada_w, ada_b, w_in,
              q_norm_g, w_uq, kv_norm_g, w_uk, w_uv, mla_out_g,
              rwkv_mu, rwkv_w0, rwkv_w2, rwkv_a0, rwkv_a2, rwkv_g2, rwkv_k_k, rwkv_k_a, rwkv_r_k,
              rwkv_gn_g, rwkv_gn_b, vres_v0, vres_v1, vres_v2, w_o, ln1_g, ln1_b,
              router_w, router_b, exp_w1, exp_b1, exp_w2, exp_b2, ln2_g, ln2_b):
    inv_freq = ROPE_THETA ** (-jnp.arange(0, QK_ROPE_DIM, 2, dtype=jnp.float32) / QK_ROPE_DIM)
    ang = positions.astype(jnp.float32)[..., None] * inv_freq
    cos, sin = jnp.cos(ang), jnp.sin(ang)
    c_act = jax.nn.silu(c)
    x = layer_norm(x, emb_ln_g, emb_ln_b)
    v_first = None
    for i in range(DEPTH):
        mod = c_act @ ada_w[i] + ada_b[i]
        sh1, sc1, gt1, sh2, sc2, gt2 = [m[:, None, :] for m in jnp.split(mod, 6, axis=-1)]
        h = x * (1.0 + sc1) + sh1
        p = h @ w_in[i]
        mla_o = mla_group(p[..., :MLA_IN], cos, sin, q_norm_g[i], w_uq[i], kv_norm_g[i],
                          w_uk[i], w_uv[i], mla_out_g[i])
        vres = None if i == 0 else (vres_v0[i - 1], vres_v1[i - 1], vres_v2[i - 1])
        rwkv_o, v_i = rwkv7_group(p[..., MLA_IN:], rwkv_mu[i], rwkv_w0[i], rwkv_w2[i], rwkv_a0[i],
                                  rwkv_a2[i], rwkv_g2[i], rwkv_k_k[i], rwkv_k_a[i], rwkv_r_k[i],
                                  rwkv_gn_g[i], rwkv_gn_b[i], v_first, vres)
        if i == 0:
            v_first = v_i
        mix = jnp.concatenate([mla_o, rwkv_o], axis=-1) @ w_o[i]
        x = layer_norm(DEEPNORM_ALPHA * x + (1.0 + gt1) * mix, ln1_g[i], ln1_b[i])
        h = x * (1.0 + sc2) + sh2
        ffn = moe_ffn(h, router_w[i], router_b[i], exp_w1[i], exp_b1[i], exp_w2[i], exp_b2[i])
        x = layer_norm(DEEPNORM_ALPHA * x + (1.0 + gt2) * ffn, ln2_g[i], ln2_b[i])
    return x


def setup_inputs(seed=0):
    out = dict(first_inputs(seed))
    for name, value in second_inputs(seed + 1).items():
        if name != "x":
            out[name + "_2"] = value
    return out


def reference(
    x, norm_g, w_in, b_gates, conv_w, w_alpha, b_alpha, rel_bias, ml_norm_g, gla_norm_g, w_out,
    final_g, c_2, positions_2, emb_ln_g_2, emb_ln_b_2, ada_w_2, ada_b_2, w_in_2, q_norm_g_2,
    w_uq_2, kv_norm_g_2, w_uk_2, w_uv_2, mla_out_g_2, rwkv_mu_2, rwkv_w0_2, rwkv_w2_2,
    rwkv_a0_2, rwkv_a2_2, rwkv_g2_2, rwkv_k_k_2, rwkv_k_a_2, rwkv_r_k_2, rwkv_gn_g_2,
    rwkv_gn_b_2, vres_v0_2, vres_v1_2, vres_v2_2, w_o_2, ln1_g_2, ln1_b_2, router_w_2,
    router_b_2, exp_w1_2, exp_b1_2, exp_w2_2, exp_b2_2, ln2_g_2, ln2_b_2,
):
    x = first_block(
        x, norm_g, w_in, b_gates, conv_w, w_alpha, b_alpha, rel_bias, ml_norm_g, gla_norm_g,
        w_out, final_g,
    )
    return second_block(
        x, c_2, positions_2, emb_ln_g_2, emb_ln_b_2, ada_w_2, ada_b_2, w_in_2, q_norm_g_2,
        w_uq_2, kv_norm_g_2, w_uk_2, w_uv_2, mla_out_g_2, rwkv_mu_2, rwkv_w0_2, rwkv_w2_2,
        rwkv_a0_2, rwkv_a2_2, rwkv_g2_2, rwkv_k_k_2, rwkv_k_a_2, rwkv_r_k_2, rwkv_gn_g_2,
        rwkv_gn_b_2, vres_v0_2, vres_v1_2, vres_v2_2, w_o_2, ln1_g_2, ln1_b_2, router_w_2,
        router_b_2, exp_w1_2, exp_b1_2, exp_w2_2, exp_b2_2, ln2_g_2, ln2_b_2,
    )


_drawn_inputs = setup_inputs


def setup_inputs(seed=0):
    import zlib

    import numpy as np

    out = dict(_drawn_inputs(seed))
    spreads = {}
    factors = {'b_alpha': 2.772,
     'rel_bias': 7.004,
     'q_norm_g_2': 3.966,
     'kv_norm_g_2': 3.301,
     'mla_out_g_2': 4.472,
     'rwkv_w2_2': 8.0,
     'rwkv_a0_2': 4.002,
     'rwkv_a2_2': 4.034,
     'rwkv_k_k_2': 8.0,
     'rwkv_k_a_2': 5.991,
     'rwkv_gn_g_2': 6.605,
     'rwkv_gn_b_2': 7.302,
     'router_b_2': 3.964,
     'exp_b1_2': 8.0,
     'exp_b2_2': 6.427,
     'ln2_g_2': 2.809,
     'ln2_b_2': 2.863}
    for name, (base, spread) in spreads.items():
        noise = np.random.default_rng([zlib.crc32(name.encode()), seed]).standard_normal(out[name].shape)
        drawn = base * np.exp(spread * noise) if base else spread * noise
        out[name] = __import__('jax').numpy.asarray(drawn.astype(out[name].dtype))
    for name, factor in factors.items():
        out[name] = (out[name] * factor).astype(out[name].dtype)
    return out
```

```python
from contextlib import ExitStack

import concourse.bass as bass
import concourse.mybir as mybir
import numpy as np

ALU = mybir.AluOpType
ACT = mybir.ActivationFunctionType
AX = mybir.AxisListType
F32 = mybir.dt.float32
BF16 = mybir.dt.bfloat16
I32 = mybir.dt.int32
U32 = mybir.dt.uint32

P = 128
SEQ = 512
D = 1024
TT = SEQ // P
DT = D // P
NEG = -1e30

CHUNK = 64
HD = 64
AW = 384
AH = AW // HD
REL = 128
MW = 384
MH = MW // HD
CONV = 4
GW = 256
GH = 4
GDV = 64
GDK = 32
GKW = GH * GDK
RANK = 16
TAU = 16.0
RMS_EPS = 1e-6

QL, KVL, ROPE, NOPE, VD = 256, 128, 32, 64, 64
QK = NOPE + ROPE
NH = 8
MLA_IN = QL + KVL + ROPE
RW = 512
RH = 8
RP = RH // 2
LORA_D, LORA_A, LORA_G = 64, 64, 128
RWKV_IN = 3 * RW + LORA_D + LORA_A + LORA_G
GN_EPS = 64e-5
LN_EPS = 1e-5
ALPHA = 2.0 ** 0.25
E = 32
TOPK = 4
FF = 1024
LIMIT = 7.0
SW_ALPHA = 1.702
CAP = 128
EXTRA = SEQ * TOPK // CAP - 1
SLOTS = (E + EXTRA) * CAP

NBANK = 8
RING = 12
RSLOT = 2048


class Signal:

    def __init__(self, nc, name, step=1):
        self.sem = nc.alloc_semaphore(name=name)
        self.step = step
        self.base = 0

    def at(self, n):
        return self.base + n * self.step

    def passed(self, n):
        self.base += n * self.step


class Chain:

    def __init__(self, nc, name):
        self.sem = nc.alloc_semaphore(name=name)
        self.n = 0

    def __call__(self, engine, instruction):
        self.n += 1
        instruction.then_inc(self.sem, 1)
        engine.wait_ge(self.sem, self.n)


class Core:

    def __init__(self, nc, ctx):
        self.nc = nc
        self.ctx = ctx
        self.banks = ctx.enter_context(nc.psum_tensor("banks", [P, NBANK, 512], F32))
        self.ring = ctx.enter_context(nc.sbuf_tensor("ring", [P, RING, RSLOT], F32))
        self.x = ctx.enter_context(nc.sbuf_tensor("x_tokens", [P, TT, D], F32))
        self.ident = ctx.enter_context(nc.sbuf_tensor("ident", [P, P], F32))
        self.upper = ctx.enter_context(nc.sbuf_tensor("upper", [P, P], F32))
        self.upper_strict = ctx.enter_context(nc.sbuf_tensor("upper_strict", [P, P], F32))
        self.ones = ctx.enter_context(nc.sbuf_tensor("ones", [P, P], F32))
        self.products = Signal(nc, "products_ready")
        self.act_done = Signal(nc, "act_evacuated")
        self.dve_done = Signal(nc, "dve_evacuated")
        self.landed = [Signal(nc, f"landed_{i}", 16) for i in range(RING)]
        self.loaded = Signal(nc, "small_loads", 16)
        self.stored = Signal(nc, "stored", 16)
        self.dve = Chain(nc, "dve_chain")
        self.act = Chain(nc, "act_chain")
        self.pool = Chain(nc, "pool_chain")
        self.masks = Signal(nc, "masks_ready")
        self.gathered = Signal(nc, "gathered", 16)
        self.final_loaded = Signal(nc, "final_loaded", 16)
        self.final_stored = Signal(nc, "final_stored", 16)
        self.extra = Signal(nc, "outputs_ready")
        self.pool_ready = Signal(nc, "pool_ready")
        self.att_turned = Signal(nc, "probs_transposed")
        self.att_copied = Signal(nc, "transposed_copied")
        self.att_out = Signal(nc, "attention_out_ready")
        self.att_masked = Signal(nc, "scores_masked")
        self.att_max = Signal(nc, "row_max_ready")


def column(ap, tiles):
    return ap.rearrange("(t p) -> p t", t=tiles)


def over_partitions(ap, n):
    return ap.rearrange("(a n) -> a n", a=1).broadcast_to([P, n])


def projection(c, name, loads, units):
    nc = c.nc
    products, landed = c.products, c.landed
    done = {"act": c.act_done, "dve": c.dve_done}
    order = []
    count = {"act": 0, "dve": 0}
    for u in units:
        count[u["engine"]] += 1
        order.append((u["engine"], count[u["engine"]]))
    uses = [0] * RING

    with nc.Block(name) as block:

        @block.sync
        def _(sp):
            for g, (dst, src, free_after) in enumerate(loads):
                if free_after is not None:
                    sp.wait_ge(products.sem, products.at(free_after + 1))
                sp.dma_start(dst, src).then_inc(landed[g % RING].sem, 16)

        @block.tensor
        def _(pe):
            seen = -1
            for u, unit in enumerate(units):
                if unit["load"] > seen:
                    seen = unit["load"]
                    pe.wait_ge(landed[seen % RING].sem, landed[seen % RING].at(seen // RING + 1))
                if u >= NBANK:
                    engine, n = order[u - NBANK]
                    pe.wait_ge(done[engine].sem, done[engine].at(n))
                bank = c.banks[:, u % NBANK, :]
                for k in range(unit["k"]):
                    last = nc.tensor.matmul(unit["out"](bank), unit["lhsT"](k), unit["rhs"](k),
                                            start=(k == 0), stop=(k == unit["k"] - 1))
                last.then_inc(products.sem, 1)

        def evacuate(engine, who):
            for u, unit in enumerate(units):
                if unit["engine"] == who:
                    engine.wait_ge(products.sem, products.at(u + 1))
                    unit["evac"](c.banks[:, u % NBANK, :]).then_inc(done[who].sem, 1)

        @block.scalar
        def _(act):
            evacuate(act, "act")

        @block.vector
        def _(dve):
            evacuate(dve, "dve")

    products.passed(len(units))
    for who in ("act", "dve"):
        done[who].passed(count[who])
    for g in range(len(loads)):
        landed[g % RING].passed(1)


def turned(c, name, src, dst, tiles, evac):
    nc = c.nc
    with nc.Block(name) as block:

        @block.tensor
        def _(pe):
            for f in range(tiles):
                if f >= NBANK:
                    copied_by = c.act_done if f % 2 else c.dve_done
                    pe.wait_ge(copied_by.sem, copied_by.at((f - NBANK) // 2 + 1))
                for t in range(TT):
                    last = nc.tensor.transpose(c.banks[:, f % NBANK, t * P:(t + 1) * P], src(t, f), c.ident[:])
                last.then_inc(c.products.sem, 1)

        @block.scalar
        def _(act):
            for f in range(1, tiles, 2):
                act.wait_ge(c.products.sem, c.products.at(f + 1))
                evac("act", f, dst(f), c.banks[:, f % NBANK, :]).then_inc(c.act_done.sem, 1)

        @block.vector
        def _(dve):
            for f in range(0, tiles, 2):
                dve.wait_ge(c.products.sem, c.products.at(f + 1))
                evac("dve", f, dst(f), c.banks[:, f % NBANK, :]).then_inc(c.dve_done.sem, 1)

    c.products.passed(tiles)
    c.act_done.passed(tiles // 2)
    c.dve_done.passed((tiles + 1) // 2)


def constants(c, x_dram, Y):
    nc = c.nc
    with nc.Block("constants") as block:

        @block.sync
        def _(sp):
            sp.dma_start(c.x[:], x_dram.rearrange("a (t p) d -> p (a t) d", p=P)).then_inc(c.loaded.sem, 16)
            sp.wait_ge(c.loaded.sem, c.loaded.at(1))
            sp.wait_ge(c.masks.sem, 4)
            sp.dma_start(Y[E * CAP:SLOTS, :].rearrange("(b s) n -> s b n", s=CAP),
                         c.ring[:, 0:1, 0:D].broadcast_to([P, EXTRA, D])).then_inc(c.stored.sem, 16)
            sp.wait_ge(c.stored.sem, c.stored.at(1))

        @block.gpsimd
        def _(pool):
            nc.gpsimd.memset(c.ring[:, 0, 0:D], 0.0).then_inc(c.masks.sem, 1)
            for m in (c.ident, c.upper, c.upper_strict):
                value = 0.0 if m is c.ident else 1.0
                nc.gpsimd.memset(m[:], value).then_inc(c.masks.sem, 1)
            nc.gpsimd.memset(c.ones[:], 1.0)
            pool.wait_ge(c.masks.sem, 4)
            nc.gpsimd.affine_select(out=c.ident[:], in_=c.ident[:], compare_op=ALU.not_equal, fill=1.0,
                                    base=0, pattern=[[-1, P]], channel_multiplier=1)
            nc.gpsimd.affine_select(out=c.upper[:], in_=c.upper[:], compare_op=ALU.is_ge, fill=0.0,
                                    base=0, pattern=[[1, P]], channel_multiplier=-1)
            nc.gpsimd.affine_select(out=c.upper_strict[:], in_=c.upper_strict[:], compare_op=ALU.is_gt, fill=0.0,
                                    base=0, pattern=[[1, P]], channel_multiplier=-1)

    c.loaded.passed(1)
    c.masks.passed(4)
    c.stored.passed(1)


def rms_rows(c, name, src, dst, junk, stat, n, width, eps, also=None):
    nc = c.nc
    sums, root = stat[:, 0:n], stat[:, n:2 * n]
    with nc.Block(name) as block:

        @block.vector
        def _(dve):
            for i in range(n):
                last = nc.vector.tensor_tensor_reduce(out=junk(i), in0=src(i), in1=src(i), scale=1.0, scalar=0.0,
                                                      op0=ALU.mult, op1=ALU.add, accum_out=sums[:, i:i + 1])
            c.dve(dve, last)
            nc.vector.tensor_scalar(sums, sums, 1.0 / width, eps, ALU.mult, ALU.add).then_inc(c.dve_done.sem, 1)
            dve.wait_ge(c.act_done.sem, c.act_done.at(1))
            c.dve(dve, nc.vector.reciprocal(root, root))
            for i in range(n):
                last = nc.vector.tensor_scalar(dst(i), src(i), root[:, i:i + 1], None, ALU.mult)
                if also is not None:
                    c.dve(dve, last)
                    also(dve, i)

        @block.scalar
        def _(act):
            act.wait_ge(c.dve_done.sem, c.dve_done.at(1))
            nc.scalar.activation(root, sums, ACT.Sqrt).then_inc(c.act_done.sem, 1)

    c.act_done.passed(1)
    c.dve_done.passed(1)


def attention(c, name, heads, qT, kT, v, dv, scale, bias, bias_source, finish):
    nc = c.nc
    units = [(h, t) for h in range(heads) for t in range(TT)]
    n = len(units)
    scores_ready, turned_ready, out_ready = c.products, c.att_turned, c.att_out
    masked, probs_ready, probs_turned, used = c.att_masked, c.act_done, c.att_copied, c.dve_done
    with ExitStack() as ctx:
        s = ctx.enter_context(nc.sbuf_tensor(name + "_s", [P, 2, SEQ], F32))
        p = ctx.enter_context(nc.sbuf_tensor(name + "_p", [P, 2, SEQ], F32))
        pT = ctx.enter_context(nc.sbuf_tensor(name + "_pT", [P, 2, SEQ], F32))
        top = ctx.enter_context(nc.sbuf_tensor(name + "_top", [P, n], F32))
        total = ctx.enter_context(nc.sbuf_tensor(name + "_total", [P, n], F32))
        rinv = ctx.enter_context(nc.sbuf_tensor(name + "_rinv", [P, n], F32))
        with nc.Block(name) as block:

            @block.sync
            def _(sp):
                if bias_source is None:
                    return
                for h in range(heads):
                    if h >= 2:
                        sp.wait_ge(masked.sem, masked.at(TT * (h - 1)))
                    sp.dma_start(bias(h), bias_source[h, :, :]).then_inc(c.landed[h % 2].sem, 16)

            @block.gpsimd
            def _(pool):
                if bias_source is None:
                    return
                for h in range(heads):
                    landed = c.landed[h % 2]
                    pool.wait_ge(landed.sem, landed.at(h // 2 + 1))
                    nc.gpsimd.memset(bias(h)[0:CHUNK, SEQ - CHUNK:SEQ], NEG).then_inc(c.masks.sem, 1)

            @block.tensor
            def _(pe):
                for i in range(n + 2):
                    if i < n:
                        h, t = units[i]
                        if i >= 2:
                            pe.wait_ge(masked.sem, masked.at(i - 1))
                        nc.tensor.matmul(c.banks[:, i % 2, 0:(t + 1) * P], qT(h)[:, t * P:(t + 1) * P],
                                         kT(h)[:, 0:(t + 1) * P], start=True, stop=True).then_inc(scores_ready.sem, 1)
                    if 1 <= i <= n:
                        j = i - 1
                        t = units[j][1]
                        pe.wait_ge(probs_ready.sem, probs_ready.at(j + 1))
                        if j >= 2:
                            pe.wait_ge(probs_turned.sem, probs_turned.at(j - 1))
                        for b in range(t + 1):
                            last = nc.tensor.transpose(c.banks[:, 2 + j % 2, b * P:(b + 1) * P],
                                                       p[:, j % 2, b * P:(b + 1) * P], c.ident[:])
                        last.then_inc(turned_ready.sem, 1)
                    if i >= 2:
                        j = i - 2
                        h, t = units[j]
                        pe.wait_ge(probs_turned.sem, probs_turned.at(j + 1))
                        if j >= 2:
                            pe.wait_ge(used.sem, used.at(j - 1))
                        for b in range(t + 1):
                            last = nc.tensor.matmul(c.banks[:, 4 + j % 2, 0:dv], pT[:, j % 2, b * P:(b + 1) * P],
                                                    v(b, h), start=(b == 0), stop=(b == t))
                        last.then_inc(out_ready.sem, 1)

            @block.scalar
            def _(act):
                for i in range(n + 1):
                    if i < n:
                        t = units[i][1]
                        act.wait_ge(c.att_max.sem, c.att_max.at(i + 1))
                        if i >= 2:
                            act.wait_ge(turned_ready.sem, turned_ready.at(i - 1))
                        nc.scalar.activation(p[:, i % 2, 0:(t + 1) * P], s[:, i % 2, 0:(t + 1) * P], ACT.Exp,
                                             bias=top[:, i:i + 1], accum_out=total[:, i:i + 1]).then_inc(probs_ready.sem, 1)
                    if i >= 1:
                        j = i - 1
                        t = units[j][1]
                        act.wait_ge(turned_ready.sem, turned_ready.at(j + 1))
                        if j >= 2:
                            act.wait_ge(out_ready.sem, out_ready.at(j - 1))
                        nc.scalar.activation(pT[:, j % 2, 0:(t + 1) * P], c.banks[:, 2 + j % 2, 0:(t + 1) * P],
                                             ACT.Copy).then_inc(probs_turned.sem, 1)

            @block.vector
            def _(dve):
                for i in range(n + 2):
                    if i < n:
                        h, t = units[i]
                        w = (t + 1) * P
                        if t == 0 and bias_source is not None:
                            dve.wait_ge(c.masks.sem, c.masks.at(h + 1))
                        dve.wait_ge(scores_ready.sem, scores_ready.at(i + 1))
                        if i >= 2:
                            dve.wait_ge(probs_ready.sem, probs_ready.at(i - 1))
                        nc.vector.scalar_tensor_tensor(out=s[:, i % 2, 0:w], in0=c.banks[:, i % 2, 0:w], scalar=scale,
                                                       in1=bias(h)[:, SEQ - w:SEQ], op0=ALU.mult,
                                                       op1=ALU.add).then_inc(masked.sem, 1)
                        dve.wait_ge(masked.sem, masked.at(i + 1))
                        nc.vector.tensor_reduce(top[:, i:i + 1], s[:, i % 2, 0:w], AX.X, ALU.max,
                                                negate=True).then_inc(c.att_max.sem, 1)
                    if i >= 2:
                        j = i - 2
                        h, t = units[j]
                        dve.wait_ge(probs_ready.sem, probs_ready.at(j + 1))
                        c.dve(dve, nc.vector.reciprocal(rinv[:, j:j + 1], total[:, j:j + 1]))
                        dve.wait_ge(out_ready.sem, out_ready.at(j + 1))
                        finish(h, t, c.banks[:, 4 + j % 2, 0:dv], rinv[:, j:j + 1]).then_inc(used.sem, 1)

    for signal in (scores_ready, turned_ready, out_ready, masked, probs_ready, probs_turned, used, c.att_max):
        signal.passed(n)
    if bias_source is not None:
        c.masks.passed(heads)
        c.landed[0].passed((heads + 1) // 2)
        c.landed[1].passed(heads // 2)


def first_attention(c, A, qk, v, y):
    nc = c.nc
    with nc.sbuf_tensor("rel_bias_rows", [P, 2, SEQ], F32) as bias:
        def finish(h, t, product, rinv):
            place = y[:, t, h * HD:(h + 1) * HD]
            return nc.vector.scalar_tensor_tensor(out=place, in0=product, scalar=rinv, in1=place,
                                                  op0=ALU.mult, op1=ALU.mult)

        def head(base):
            return lambda h: qk[(h % 2) * HD:(h % 2 + 1) * HD, base + h // 2, :]

        attention(c, "band_attention", AH, head(0), head(3), lambda b, h: v[:, b, h * HD:(h + 1) * HD], HD,
                  HD ** -0.5, lambda h: bias[:, h % 2, :], A["rel_rows"], finish)


def first_block(c, A):
    nc = c.nc
    with ExitStack() as ctx:
        def sb(name, shape, dt=F32):
            return ctx.enter_context(nc.sbuf_tensor(name, shape, dt))

        y = sb("y", [P, TT, D])
        qk_m = sb("ml_qk", [P, 6, SEQ])
        v_m = sb("ml_v", [P, TT, MH, HD + 1])
        gate_m = sb("ml_gate", [P, TT, MW])
        pre_if = sb("ml_if", [P, TT, 2 * MH])
        qk_g = sb("gla_qk", [P, 2, SEQ])
        v_g = sb("gla_v", [P, TT, GW])
        rank_g = sb("gla_rank", [RANK, SEQ])
        stat = sb("stat_a", [P, 64])
        g_col = sb("norm_col", [P, DT])
        attention_only = ExitStack()
        qk_a = attention_only.enter_context(nc.sbuf_tensor("att_qk", [P, 6, SEQ], F32))
        v_a = attention_only.enter_context(nc.sbuf_tensor("att_v", [P, TT, AW], F32))
        with nc.sbuf_tensor("hnT", [P, DT, SEQ], F32) as hnT:
            def load_g():
                with nc.Block("load_norm_g") as block:
                    @block.sync
                    def _(sp):
                        sp.dma_start(g_col[:], column(A["norm_g"].rearrange("a d -> (a d)"), DT), allow_slow_non_contiguous=True).then_inc(c.loaded.sem, 16)
                        sp.wait_ge(c.loaded.sem, c.loaded.at(1))
                    @block.gpsimd
                    def _(pool):
                        nc.gpsimd.memset(v_m[:, :, :, HD:HD + 1], 1.0)
                c.loaded.passed(1)
            load_g()
            rms_rows(c, "rms_in", lambda i: c.x[:, i, :], lambda i: y[:, i, :], lambda i: y[:, i, :], stat, TT, D, RMS_EPS)

            def scaled(who, f, dst, src):
                if who == "act":
                    return nc.scalar.activation(dst, src, ACT.Copy, scale=g_col[:, f:f + 1])
                return nc.vector.tensor_scalar(dst, src, g_col[:, f:f + 1], None, ALU.mult)

            turned(c, "turn_in", lambda t, f: y[:, t, f * P:(f + 1) * P], lambda f: hnT[:, f, :], DT, scaled)

            w_in = A["w_in"].rearrange("a (k p) n -> p (a k) n", p=P)
            flat = c.ring[:].rearrange("p a b -> p (a b)")
            groups = [(0, 384), (384, 384), (768, 384), (1152, 384), (1536, 384), (1920, 384), (2304, 384),
                      (2688, 384), (3072, 396), (3468, 256), (3724, 528)]
            slot = 8 * 528
            nslot = RING * RSLOT // slot
            spots = [flat[:, (g % nslot) * slot:(g % nslot) * slot + DT * n].rearrange("p (k n) -> p k n", k=DT)
                     for g, (_, n) in enumerate(groups)]
            units = []

            def feature_unit(g, off, n, dst):
                w = spots[g]
                engine = "dve" if len(units) % 2 else "act"
                units.append(dict(load=g, k=DT, lhsT=lambda k: w[:, k, off:off + n], rhs=lambda k: hnT[:, k, :],
                                  out=lambda b: b[0:n, :], engine=engine,
                                  evac=(lambda b: nc.vector.tensor_copy(dst, b[0:n, :])) if engine == "dve"
                                  else (lambda b: nc.scalar.activation(dst, b[0:n, :], ACT.Copy))))

            def token_unit(g, t, off, n, engine, evac):
                w = spots[g]
                units.append(dict(load=g, k=DT, lhsT=lambda k: hnT[:, k, t * P:(t + 1) * P],
                                  rhs=lambda k: w[:, k, off:off + n], out=lambda b: b[:, 0:n],
                                  engine=engine, evac=evac))

            for f in range(3):
                feature_unit(0, f * P, P, qk_a[:, f, :])
            for f in range(3):
                feature_unit(1, f * P, P, qk_a[:, 3 + f, :])
            for t in range(TT):
                token_unit(2, t, 0, AW, "dve", lambda b, t=t: nc.vector.tensor_copy(v_a[:, t, :], b[:, 0:AW]))
            for t in range(TT):
                token_unit(3, t, 0, AW, "act", lambda b, t=t: nc.scalar.activation(y[:, t, 0:AW], b[:, 0:AW], ACT.Silu))
            for f in range(3):
                feature_unit(4, f * P, P, qk_m[:, f, :])
            for f in range(3):
                feature_unit(5, f * P, P, qk_m[:, 3 + f, :])
            for t in range(TT):
                token_unit(6, t, 0, MW, "dve", lambda b, t=t: nc.vector.tensor_copy(
                    v_m[:, t, :, 0:HD], b[:, 0:MW].rearrange("p (h d) -> p h d", h=MH)))
            for t in range(TT):
                token_unit(7, t, 0, MW, "act", lambda b, t=t: nc.scalar.activation(gate_m[:, t, :], b[:, 0:MW], ACT.Sigmoid))
            for t in range(TT):
                token_unit(8, t, 0, 12, "dve", lambda b, t=t: nc.vector.tensor_copy(pre_if[:, t, :], b[:, 0:12]))
            for t in range(TT):
                token_unit(8, t, 12, MW, "act", lambda b, t=t: nc.scalar.activation(
                    y[:, t, AW:AW + MW], b[:, 0:MW], ACT.Silu))
            for f in range(2):
                feature_unit(9, f * P, P, qk_g[:, f, :])
            for t in range(TT):
                token_unit(10, t, 0, GW, "dve", lambda b, t=t: nc.vector.tensor_copy(v_g[:, t, :], b[:, 0:GW]))
            feature_unit(10, GW, RANK, rank_g[:, :])
            for t in range(TT):
                token_unit(10, t, GW + RANK, GW, "act", lambda b, t=t: nc.scalar.activation(y[:, t, AW + MW:D], b[:, 0:GW], ACT.Silu))
            last_unit = {}
            for i, u in enumerate(units):
                last_unit[u["load"]] = i
            loads = [(spots[g], w_in[:, :, a:a + n], last_unit[g - nslot] if g >= nslot else None)
                     for g, (a, n) in enumerate(groups)]
            projection(c, "project_in", loads, units)
        first_attention(c, A, qk_a, v_a, y)
        attention_only.close()
        first_mlstm(c, A, qk_m, v_m, gate_m, pre_if, y)
        first_gla(c, A, qk_g, v_g, rank_g, y)
        with nc.sbuf_tensor("yT", [P, DT, SEQ], F32) as yT:
            out_projection(c, "project_out", A["w_out"].rearrange("a k n -> (a k) n"), y, yT, lambda t, n, b:
                           nc.vector.tensor_tensor(c.x[:, t, n * 512:(n + 1) * 512], c.x[:, t, n * 512:(n + 1) * 512], b, ALU.add))


def log_sigmoid(c, dve, act_ready, act_done, x, t1, t2, out):
    nc = c.nc
    c.dve(dve, nc.vector.scalar_tensor_tensor(out=t1, in0=x, scalar=-1.0, in1=x, op0=ALU.mult, op1=ALU.max))
    nc.vector.tensor_scalar(out, x, 0.0, None, ALU.min).then_inc(act_ready.sem, 1)
    dve.wait_ge(act_done.sem, act_done.at(1))
    c.dve(dve, nc.vector.tensor_tensor(out, out, t2, ALU.subtract))


def log_sigmoid_act(c, act, act_ready, act_done, t1, t2):
    nc = c.nc
    act.wait_ge(act_ready.sem, act_ready.at(1))
    c.act(act, nc.scalar.activation(t2, t1, ACT.Exp, scale=-1.0))
    nc.scalar.activation(t2, t2, ACT.Ln, bias=1.0).then_inc(act_done.sem, 1)


def first_mlstm(c, A, qk, v, gate_o, pre_if, y):
    nc = c.nc
    H = MH
    with ExitStack() as ctx:
        def sb(name, shape, dt=F32):
            return ctx.enter_context(nc.sbuf_tensor(name, shape, dt))

        a_row = sb("a_rows", [H, SEQ])
        pick = sb("pick_head", [H, H, P])
        b_col = sb("b_cols", [P, TT, H])
        em_col = sb("em_cols", [P, TT, H])
        ml_g = sb("ml_norm", [P, MW])
        stat = sb("ml_stat", [P, 2, TT * H])
        hout = sb("ml_out", [P, TT, MW])
        early = ExitStack()
        gi, gf, t1, t2, lf, F, m, onerow, b_row = (
            early.enter_context(nc.sbuf_tensor(name, [H, SEQ], F32)) for name in
            ("gate_i", "gate_f", "mt1", "mt2", "log_f", "cum_f", "stabiliser", "one_rows", "b_rows"))
        taps = early.enter_context(nc.sbuf_tensor("conv_taps", [P, CONV, 6], F32))
        bias_if = early.enter_context(nc.sbuf_tensor("bias_if", [H, 2], F32))
        acc = early.enter_context(nc.sbuf_tensor("conv_acc", [P, 2, SEQ], F32))

        with nc.Block("mlstm_gates") as block:

            @block.sync
            def _(sp):
                sp.dma_start(taps[:], A["conv_w"].rearrange("a j (f p) -> p (a j) f", p=P), allow_slow_non_contiguous=True).then_inc(c.loaded.sem, 16)
                sp.dma_start(bias_if[:], A["b_gates"].rearrange("a (g h) -> h (a g)", g=2), allow_slow_non_contiguous=True).then_inc(c.loaded.sem, 16)
                sp.dma_start(ml_g[:], over_partitions(A["ml_norm_g"].rearrange("a n -> (a n)"), MW)).then_inc(c.loaded.sem, 16)

            @block.tensor
            def _(pe):
                for g in range(2):
                    for t in range(TT):
                        last = nc.tensor.transpose(c.banks[0:H, g, t * P:(t + 1) * P],
                                                   pre_if[:, t, g * H:(g + 1) * H], c.ident[:])
                last.then_inc(c.products.sem, 1)

            @block.gpsimd
            def _(pool):
                nc.gpsimd.memset(onerow[:], 1.0)
                c.pool(pool, nc.gpsimd.memset(pick[:], 0.0))
                nc.gpsimd.affine_select(out=pick[:], in_=pick[:], compare_op=ALU.not_equal, fill=1.0, base=0,
                                        pattern=[[-1, H], [0, P]], channel_multiplier=1)

            @block.vector
            def _(dve):
                dve.wait_ge(c.loaded.sem, c.loaded.at(3))
                for f in range(6):
                    x, o = qk[:, f, :], acc[:, f % 2, :]
                    if f >= 2:
                        dve.wait_ge(c.act_done.sem, c.act_done.at(f - 1))
                    c.dve(dve, nc.vector.tensor_scalar(o, x, taps[:, CONV - 1, f:f + 1], None, ALU.mult))
                    for back in range(1, CONV):
                        last = nc.vector.scalar_tensor_tensor(
                            out=o[:, back:SEQ], in0=x[:, 0:SEQ - back], scalar=taps[:, CONV - 1 - back, f:f + 1],
                            in1=o[:, back:SEQ], op0=ALU.mult, op1=ALU.add)
                        if back < CONV - 1:
                            c.dve(dve, last)
                    last.then_inc(c.dve_done.sem, 1)
                dve.wait_ge(c.products.sem, c.products.at(1))
                nc.vector.tensor_scalar(gi[:], c.banks[0:H, 0, :], bias_if[:, 0:1], None, ALU.add)
                c.dve(dve, nc.vector.tensor_scalar(gf[:], c.banks[0:H, 1, :], bias_if[:, 1:2], None, ALU.add))

            @block.scalar
            def _(act):
                for f in range(6):
                    act.wait_ge(c.dve_done.sem, c.dve_done.at(f + 1))
                    nc.scalar.activation(qk[:, f, :], acc[:, f % 2, :], ACT.Silu).then_inc(c.act_done.sem, 1)

        c.products.passed(1)
        c.dve_done.passed(6)
        c.act_done.passed(6)
        c.loaded.passed(3)

        with nc.Block("mlstm_scans") as block:

            @block.vector
            def _(dve):
                log_sigmoid(c, dve, c.dve_done, c.act_done, gf[:], t1[:], t2[:], lf[:])
                nc.vector.tensor_tensor_scan(F[:], onerow[:], lf[:], 0.0, ALU.mult, ALU.add)
                c.dve(dve, nc.vector.tensor_tensor_scan(m[:], lf[:], gi[:], 0.0, ALU.add, ALU.max))
                nc.vector.tensor_tensor(a_row[:], F[:], m[:], ALU.subtract)
                nc.vector.tensor_tensor(b_row[:], gi[:], F[:], ALU.subtract).then_inc(c.dve_done.sem, 1)
                dve.wait_ge(c.products.sem, c.products.at(1))
                nc.vector.tensor_copy(b_col[:], c.banks[:, 0, 0:TT * H].rearrange("p (t h) -> p t h", t=TT))
                nc.vector.tensor_copy(em_col[:], c.banks[:, 1, 0:TT * H].rearrange("p (t h) -> p t h", t=TT))

            @block.scalar
            def _(act):
                log_sigmoid_act(c, act, c.dve_done, c.act_done, t1[:], t2[:])
                act.wait_ge(c.dve_done.sem, c.dve_done.at(2))
                nc.scalar.activation(t1[:], m[:], ACT.Exp, scale=-1.0).then_inc(c.act_done.sem, 1)

            @block.tensor
            def _(pe):
                pe.wait_ge(c.dve_done.sem, c.dve_done.at(2))
                pe.wait_ge(c.act_done.sem, c.act_done.at(2))
                for bank, rows in ((0, b_row), (1, t1)):
                    for t in range(TT):
                        last = nc.tensor.transpose(c.banks[:, bank, t * H:(t + 1) * H], rows[:, t * P:(t + 1) * P],
                                                   c.ident[0:H, 0:H])
                last.then_inc(c.products.sem, 1)

        c.products.passed(1)
        c.dve_done.passed(2)
        c.act_done.passed(2)

        early.close()
        with ExitStack() as inner:
            expo = inner.enter_context(nc.sbuf_tensor("decay_exp", [P, 2, SEQ], F32))
            dec = inner.enter_context(nc.sbuf_tensor("decay", [P, 2, SEQ], F32))
            start = [sum((TT - i) * P for i in range(j)) for j in range(TT)]
            sd = inner.enter_context(nc.sbuf_tensor("scores_decayed", [P, 2, sum((TT - j) * P for j in range(TT))], F32))
            den = inner.enter_context(nc.sbuf_tensor("ml_den", [P, 2, TT], F32))
            units = [(h, j) for h in range(H) for j in range(TT)]
            n = len(units)
            rows_ready, s_ready, out_ready = c.products, c.att_turned, c.att_out
            expo_ready, decay_ready, masked_ready, sd_ready, used = c.att_max, c.act_done, c.masks, c.att_masked, c.dve_done
            with nc.Block("mlstm_attention") as block:

                @block.tensor
                def _(pe):
                    for h in range(H + 1):
                        if h < H:
                            if h >= 2:
                                pe.wait_ge(expo_ready.sem, expo_ready.at(TT * (h - 1)))
                            nc.tensor.matmul(c.banks[:, h % 2, :], pick[:, h, :], a_row[:], start=True,
                                             stop=True).then_inc(rows_ready.sem, 1)
                            lo = (h % 2) * HD
                            for j in range(TT):
                                i = TT * h + j
                                if i >= 2:
                                    pe.wait_ge(sd_ready.sem, sd_ready.at(i - 1))
                                nc.tensor.matmul(c.banks[:, 2 + i % 2, j * P:SEQ],
                                                 qk[lo:lo + HD, 3 + h // 2, j * P:(j + 1) * P],
                                                 qk[lo:lo + HD, h // 2, j * P:SEQ], start=True,
                                                 stop=True).then_inc(s_ready.sem, 1)
                        if h >= 1:
                            g = h - 1
                            pe.wait_ge(sd_ready.sem, sd_ready.at(TT * (g + 1)))
                            if g >= 2:
                                pe.wait_ge(used.sem, used.at(g - 1))
                            for t in range(TT):
                                for j in range(t + 1):
                                    last = nc.tensor.matmul(c.banks[:, 4 + g % 2, t * (HD + 1):(t + 1) * (HD + 1)],
                                                            sd[:, g % 2, start[j] + (t - j) * P:start[j] + (t - j + 1) * P], v[:, j, g, :],
                                                            start=(j == 0), stop=(j == t))
                            last.then_inc(out_ready.sem, 1)

                def take(dve, h):
                    dve.wait_ge(out_ready.sem, out_ready.at(h + 1))
                    o = c.banks[:, 4 + h % 2, 0:TT * (HD + 1)].rearrange("p (t d) -> p t d", t=TT)
                    d = den[:, h % 2, :]
                    c.dve(dve, nc.vector.tensor_scalar(d, o[:, :, HD], -1.0, None, ALU.mult))
                    c.dve(dve, nc.vector.tensor_tensor(d, d, o[:, :, HD], ALU.max))
                    c.dve(dve, nc.vector.tensor_tensor(d, d, em_col[:, :, h], ALU.max))
                    c.dve(dve, nc.vector.reciprocal(d, d))
                    for t in range(TT):
                        last = nc.vector.tensor_scalar(hout[:, t, h * HD:(h + 1) * HD], o[:, t, 0:HD], d[:, t:t + 1],
                                                       None, ALU.mult)
                    last.then_inc(used.sem, 1)

                @block.vector
                def _(dve):
                    def exponent(i):
                        h, j = units[i]
                        if j == 0:
                            dve.wait_ge(rows_ready.sem, rows_ready.at(h + 1))
                        if i >= 2:
                            dve.wait_ge(decay_ready.sem, decay_ready.at(i - 1))
                        nc.vector.tensor_scalar(expo[:, i % 2, j * P:SEQ], c.banks[:, h % 2, j * P:SEQ],
                                                b_col[:, j, h:h + 1], 0.0, ALU.add, ALU.min).then_inc(expo_ready.sem, 1)

                    exponent(0)
                    for i in range(n):
                        h, j = units[i]
                        if i + 1 < n:
                            exponent(i + 1)
                        dve.wait_ge(masked_ready.sem, masked_ready.at(i + 1))
                        dve.wait_ge(s_ready.sem, s_ready.at(i + 1))
                        if h >= 2:
                            dve.wait_ge(out_ready.sem, out_ready.at(h - 1))
                        nc.vector.scalar_tensor_tensor(out=sd[:, h % 2, start[j]:start[j] + SEQ - j * P], in0=c.banks[:, 2 + i % 2, j * P:SEQ],
                                                       scalar=HD ** -0.5, in1=dec[:, i % 2, j * P:SEQ], op0=ALU.mult,
                                                       op1=ALU.mult).then_inc(sd_ready.sem, 1)
                        if j == 1 and h >= 1:
                            take(dve, h - 1)
                    take(dve, H - 1)

                @block.scalar
                def _(act):
                    for i in range(n):
                        h, j = units[i]
                        act.wait_ge(expo_ready.sem, expo_ready.at(i + 1))
                        if i >= 2:
                            act.wait_ge(sd_ready.sem, sd_ready.at(i - 1))
                        nc.scalar.activation(dec[:, i % 2, j * P:SEQ], expo[:, i % 2, j * P:SEQ],
                                             ACT.Exp).then_inc(decay_ready.sem, 1)

                @block.gpsimd
                def _(pool):
                    for i in range(n):
                        j = units[i][1]
                        pool.wait_ge(decay_ready.sem, decay_ready.at(i + 1))
                        diag = dec[:, i % 2, j * P:(j + 1) * P]
                        nc.gpsimd.tensor_tensor(diag, diag, c.upper[:], ALU.mult).then_inc(masked_ready.sem, 1)

            rows_ready.passed(H)
            out_ready.passed(H)
            used.passed(H)
            for signal in (s_ready, expo_ready, decay_ready, masked_ready, sd_ready):
                signal.passed(n)

        def gated(dve):
            place = y[:, :, AW:AW + MW]
            c.dve(dve, nc.vector.tensor_tensor(hout[:], hout[:], ml_g[:].unsqueeze(1).broadcast_to([P, TT, MW]), ALU.mult))
            c.dve(dve, nc.vector.tensor_tensor(place, place, gate_o[:], ALU.mult))
            nc.vector.tensor_tensor(place, place, hout[:], ALU.mult)

        with nc.sbuf_tensor("ml_square", [P, TT * H, HD], F32) as square:
            head_norm(c, "mlstm_norm", hout[:].rearrange("p t (h d) -> p (t h) d", h=H), square[:], stat[:], TT * H, HD,
                      RMS_EPS, False, gated)


def head_norm(c, name, x3, square, stat, n, width, eps, centered, after):
    nc = c.nc
    s, r = stat[:, 0, :], stat[:, 1, :]
    with nc.Block(name) as block:

        @block.vector
        def _(dve):
            if centered:
                c.dve(dve, nc.vector.tensor_reduce(s, x3, AX.X, ALU.add))
                c.dve(dve, nc.vector.tensor_scalar(s, s, 1.0 / width, None, ALU.mult))
                c.dve(dve, nc.vector.tensor_tensor(x3, x3, s.unsqueeze(2).broadcast_to([P, n, width]), ALU.subtract))
            c.dve(dve, nc.vector.tensor_tensor(square, x3, x3, ALU.mult))
            c.dve(dve, nc.vector.tensor_reduce(s, square, AX.X, ALU.add))
            nc.vector.tensor_scalar(s, s, 1.0 / width, eps, ALU.mult, ALU.add).then_inc(c.dve_done.sem, 1)
            dve.wait_ge(c.act_done.sem, c.act_done.at(1))
            c.dve(dve, nc.vector.reciprocal(r, r))
            c.dve(dve, nc.vector.tensor_tensor(x3, x3, r.unsqueeze(2).broadcast_to([P, n, width]), ALU.mult))
            after(dve)

        @block.scalar
        def _(act):
            act.wait_ge(c.dve_done.sem, c.dve_done.at(1))
            nc.scalar.activation(r, s, ACT.Sqrt).then_inc(c.act_done.sem, 1)

    c.dve_done.passed(1)
    c.act_done.passed(1)


def first_gla(c, A, qk, v, rank, y):
    nc = c.nc
    MID = P // 2 - 1
    CLAMP = 40.0
    with ExitStack() as ctx:
        def sb(name, shape, dt=F32):
            return ctx.enter_context(nc.sbuf_tensor(name, shape, dt))

        wa = sb("w_alpha_s", [RANK, GKW])
        ba = sb("b_alpha_s", [P, 1])
        la = sb("log_alpha", [P, SEQ])
        xa = sb("alpha_x", [P, SEQ])
        t1 = sb("gt1", [P, SEQ])
        t2 = sb("gt2", [P, SEQ])
        F = sb("cum_alpha", [P, SEQ])
        onerow = sb("gla_ones", [P, P])
        bd = sb("gla_blocks", [P, GW])
        diff = sb("gla_diff", [P, TT])
        into = sb("gla_into", [P, TT])
        outof = sb("gla_outof", [P, TT])
        ktok = sb("gla_ktok", [P, TT, P])
        at = sb("gla_at", [P, 2, SEQ])
        state = sb("gla_state", [P, 2, GW])
        hout = sb("gla_out", [P, TT, GW])
        square = sb("gla_square", [P, TT * GH, GDV])
        stat = sb("gla_stat", [P, 2, TT * GH])
        gg = sb("gla_norm", [P, GW])
        q, k = qk[:, 0, :], qk[:, 1, :]

        with nc.Block("gla_decays") as block:

            @block.sync
            def _(sp):
                sp.dma_start(wa[:], A["w_alpha"].rearrange("a r k -> (a r) k")).then_inc(c.loaded.sem, 16)
                sp.dma_start(ba[:], column(A["b_alpha"].rearrange("a n -> (a n)"), 1), allow_slow_non_contiguous=True).then_inc(c.loaded.sem, 16)
                sp.dma_start(gg[:], over_partitions(A["gla_norm_g"].rearrange("a n -> (a n)"), GW)).then_inc(c.loaded.sem, 16)
                sp.wait_ge(c.loaded.sem, c.loaded.at(3))

            @block.gpsimd
            def _(pool):
                nc.gpsimd.memset(onerow[:], 1.0)
                nc.gpsimd.memset(state[:], 0.0)
                c.pool(pool, nc.gpsimd.memset(bd[:], 0.0))
                for h in range(GH):
                    nc.gpsimd.memset(bd[h * GDK:(h + 1) * GDK, h * GDV:(h + 1) * GDV], 1.0)

            @block.tensor
            def _(pe):
                pe.wait_ge(c.loaded.sem, c.loaded.at(3))
                nc.tensor.matmul(c.banks[:, 0, :], wa[:], rank[:], start=True, stop=True).then_inc(c.products.sem, 1)

            @block.vector
            def _(dve):
                dve.wait_ge(c.loaded.sem, c.loaded.at(3))
                dve.wait_ge(c.products.sem, c.products.at(1))
                c.dve(dve, nc.vector.tensor_scalar(xa[:], c.banks[:, 0, :], ba[:], None, ALU.add))
                log_sigmoid(c, dve, c.dve_done, c.act_done, xa[:], t1[:], t2[:], la[:])
                c.dve(dve, nc.vector.tensor_scalar(la[:], la[:], 1.0 / TAU, None, ALU.mult))

            @block.scalar
            def _(act):
                log_sigmoid_act(c, act, c.dve_done, c.act_done, t1[:], t2[:])

        c.loaded.passed(3)
        c.products.passed(1)
        c.dve_done.passed(1)
        c.act_done.passed(1)

        with nc.Block("gla_scaled") as block:

            @block.vector
            def _(dve):
                for t in range(TT):
                    s = slice(t * P, (t + 1) * P)
                    last = nc.vector.tensor_tensor_scan(F[:, s], onerow[:], la[:, s], 0.0, ALU.mult, ALU.add)
                c.dve(dve, last)
                ends = F[:].rearrange("p (t s) -> p t s", t=TT)
                nc.vector.tensor_tensor(diff[:], ends[:, :, P - 1], ends[:, :, MID], ALU.subtract)
                for t in range(TT):
                    s, mid = slice(t * P, (t + 1) * P), F[:, t * P + MID:t * P + MID + 1]
                    nc.vector.tensor_scalar(t1[:, s], F[:, s], mid, CLAMP, ALU.subtract, ALU.min)
                    last = nc.vector.tensor_scalar(t2[:, s], F[:, s], mid, -CLAMP, ALU.subtract, ALU.max)
                last.then_inc(c.dve_done.sem, 1)
                dve.wait_ge(c.act_done.sem, c.act_done.at(1))
                nc.vector.scalar_tensor_tensor(out=q, in0=q, scalar=GDK ** -0.5, in1=t1[:], op0=ALU.mult, op1=ALU.mult)
                nc.vector.tensor_tensor(k, k, t2[:], ALU.mult).then_inc(c.dve_done.sem, 1)
                dve.wait_ge(c.products.sem, c.products.at(1))
                nc.vector.tensor_copy(ktok[:], c.banks[:, 0, :].rearrange("p (t s) -> p t s", t=TT))

            @block.scalar
            def _(act):
                act.wait_ge(c.dve_done.sem, c.dve_done.at(1))
                nc.scalar.activation(t1[:], t1[:], ACT.Exp)
                nc.scalar.activation(into[:], F[:].rearrange("p (t s) -> p t s", t=TT)[:, :, MID], ACT.Exp)
                nc.scalar.activation(outof[:], diff[:], ACT.Exp)
                nc.scalar.activation(t2[:], t2[:], ACT.Exp, scale=-1.0).then_inc(c.act_done.sem, 1)

            @block.tensor
            def _(pe):
                pe.wait_ge(c.dve_done.sem, c.dve_done.at(2))
                for t in range(TT):
                    last = nc.tensor.transpose(c.banks[:, 0, t * P:(t + 1) * P], k[:, t * P:(t + 1) * P], c.ident[:])
                last.then_inc(c.products.sem, 1)

        c.products.passed(1)
        c.dve_done.passed(2)
        c.act_done.passed(1)

        masked, out_ready, used, state_ready = c.att_masked, c.att_out, c.dve_done, c.att_max
        with nc.Block("gla_tiles") as block:

            @block.tensor
            def _(pe):
                for t in range(TT):
                    s = slice(t * P, (t + 1) * P)
                    for h in range(GH):
                        r = slice(h * GDK, (h + 1) * GDK)
                        last = nc.tensor.matmul(c.banks[:, h, s], k[r, s], q[r, s], start=True, stop=True)
                last.then_inc(c.products.sem, 1)
                for t in range(TT):
                    s = slice(t * P, (t + 1) * P)
                    if t >= 2:
                        pe.wait_ge(used.sem, used.at(t - 1))
                        pe.wait_ge(state_ready.sem, state_ready.at(2 * (t - 1)))
                    nc.tensor.matmul(c.banks[:, 6 + t % 2, 0:GW], ktok[:, t, :], v[:, t, :], start=True,
                                     stop=True).then_inc(c.att_turned.sem, 1)
                    pe.wait_ge(masked.sem, masked.at(t + 1))
                    pe.wait_ge(state_ready.sem, state_ready.at(2 * t + 1))
                    for h in range(GH):
                        o = c.banks[:, 4 + t % 2, h * GDV:(h + 1) * GDV]
                        nc.tensor.matmul(o, q[:, s], state[:, t % 2, h * GDV:(h + 1) * GDV], start=True, stop=False)
                        last = nc.tensor.matmul(o, at[:, t % 2, h * P:(h + 1) * P], v[:, t, h * GDV:(h + 1) * GDV],
                                                start=False, stop=True)
                    last.then_inc(out_ready.sem, 1)

            @block.vector
            def _(dve):
                dve.wait_ge(c.products.sem, c.products.at(1))
                for t in range(TT):
                    if t >= 2:
                        dve.wait_ge(out_ready.sem, out_ready.at(t - 1))
                    nc.vector.tensor_tensor(at[:, t % 2, :].rearrange("p (h s) -> p h s", h=GH),
                                            c.banks[:, 0:GH, t * P:(t + 1) * P],
                                            c.upper[:].unsqueeze(1).broadcast_to([P, GH, P]), ALU.mult).then_inc(masked.sem, 1)
                    cur, nxt = state[:, t % 2, :], state[:, (t + 1) % 2, :]
                    nc.vector.tensor_scalar(cur, cur, into[:, t:t + 1], None, ALU.mult).then_inc(state_ready.sem, 1)
                    dve.wait_ge(c.att_turned.sem, c.att_turned.at(t + 1))
                    if t >= 1:
                        dve.wait_ge(out_ready.sem, out_ready.at(t))
                    c.dve(dve, nc.vector.tensor_tensor(nxt, c.banks[:, 6 + t % 2, 0:GW], bd[:], ALU.mult))
                    c.dve(dve, nc.vector.tensor_tensor(nxt, nxt, cur, ALU.add))
                    nc.vector.tensor_scalar(nxt, nxt, outof[:, t:t + 1], None, ALU.mult).then_inc(state_ready.sem, 1)
                    dve.wait_ge(state_ready.sem, state_ready.at(2 * (t + 1)))
                    dve.wait_ge(out_ready.sem, out_ready.at(t + 1))
                    nc.vector.tensor_copy(hout[:, t, :], c.banks[:, 4 + t % 2, 0:GW]).then_inc(used.sem, 1)

        c.products.passed(1)
        for signal in (masked, out_ready, used, c.att_turned):
            signal.passed(TT)
        state_ready.passed(2 * TT)

        def gated(dve):
            place = y[:, :, AW + MW:D]
            c.dve(dve, nc.vector.tensor_tensor(hout[:], hout[:], gg[:].unsqueeze(1).broadcast_to([P, TT, GW]), ALU.mult))
            nc.vector.tensor_tensor(place, place, hout[:], ALU.mult)

        head_norm(c, "gla_norm", hout[:].rearrange("p t (h d) -> p (t h) d", h=GH), square[:], stat[:], TT * GH, GDV,
                  RMS_EPS, False, gated)


def copied(c):
    nc = c.nc

    def evac(who, f, dst, src):
        if who == "act":
            return nc.scalar.activation(dst, src, ACT.Copy)
        return nc.vector.tensor_copy(dst, src)

    return evac


def out_projection(c, name, weights, y, yT, evac):
    turned(c, name + "_turn", lambda t, f: y[:, t, f * P:(f + 1) * P], lambda f: yT[:, f, :], DT, copied(c))
    w = weights.rearrange("(k p) n -> p k n", p=P)
    half = D // 2
    spots = [c.ring[:, 2 * g:2 * g + 2, :].rearrange("p a (k n) -> p (a k) n", k=4) for g in range(2)]
    loads = [(spots[g][:, :, :], w[:, g * 0:DT, :][:, :, g * half:(g + 1) * half], None) for g in range(2)]
    units = [dict(load=n, k=DT, lhsT=lambda k, t=t: yT[:, k, t * P:(t + 1) * P], rhs=lambda k, n=n: spots[n][:, k, :],
                  out=lambda b: b, engine="dve", evac=lambda b, t=t, n=n: evac(t, n, b))
             for n in range(2) for t in range(TT)]
    projection(c, name, loads, units)


class Carve:

    def __init__(self, flat):
        self.flat = flat
        self.at = 0

    def __call__(self, *shape):
        n = 1
        for d in shape:
            n *= d
        piece = self.flat[:, self.at:self.at + n]
        self.at += n
        assert self.at <= self.flat.shape[1], self.at
        if len(shape) == 1:
            return piece
        names = " ".join("abcde"[i] for i in range(len(shape)))
        sizes = {"abcde"[i]: d for i, d in enumerate(shape[1:], 1)}
        return piece.rearrange(f"p ({names}) -> p {names}", **sizes)


def spread(v, n):
    return v.unsqueeze(1).broadcast_to([P, n, v.shape[-1]])


def modulation(c, A, mod):
    nc = c.nc
    passes, wide = 3, 2048
    ada = A["ada_w_2"].rearrange("a (k p) n -> p (a k) n", p=P)
    with ExitStack() as ctx:
        col = ctx.enter_context(nc.sbuf_tensor("c_col", [P, DT], F32))
        row = ctx.enter_context(nc.sbuf_tensor("mod_row", [1, 6 * D], F32))
        brow = ctx.enter_context(nc.sbuf_tensor("ada_b_row", [1, 6 * D], F32))
        with nc.Block("modulation") as block:

            @block.sync
            def _(sp):
                sp.dma_start(col[:], column(A["c_2"].rearrange("a d -> (a d)"), DT),
                             allow_slow_non_contiguous=True).then_inc(c.loaded.sem, 16)
                sp.dma_start(brow[:], A["ada_b_2"]).then_inc(c.loaded.sem, 16)
                for i in range(passes * DT):
                    if i >= RING:
                        sp.wait_ge(c.products.sem, c.products.at(i - RING + 1))
                    q, k = i // DT, i % DT
                    sp.dma_start(c.ring[:, i % RING, :], ada[:, k, q * wide:(q + 1) * wide]).then_inc(
                        c.landed[i % RING].sem, 16)
                sp.wait_ge(c.dve_done.sem, c.dve_done.at(passes * 4))
                sp.dma_start(mod.rearrange("(a n) -> a n", a=1), row[:]).then_inc(c.stored.sem, 16)
                sp.wait_ge(c.stored.sem, c.stored.at(1))

            @block.scalar
            def _(act):
                act.wait_ge(c.loaded.sem, c.loaded.at(2))
                nc.scalar.activation(col[:], col[:], ACT.Silu).then_inc(c.act_done.sem, 1)

            @block.tensor
            def _(pe):
                pe.wait_ge(c.act_done.sem, c.act_done.at(1))
                for i in range(passes * DT):
                    q, k = i // DT, i % DT
                    landed = c.landed[i % RING]
                    pe.wait_ge(landed.sem, landed.at(i // RING + 1))
                    if k == 0 and q >= 2:
                        pe.wait_ge(c.dve_done.sem, c.dve_done.at(4 * (q - 1)))
                    for n in range(4):
                        last = nc.tensor.matmul(c.banks[0:1, (q % 2) * 4 + n, :], col[:, k:k + 1],
                                                c.ring[:, i % RING, n * 512:(n + 1) * 512],
                                                start=(k == 0), stop=(k == DT - 1))
                    last.then_inc(c.products.sem, 1)

            @block.vector
            def _(dve):
                dve.wait_ge(c.loaded.sem, c.loaded.at(2))
                for q in range(passes):
                    dve.wait_ge(c.products.sem, c.products.at((q + 1) * DT))
                    for n in range(4):
                        s = slice(q * wide + n * 512, q * wide + (n + 1) * 512)
                        nc.vector.tensor_tensor(row[:, s], c.banks[0:1, (q % 2) * 4 + n, :], brow[:, s],
                                                ALU.add).then_inc(c.dve_done.sem, 1)

    c.loaded.passed(2)
    c.stored.passed(1)
    c.act_done.passed(1)
    c.products.passed(passes * DT)
    c.dve_done.passed(passes * 4)
    for i in range(RING):
        c.landed[i].passed(passes * DT // RING)


def layer_norm(c, name, src, dst, vectors, then, before=None):
    nc = c.nc
    with ExitStack() as ctx:
        stats = ctx.enter_context(nc.sbuf_tensor(name + "_stats", [P, TT, 2, 6], F32))
        mv = ctx.enter_context(nc.sbuf_tensor(name + "_mv", [P, TT, 2], F32))
        rstd = ctx.enter_context(nc.sbuf_tensor(name + "_rstd", [P, TT], F32))
        g, b = vectors[0][0], vectors[1][0]
        with nc.Block(name) as block:

            @block.sync
            def _(sp):
                for place, vector in vectors:
                    sp.dma_start(place, over_partitions(vector, D)).then_inc(c.loaded.sem, 16)

            @block.vector
            def _(dve):
                if before is not None:
                    before(dve)
                for t in range(TT):
                    for half in range(2):
                        last = nc.vector.bn_stats(stats[:, t, half, :], src(t)[:, half * 512:(half + 1) * 512])
                c.dve(dve, last)
                for t in range(TT):
                    last = nc.vector.bn_aggr(mv[:, t, :], stats[:, t, :, :].rearrange("p a b -> p (a b)"))
                c.dve(dve, last)
                nc.vector.tensor_scalar(rstd[:], mv[:, :, 1], LN_EPS, None, ALU.add).then_inc(c.dve_done.sem, 1)
                dve.wait_ge(c.act_done.sem, c.act_done.at(1))
                c.dve(dve, nc.vector.reciprocal(rstd[:], rstd[:]))
                dve.wait_ge(c.loaded.sem, c.loaded.at(len(vectors)))
                for t in range(TT):
                    c.dve(dve, nc.vector.tensor_scalar(dst(t), src(t), mv[:, t, 0:1], rstd[:, t:t + 1],
                                                       ALU.subtract, ALU.mult))
                    c.dve(dve, nc.vector.tensor_tensor(dst(t), dst(t), g, ALU.mult))
                    c.dve(dve, nc.vector.tensor_tensor(dst(t), dst(t), b, ALU.add))
                    then(dve, t)

            @block.scalar
            def _(act):
                act.wait_ge(c.dve_done.sem, c.dve_done.at(1))
                nc.scalar.activation(rstd[:], rstd[:], ACT.Sqrt).then_inc(c.act_done.sem, 1)

    c.loaded.passed(len(vectors))
    c.dve_done.passed(1)
    c.act_done.passed(1)


def second_block(c, A, Y, out):
    nc = c.nc
    flat = c.ring[:].rearrange("p a b -> p (a b)")
    mod = nc.dram_tensor("mod_scratch", [6 * D], F32).ap()
    part = lambda i: mod[i * D:(i + 1) * D]
    modulation(c, A, mod)
    with ExitStack() as ctx:
        h = ctx.enter_context(nc.sbuf_tensor("h_mix", [P, TT, D], F32))
        hT = c.ring[:, RING - 2:RING, :].rearrange("p a (k s) -> p (a k) s", k=DT // 2)
        with ExitStack() as raw_free:
            with ExitStack() as inner:
                vec = inner.enter_context(nc.sbuf_tensor("enter_vectors", [P, 5, D], F32))
                stat = inner.enter_context(nc.sbuf_tensor("final_stat", [P, 2 * TT], F32))
                with nc.Block("load_final_g") as block:
                    @block.sync
                    def _(sp):
                        sp.dma_start(vec[:, 4, :], over_partitions(A["final_g"], D)).then_inc(c.loaded.sem, 16)
                        sp.wait_ge(c.loaded.sem, c.loaded.at(1))
                c.loaded.passed(1)
                rms_rows(c, "rms_final", lambda i: c.x[:, i, :], lambda i: h[:, i, :], lambda i: h[:, i, :], stat, TT, D,
                         RMS_EPS, lambda dve, i: c.dve(dve, nc.vector.tensor_tensor(h[:, i, :], h[:, i, :], vec[:, 4, :], ALU.mult)))

                def modulated(dve, t):
                    c.dve(dve, nc.vector.scalar_tensor_tensor(out=h[:, t, :], in0=vec[:, 2, :], scalar=1.0, in1=c.x[:, t, :],
                                                              op0=ALU.add, op1=ALU.mult))
                    nc.vector.tensor_tensor(h[:, t, :], h[:, t, :], vec[:, 3, :], ALU.add)

                layer_norm(c, "embedding_norm", lambda t: h[:, t, :], lambda t: c.x[:, t, :],
                           [(vec[:, 0, :], A["emb_ln_g_2"]), (vec[:, 1, :], A["emb_ln_b_2"]),
                            (vec[:, 2, :], part(1)), (vec[:, 3, :], part(0))], modulated)
            turned(c, "turn_h", lambda t, f: h[:, t, f * P:(f + 1) * P], lambda f: hT[:, f, :], DT, copied(c))
            latent_attention(c, A, hT, h, flat)
            raw_free = ExitStack()
            raw = raw_free.enter_context(nc.sbuf_tensor("rwkv_raw", [P, RWKV_IN // P * (SEQ + 1)], F32))
            rwkv_projection(c, A, hT, raw)
        rwkv(c, A, raw, h, flat)
        raw_free.close()
        gates = ctx.enter_context(nc.sbuf_tensor("gates", [P, TT, TOPK], F32))
        slots = ctx.enter_context(nc.sbuf_tensor("token_slots", [P, TT, TOPK], I32))
        plan = ctx.enter_context(nc.sbuf_tensor("extra_plan", [1, 1 + EXTRA], I32))
        with ExitStack() as inner:
            h_rows, slot_tok = mixed(c, A, h, part, inner, gates, slots, plan)
        experts(c, A, h_rows, slot_tok, plan, Y)
        combine(c, A, h, Y, gates, slots, part, out)


def latent_attention(c, A, hT, mix, flat):
    nc = c.nc
    w = Carve(flat)
    w_a = w(DT, MLA_IN)
    uq = w(2, NH * QK)
    uk = w(NH * NOPE)
    uv = w(NH * VD)
    lat = w(TT, MLA_IN)
    latn = w(TT, QL + KVL)
    latT = w(3, SEQ)
    q_tok = w(TT, NH, QK)
    v_tok = w(TT, NH * VD)
    with ExitStack() as ctx:
        def sb(name, shape, dt=F32):
            return ctx.enter_context(nc.sbuf_tensor(name, shape, dt))

        qT = sb("mla_qT", [QK, NH, SEQ])
        kT = sb("mla_kT", [QK, NH, SEQ])
        gcol = sb("lat_g", [P, 3])
        stat = sb("lat_stat", [P, 2 * TT])
        out_g = sb("mla_out_gain", [P, NH * VD])
        mask = sb("causal_bias", [P, SEQ])
        small = ExitStack()
        pos_i = small.enter_context(nc.sbuf_tensor("pos_i", [P, TT], I32))
        pos = small.enter_context(nc.sbuf_tensor("pos_f", [P, TT], F32))
        inv = small.enter_context(nc.sbuf_tensor("inv_freq_rows", [P, ROPE // 2], F32))
        ang = small.enter_context(nc.sbuf_tensor("angle", [P, 2, TT, ROPE // 2], F32))
        turns = small.enter_context(nc.sbuf_tensor("turns", [P, 2, TT, ROPE // 2], F32))
        turns_i = small.enter_context(nc.sbuf_tensor("turns_i", [P, 2, TT, ROPE // 2], I32))
        krot = small.enter_context(nc.sbuf_tensor("k_rotated", [P, TT, ROPE], F32))
        r4 = small.enter_context(nc.sbuf_tensor("rope_parts", [P, 4, NH, ROPE // 2], F32))
        k_tok = q_tok

        w_in = A["w_in_2"].rearrange("a (k p) n -> p (a k) n", p=P)
        projection(c, "project_latents", [(w_a, w_in[:, :, 0:MLA_IN], None)],
                   [dict(load=0, k=DT, lhsT=lambda k, t=t: hT[:, k, t * P:(t + 1) * P], rhs=lambda k: w_a[:, k, :],
                         out=lambda b: b[:, 0:MLA_IN], engine="dve",
                         evac=lambda b, t=t: nc.vector.tensor_copy(lat[:, t, :], b[:, 0:MLA_IN])) for t in range(TT)])

        with nc.Block("rotary_tables") as block:

            @block.sync
            def _(sp):
                slow = dict(allow_slow_non_contiguous=True)
                sp.dma_start(pos_i[:], column(A["positions_2"].rearrange("a s -> (a s)"), TT), **slow).then_inc(c.loaded.sem, 16)
                sp.dma_start(inv[:], over_partitions(A["inv_freq"], ROPE // 2)).then_inc(c.loaded.sem, 16)
                sp.dma_start(gcol[:, 0:2], column(A["q_norm_g_2"].rearrange("a n -> (a n)"), 2), **slow).then_inc(c.loaded.sem, 16)
                sp.dma_start(gcol[:, 2:3], column(A["kv_norm_g_2"].rearrange("a n -> (a n)"), 1), **slow).then_inc(c.loaded.sem, 16)
                sp.dma_start(out_g[:], over_partitions(A["mla_out_g_2"].rearrange("a n -> (a n)"), NH * VD)).then_inc(c.loaded.sem, 16)
                sp.dma_start(uq, A["w_uq_2"].rearrange("a (k p) n -> p (a k) n", p=P)).then_inc(c.loaded.sem, 16)
                sp.dma_start(uk, A["w_uk_2"].rearrange("a k n -> (a k) n")).then_inc(c.loaded.sem, 16)
                sp.dma_start(uv, A["w_uv_2"].rearrange("a k n -> (a k) n")).then_inc(c.loaded.sem, 16)
                sp.wait_ge(c.loaded.sem, c.loaded.at(8))

            @block.gpsimd
            def _(pool):
                c.pool(pool, nc.gpsimd.memset(mask[:], 0.0))
                nc.gpsimd.affine_select(out=mask[:, SEQ - P:SEQ], in_=mask[:, SEQ - P:SEQ], compare_op=ALU.is_ge,
                                        fill=NEG, base=0, pattern=[[-1, P]], channel_multiplier=1)

            @block.vector
            def _(dve):
                pi = float(np.pi)
                limit = 3.1415925
                dve.wait_ge(c.loaded.sem, c.loaded.at(8))
                c.dve(dve, nc.vector.tensor_copy(pos[:], pos_i[:]))
                for t in range(TT):
                    last = nc.vector.tensor_scalar(ang[:, 0, t, :], inv[:], pos[:, t:t + 1], None, ALU.mult)
                c.dve(dve, last)
                c.dve(dve, nc.vector.tensor_scalar(turns[:, 0], ang[:, 0], 1.0 / (2 * pi), None, ALU.mult))
                c.dve(dve, nc.vector.tensor_copy(turns_i[:, 0], turns[:, 0]))
                c.dve(dve, nc.vector.tensor_copy(turns[:, 0], turns_i[:, 0]))
                for part in (-6.28125, -(2 * pi - 6.28125)):
                    c.dve(dve, nc.vector.scalar_tensor_tensor(out=ang[:, 0], in0=turns[:, 0], scalar=part, in1=ang[:, 0],
                                                              op0=ALU.mult, op1=ALU.add))
                c.dve(dve, nc.vector.tensor_scalar(ang[:, 1], ang[:, 0], pi / 2, None, ALU.add))
                for compare, turn in ((ALU.is_gt, -2 * pi), (ALU.is_lt, 2 * pi)):
                    edge = pi if compare == ALU.is_gt else -pi
                    c.dve(dve, nc.vector.tensor_scalar(turns[:], ang[:], edge, turn, compare, ALU.mult))
                    c.dve(dve, nc.vector.tensor_tensor(ang[:], ang[:], turns[:], ALU.add))
                nc.vector.tensor_scalar(ang[:], ang[:], limit, -limit, ALU.min, ALU.max).then_inc(c.dve_done.sem, 1)

            @block.scalar
            def _(act):
                act.wait_ge(c.dve_done.sem, c.dve_done.at(1))
                nc.scalar.activation(ang[:], ang[:], ACT.Sin).then_inc(c.act_done.sem, 1)

        c.loaded.passed(8)
        c.dve_done.passed(1)
        c.act_done.passed(1)

        rms_rows(c, "rms_q", lambda i: lat[:, i, 0:QL], lambda i: latn[:, i, 0:QL], lambda i: latn[:, i, 0:QL], stat, TT, QL, RMS_EPS)
        rms_rows(c, "rms_kv", lambda i: lat[:, i, QL:QL + KVL], lambda i: latn[:, i, QL:QL + KVL],
                 lambda i: latn[:, i, QL:QL + KVL], stat, TT, KVL, RMS_EPS)

        def scaled(who, f, dst, src):
            if who == "act":
                return nc.scalar.activation(dst, src, ACT.Copy, scale=gcol[:, f:f + 1])
            return nc.vector.tensor_scalar(dst, src, gcol[:, f:f + 1], None, ALU.mult)

        turned(c, "turn_latents", lambda t, f: latn[:, t, f * P:(f + 1) * P], lambda f: latT[:, f, :], 3, scaled)

        half = NH * QK // 2
        units = [dict(load=-1, k=2, lhsT=lambda k, t=t: latT[:, k, t * P:(t + 1) * P],
                      rhs=lambda k, n=n: uq[:, k, n * half:(n + 1) * half], out=lambda b: b[:, 0:half],
                      engine=("act", "dve")[n],
                      evac=(lambda b, t=t: nc.scalar.activation(q_tok[:, t, 0:NH // 2, :], b[:, 0:half].rearrange("p (h d) -> p h d", d=QK), ACT.Copy),
                            lambda b, t=t: nc.vector.tensor_copy(q_tok[:, t, NH // 2:NH, :], b[:, 0:half].rearrange("p (h d) -> p h d", d=QK)))[n])
                 for t in range(TT) for n in range(2)]
        projection(c, "queries", [], units)

        def rotate(dve, x, heads, t, dst=None):
            sin = ang[:, 0, t, :].unsqueeze(1).broadcast_to([P, heads, ROPE // 2])
            cos = ang[:, 1, t, :].unsqueeze(1).broadcast_to([P, heads, ROPE // 2])
            even, odd = x[:, :, 0:ROPE:2], x[:, :, 1:ROPE:2]
            for i, (a, b) in enumerate(((even, cos), (odd, sin), (even, sin), (odd, cos))):
                last = nc.vector.tensor_tensor(r4[:, i, 0:heads, :], a, b, ALU.mult)
            c.dve(dve, last)
            dst = x if dst is None else dst
            nc.vector.tensor_tensor(dst[:, :, 0:ROPE:2], r4[:, 0, 0:heads, :], r4[:, 1, 0:heads, :], ALU.subtract)
            c.dve(dve, nc.vector.tensor_tensor(dst[:, :, 1:ROPE:2], r4[:, 2, 0:heads, :], r4[:, 3, 0:heads, :], ALU.add))

        with nc.Block("rotate_queries") as block:

            @block.vector
            def _(dve):
                for t in range(TT):
                    rotate(dve, q_tok[:, t, :, NOPE:QK], NH, t)
                    rotate(dve, lat[:, t:t + 1, QL + KVL:MLA_IN], 1, t, krot[:, t:t + 1, :])

        def head_turn(name, dst):
            with nc.Block(name) as block:

                @block.tensor
                def _(pe):
                    for f in range(NH):
                        for t in range(TT):
                            last = nc.tensor.transpose(c.banks[0:QK, f, t * P:(t + 1) * P], q_tok[:, t, f, :], c.ident[:])
                        last.then_inc(c.products.sem, 1)

                @block.scalar
                def _(act):
                    for f in range(0, NH, 2):
                        act.wait_ge(c.products.sem, c.products.at(f + 1))
                        nc.scalar.activation(dst[:, f, :], c.banks[0:QK, f, :], ACT.Copy)

                @block.vector
                def _(dve):
                    for f in range(1, NH, 2):
                        dve.wait_ge(c.products.sem, c.products.at(f + 1))
                        nc.vector.tensor_copy(dst[:, f, :], c.banks[0:QK, f, :])

            c.products.passed(NH)

        head_turn("turn_queries", qT)
        units = []
        for t in range(TT):
            units.append(dict(load=-1, k=1, lhsT=lambda k, t=t: latT[:, 2, t * P:(t + 1) * P], rhs=lambda k: uk,
                              out=lambda b: b, engine="dve",
                              evac=lambda b, t=t: nc.vector.tensor_copy(k_tok[:, t, :, 0:NOPE], b.rearrange("p (h d) -> p h d", h=NH))))
            units.append(dict(load=-1, k=1, lhsT=lambda k, t=t: latT[:, 2, t * P:(t + 1) * P], rhs=lambda k: uv,
                              out=lambda b: b, engine="act",
                              evac=lambda b, t=t: nc.scalar.activation(v_tok[:, t, :], b, ACT.Copy)))
        projection(c, "keys_values", [], units)
        with nc.Block("shared_rotary_key") as block:

            @block.vector
            def _(dve):
                for t in range(TT):
                    nc.vector.tensor_copy(k_tok[:, t, :, NOPE:QK], krot[:, t, :].unsqueeze(1).broadcast_to([P, NH, ROPE]))

        head_turn("turn_keys", kT)
        small.close()

        def finish(h, t, product, rinv):
            return nc.vector.tensor_scalar(mix[:, t, h * VD:(h + 1) * VD], product, rinv, None, ALU.mult)

        attention(c, "causal_attention", NH, lambda h: qT[:, h, :], lambda h: kT[:, h, :],
                  lambda b, h: v_tok[:, b, h * VD:(h + 1) * VD], VD, QK ** -0.5, lambda h: mask[:], None, finish)

        W = NH * VD
        junk = Carve(flat)(TT, W)
        rms_rows(c, "rms_mla", lambda i: mix[:, i, 0:W], lambda i: mix[:, i, 0:W], lambda i: junk[:, i, :], stat, TT, W,
                 RMS_EPS, lambda dve, i: c.dve(dve, nc.vector.tensor_tensor(mix[:, i, 0:W], mix[:, i, 0:W], out_g[:], ALU.mult)))


def rwkv_projection(c, A, hT, raw):
    nc = c.nc
    tiles = RWKV_IN // P
    p = raw[:].rearrange("p (f s) -> p f s", f=tiles)
    w_in = A["w_in_2"].rearrange("a (k p) n -> p (a k) n", p=P)
    spots = [c.ring[:, g, :].rearrange("p (k n) -> p k n", k=DT) for g in range(tiles // 2)]
    loads = [(spots[g], w_in[:, :, MLA_IN + g * 2 * P:MLA_IN + (g + 1) * 2 * P], None) for g in range(tiles // 2)]
    units = [dict(load=f // 2, k=DT, lhsT=lambda k, f=f: spots[f // 2][:, k, (f % 2) * P:(f % 2 + 1) * P],
                  rhs=lambda k: hT[:, k, :], out=lambda b: b, engine=("act", "dve")[f % 2],
                  evac=(lambda b, f=f: nc.scalar.activation(p[:, f, 1:SEQ + 1], b, ACT.Copy),
                        lambda b, f=f: nc.vector.tensor_copy(p[:, f, 1:SEQ + 1], b))[f % 2]) for f in range(tiles)]
    projection(c, "project_rwkv", loads, units)
    with ExitStack() as ctx:
        mu = ctx.enter_context(nc.sbuf_tensor("rwkv_mu_col", [P, tiles], F32))
        d = ctx.enter_context(nc.sbuf_tensor("rwkv_step", [P, 2, SEQ], F32))
        with nc.Block("token_shift") as block:

            @block.sync
            def _(sp):
                sp.dma_start(mu[:], column(A["rwkv_mu_2"].rearrange("a n -> (a n)"), tiles),
                             allow_slow_non_contiguous=True).then_inc(c.loaded.sem, 16)

            @block.gpsimd
            def _(pool):
                c.pool(pool, nc.gpsimd.memset(p[:, :, 0:1], 0.0))
                for f in range(tiles):
                    if f >= 2:
                        pool.wait_ge(c.dve_done.sem, c.dve_done.at(f - 1))
                    nc.gpsimd.tensor_tensor(d[:, f % 2, :], p[:, f, 0:SEQ], p[:, f, 1:SEQ + 1],
                                            ALU.subtract).then_inc(c.masks.sem, 1)

            @block.vector
            def _(dve):
                dve.wait_ge(c.loaded.sem, c.loaded.at(1))
                for f in range(tiles):
                    dve.wait_ge(c.masks.sem, c.masks.at(f + 1))
                    nc.vector.scalar_tensor_tensor(out=p[:, f, 1:SEQ + 1], in0=d[:, f % 2, :], scalar=mu[:, f:f + 1],
                                                   in1=p[:, f, 1:SEQ + 1], op0=ALU.mult, op1=ALU.add).then_inc(c.dve_done.sem, 1)

    c.loaded.passed(1)
    c.masks.passed(tiles)
    c.dve_done.passed(tiles)


def rwkv(c, A, raw, mix, flat):
    nc = c.nc
    tiles = RWKV_IN // P
    MID = P // 2 - 1
    p = raw[:].rearrange("p (f s) -> p f s", f=tiles)[:, :, 1:SEQ + 1]
    r, k, v = p[:, 0:RP, :], p[:, RP:2 * RP, :], p[:, 2 * RP:3 * RP, :]
    lora, gate_in = p[:, 3 * RP, :], p[:, 3 * RP + 1, :]
    w = Carve(flat)
    ar = w(RP, TT, 2, P)
    bT = w(RP, SEQ)
    kT = w(RP, SEQ)
    inverse = w(TT, RH, P)
    a = w(RP, SEQ)
    F = w(RP, SEQ)
    kk = w(RP, SEQ)
    e = w(RP, SEQ)
    with ExitStack() as ctx:
        def sb(name, shape, dt=F32):
            return ctx.enter_context(nc.sbuf_tensor(name, shape, dt))

        tok = sb("rwkv_tok", [P, 3, TT, RW])
        v_tok, b_tok, k_tok = tok[:, 0], tok[:, 1], tok[:, 2]
        into = sb("rwkv_into", [P, RP, TT])
        outof = sb("rwkv_outof", [P, RP, TT])
        bonus = sb("rwkv_bonus", [P, TT, RH])
        bd = sb("pair_blocks", [P, P])
        g2 = sb("rwkv_g2", [P, RW])
        with ExitStack() as inner:
            cols = inner.enter_context(nc.sbuf_tensor("rwkv_cols", [P, 6, RP], F32))
            w0, a0, k_k, k_a, r_k, omka = (cols[:, i, :] for i in range(6))
            wa2 = inner.enter_context(nc.sbuf_tensor("lora_w", [P, RW], F32))
            head_sum = inner.enter_context(nc.sbuf_tensor("pair_select", [P, 2], F32))

            with nc.Block("rwkv_gates") as block:

                @block.sync
                def _(sp):
                    for place, name in ((w0, "rwkv_w0_2"), (a0, "rwkv_a0_2"), (k_k, "rwkv_k_k_2"), (k_a, "rwkv_k_a_2")):
                        sp.dma_start(place, column(A[name].rearrange("a n -> (a n)"), RP),
                                     allow_slow_non_contiguous=True).then_inc(c.loaded.sem, 16)
                    sp.dma_start(r_k, column(A["rwkv_r_k_2"].rearrange("a h d -> (a h d)"), RP),
                                 allow_slow_non_contiguous=True).then_inc(c.loaded.sem, 16)
                    sp.dma_start(wa2[0:LORA_D, :], A["rwkv_w2_2"].rearrange("a k n -> (a k) n")).then_inc(c.loaded.sem, 16)
                    sp.dma_start(wa2[LORA_D:P, :], A["rwkv_a2_2"].rearrange("a k n -> (a k) n")).then_inc(c.loaded.sem, 16)
                    sp.dma_start(g2[:], A["rwkv_g2_2"].rearrange("a k n -> (a k) n")).then_inc(c.loaded.sem, 16)
                    sp.wait_ge(c.loaded.sem, c.loaded.at(8))

                @block.gpsimd
                def _(pool):
                    nc.gpsimd.memset(head_sum[:], 0.0)
                    c.pool(pool, nc.gpsimd.memset(bd[:], 0.0))
                    for j in range(2):
                        nc.gpsimd.memset(head_sum[j * 64:(j + 1) * 64, j:j + 1], 1.0)
                        nc.gpsimd.memset(bd[j * 64:(j + 1) * 64, j * 64:(j + 1) * 64], 1.0)

                @block.scalar
                def _(act):
                    nc.scalar.activation(lora[0:LORA_D, :], lora[0:LORA_D, :], ACT.Tanh).then_inc(c.act_done.sem, 1)
                    nc.scalar.activation(gate_in, gate_in, ACT.Sigmoid)
                    act.wait_ge(c.loaded.sem, c.loaded.at(8))
                    for f in range(RP):
                        act.wait_ge(c.products.sem, c.products.at(f + 1))
                        nc.scalar.activation(e[:, f, :], c.banks[:, f, :], ACT.Sigmoid, bias=w0[:, f:f + 1])
                        nc.scalar.activation(a[:, f, :], c.banks[:, 4 + f, :], ACT.Sigmoid, bias=a0[:, f:f + 1])

                @block.tensor
                def _(pe):
                    pe.wait_ge(c.loaded.sem, c.loaded.at(8))
                    pe.wait_ge(c.act_done.sem, c.act_done.at(1))
                    for f in range(RP):
                        nc.tensor.matmul(c.banks[:, f, :], wa2[0:LORA_D, f * P:(f + 1) * P], lora[0:LORA_D, :], start=True, stop=True)
                        nc.tensor.matmul(c.banks[:, 4 + f, :], wa2[LORA_D:P, f * P:(f + 1) * P], lora[LORA_D:P, :],
                                         start=True, stop=True).then_inc(c.products.sem, 1)

                @block.vector
                def _(dve):
                    dve.wait_ge(c.loaded.sem, c.loaded.at(8))
                    nc.vector.tensor_scalar(omka, k_a, -1.0, 1.0, ALU.mult, ALU.add)
                    for f in range(RP):
                        nc.vector.tensor_scalar(kk[:, f, :], k[:, f, :], k_k[:, f:f + 1], None, ALU.mult)

            c.loaded.passed(8)
            c.act_done.passed(1)
            c.products.passed(RP)

            by_tile = lambda x: x.rearrange("p f (t s) -> p (f t) s", t=TT)
            all_of = lambda x: x.rearrange("p f s -> p (f s)")
            decay_scale = -float(np.exp(-0.5))
            kk2 = ar.rearrange("p f t k s -> p (f t k s)")[:, 0:RP * SEQ]
            kk2f = kk2.rearrange("p (f s) -> p f s", f=RP)
            with nc.Block("rwkv_decays") as block:

                @block.tensor
                def _(pe):
                    pe.wait_ge(c.dve_done.sem, c.dve_done.at(1))
                    for f in range(RP):
                        last = nc.tensor.matmul(c.banks[:, f, :], bd[:], kk2f[:, f, :], start=True, stop=True)
                    last.then_inc(c.products.sem, 1)
                    pe.wait_ge(c.dve_done.sem, c.dve_done.at(2))
                    for t in range(TT):
                        for f in range(RP):
                            last = nc.tensor.matmul(c.banks[:, 4, t * RH + 2 * f:t * RH + 2 * f + 2],
                                                    bT[:, f, t * P:(t + 1) * P], head_sum[:], start=True, stop=True)
                    last.then_inc(c.products.sem, 1)

                @block.scalar
                def _(act):
                    act.wait_ge(c.products.sem, c.products.at(1))
                    for f in range(RP):
                        last = nc.scalar.activation(kT[:, f, :], c.banks[:, f, :], ACT.Sqrt)
                    last.then_inc(c.act_done.sem, 1)

                @block.vector
                def _(dve):
                    nc.vector.tensor_tensor(kk2, all_of(kk), all_of(kk), ALU.mult).then_inc(c.dve_done.sem, 1)
                    c.dve(dve, nc.vector.tensor_scalar(all_of(e), all_of(e), decay_scale, None, ALU.mult))
                    for f in range(RP):
                        nc.vector.tensor_scalar(inverse.rearrange("p t h s -> p (t h s)")[:, f * SEQ:(f + 1) * SEQ], a[:, f, :],
                                                k_a[:, f:f + 1], omka[:, f:f + 1], ALU.mult, ALU.add)
                        for t in range(TT):
                            s = slice(t * P, (t + 1) * P)
                            last = nc.vector.tensor_tensor_scan(F[:, f, s], c.ones[:], e[:, f, s], 0.0, ALU.mult, ALU.add)
                    c.dve(dve, last)
                    c.dve(dve, nc.vector.tensor_tensor(k, k, inverse.rearrange("p t h s -> p (t h s)")[:, 0:RP * SEQ].rearrange(
                        "p (f s) -> p f s", f=RP), ALU.mult))
                    for f in range(RP):
                        last = nc.vector.scalar_tensor_tensor(out=bT[:, f, :], in0=r[:, f, :], scalar=r_k[:, f:f + 1],
                                                              in1=k[:, f, :], op0=ALU.mult, op1=ALU.mult)
                    last.then_inc(c.dve_done.sem, 1)
                    dve.wait_ge(c.act_done.sem, c.act_done.at(1))
                    c.dve(dve, nc.vector.tensor_scalar(all_of(kT), all_of(kT), 1e-12, None, ALU.max))
                    c.dve(dve, nc.vector.reciprocal(all_of(kT), all_of(kT)))
                    c.dve(dve, nc.vector.tensor_tensor(all_of(kk), all_of(kk), all_of(kT), ALU.mult))
                    dve.wait_ge(c.products.sem, c.products.at(2))
                    nc.vector.tensor_copy(bonus[:].rearrange("p t h -> p (t h)"), c.banks[:, 4, 0:TT * RH])

            c.products.passed(2)
            c.dve_done.passed(2)
            c.act_done.passed(1)

            Fm = by_tile(F)
            ends = into[:].rearrange("p f t -> p (f t)")
            with nc.Block("rwkv_scaled") as block:

                @block.vector
                def _(dve):
                    nc.vector.tensor_copy(into[:].rearrange("p f t -> p (f t)"), Fm[:, :, MID])
                    c.dve(dve, nc.vector.tensor_tensor(outof[:].rearrange("p f t -> p (f t)"), Fm[:, :, P - 1], Fm[:, :, MID],
                                                       ALU.subtract))
                    c.dve(dve, nc.vector.tensor_tensor(Fm, Fm, ends.unsqueeze(2).broadcast_to([P, RP * TT, P]), ALU.subtract))
                    nc.vector.tensor_tensor(all_of(e), all_of(F), all_of(e), ALU.subtract).then_inc(c.dve_done.sem, 1)
                    dve.wait_ge(c.act_done.sem, c.act_done.at(2))
                    for f in range(RP):
                        nc.vector.scalar_tensor_tensor(out=ar[:, f, :, 0, :], in0=kk[:, f, :].rearrange("p (t s) -> p t s", t=TT),
                                                       scalar=-1.0, in1=e[:, f, :].rearrange("p (t s) -> p t s", t=TT),
                                                       op0=ALU.mult, op1=ALU.mult)
                        nc.vector.tensor_tensor(ar[:, f, :, 1, :], r[:, f, :].rearrange("p (t s) -> p t s", t=TT),
                                                ar[:, f, :, 1, :], ALU.mult)
                    c.dve(dve, nc.vector.tensor_tensor(all_of(bT), all_of(kk), all_of(a), ALU.mult))
                    dve.wait_ge(c.act_done.sem, c.act_done.at(3))
                    nc.vector.tensor_tensor(all_of(bT), all_of(bT), all_of(F), ALU.mult)
                    c.dve(dve, nc.vector.tensor_tensor(kT, k, F, ALU.mult))

                @block.scalar
                def _(act):
                    act.wait_ge(c.dve_done.sem, c.dve_done.at(1))
                    nc.scalar.activation(all_of(e), all_of(e), ACT.Exp).then_inc(c.act_done.sem, 1)
                    for f in range(RP):
                        last = nc.scalar.activation(ar[:, f, :, 1, :], F[:, f, :].rearrange("p (t s) -> p t s", t=TT), ACT.Exp)
                    last.then_inc(c.act_done.sem, 1)
                    act.wait_ge(c.act_done.sem, c.act_done.at(2))
                    nc.scalar.activation(all_of(F), all_of(F), ACT.Exp, scale=-1.0).then_inc(c.act_done.sem, 1)
                    nc.scalar.activation(into[:], into[:], ACT.Exp)
                    nc.scalar.activation(outof[:], outof[:], ACT.Exp)

            c.dve_done.passed(1)
            c.act_done.passed(3)

            def token_rows(name, x, dst):
                turned(c, name, lambda s, f: x[:, s, f * P:(f + 1) * P], lambda f: dst[:, f, :], TT, copied(c))

            token_rows("turn_values", v, v_tok)
            token_rows("turn_b", bT, b_tok)
            token_rows("turn_k", kT, k_tok)

        free = Carve(raw[:, 0:3 * RP * (SEQ + 1)])
        w2 = Carve(flat)
        w2.at = 4 * RP * SEQ + TT * RH * P
        rwkv_inverse(c, ar, bT, inverse, free, w2)
        free = Carve(raw[:, 0:3 * RP * (SEQ + 1)])
        w2 = Carve(flat)
        w2.at = 4 * RP * SEQ + TT * RH * P
        o_tok = w2(TT, RW)
        rwkv_scan(c, ar, bT, kT, inverse, v_tok, b_tok, k_tok, into, outof, bd, o_tok, free, w2)

        square = w2(TT * RH, 64)
        gain = w2(2, RW)
        stat = sb("gn_stat", [P, 2, TT * RH])
        with nc.Block("rwkv_gate") as block:

            @block.sync
            def _(sp):
                sp.dma_start(gain[:, 0, :], over_partitions(A["rwkv_gn_g_2"].rearrange("a n -> (a n)"), RW)).then_inc(c.loaded.sem, 16)
                sp.dma_start(gain[:, 1, :], over_partitions(A["rwkv_gn_b_2"].rearrange("a n -> (a n)"), RW)).then_inc(c.loaded.sem, 16)
                sp.wait_ge(c.loaded.sem, c.loaded.at(2))

            @block.tensor
            def _(pe):
                for t in range(TT):
                    last = nc.tensor.matmul(c.banks[:, t, :], gate_in[:, t * P:(t + 1) * P], g2[:], start=True, stop=True)

        c.loaded.passed(2)

        def gated(dve):
            place = mix[:, :, D - RW:D]
            heads = lambda x: x.rearrange("p t (h d) -> p (t h) d", h=RH)
            c.dve(dve, nc.vector.tensor_tensor(o_tok, o_tok, spread(gain[:, 0, :], TT), ALU.mult))
            c.dve(dve, nc.vector.tensor_tensor(o_tok, o_tok, spread(gain[:, 1, :], TT), ALU.add))
            c.dve(dve, nc.vector.tensor_tensor(square, heads(v_tok), bonus[:].rearrange("p t h -> p (t h)").unsqueeze(2)
                                               .broadcast_to([P, TT * RH, 64]), ALU.mult))
            c.dve(dve, nc.vector.tensor_tensor(heads(o_tok), heads(o_tok), square, ALU.add))
            nc.vector.tensor_tensor(place, o_tok, c.banks[:, 0:TT, :], ALU.mult)

        head_norm(c, "rwkv_norm", o_tok.rearrange("p t (h d) -> p (t h) d", h=RH), square, stat[:], TT * RH, 64, GN_EPS,
                  True, gated)


def rwkv_inverse(c, ar, bT, inverse, free, work):
    nc = c.nc
    levels = [2 ** i for i in range(1, 7)]
    L = len(levels)
    upper_of = free(L + 1, P)
    lower1 = free(P)
    nt = free(2, 4, P)
    n1 = free(2, 4, P)
    ntm = free(2, 2, 4, P)
    X = free(2, 4, P)
    y = work(2, 4, P)
    rounds = TT
    with nc.Block("join_masks") as block:

        @block.gpsimd
        def _(pool):
            c.pool(pool, nc.gpsimd.memset(upper_of, 1.0))
            for i in range(L + 1):
                m = 2 ** i
                blocks = P // (2 * m)
                view = upper_of[:, i, :].rearrange("p (b h m) -> p b h m", b=blocks, h=2)
                c.pool(pool, nc.gpsimd.affine_select(out=view, in_=view, compare_op=ALU.is_ge, fill=0.0, base=0,
                                                     pattern=[[-2 * m, blocks], [0, 2], [0, m]], channel_multiplier=1))
                c.pool(pool, nc.gpsimd.affine_select(out=view, in_=view, compare_op=ALU.is_ge, fill=0.0, base=m - 1,
                                                     pattern=[[2 * m, blocks], [0, 2], [0, m]], channel_multiplier=-1))
                c.pool(pool, nc.gpsimd.affine_select(out=view, in_=view, compare_op=ALU.is_gt, fill=0.0, base=0,
                                                     pattern=[[0, blocks], [1, 2], [0, m]], channel_multiplier=0))

        @block.tensor
        def _(pe):
            pe.wait_ge(c.pool.sem, c.pool.n)
            nc.tensor.transpose(c.banks[:, 0, 0:P], upper_of[:, 0, :], c.ident[:]).then_inc(c.products.sem, 1)

        @block.vector
        def _(dve):
            dve.wait_ge(c.products.sem, c.products.at(1))
            nc.vector.tensor_copy(lower1, c.banks[:, 0, 0:P])

    c.products.passed(1)

    n_ready, y_ready, x_ready = c.products, c.att_turned, c.att_out
    taken, nt_ready, y_copied, x_updated, joined = c.dve_done, c.att_masked, c.act_done, c.att_max, c.masks
    four = lambda x: x.unsqueeze(1).broadcast_to([P, 4, P])
    with nc.Block("rwkv_inverse") as block:

        @block.tensor
        def _(pe):
            for g in range(rounds):
                for q in range(2):
                    i = 2 * g + q
                    if i >= 1:
                        pe.wait_ge(taken.sem, taken.at(i))
                    for b in range(2):
                        for j in range(2):
                            rows, f = slice(64 * j, 64 * j + 64), 2 * q + b
                            A_, B_ = ar[rows, f, g, 0, :], bT[rows, f, g * P:(g + 1) * P]
                            nc.tensor.matmul(c.banks[:, 6 + j, b * P:(b + 1) * P], B_, A_, start=True, stop=True)
                            last = nc.tensor.matmul(c.banks[:, 6 + j, (2 + b) * P:(3 + b) * P], A_, B_, start=True, stop=True)
                    last.then_inc(n_ready.sem, 1)
                for l in range(L):
                    for q in range(2):
                        i = (g * L + l) * 2 + q
                        pe.wait_ge(joined.sem, joined.at(i + 1))
                        pe.wait_ge(x_updated.sem, x_updated.at((g * (L + 1) + l) * 2 + q + 1))
                        for h in range(4):
                            last = nc.tensor.matmul(c.banks[:, 3 * q, h * P:(h + 1) * P], ntm[:, l % 2, q, h, :], X[:, q, h, :],
                                                    start=True, stop=True)
                        last.then_inc(y_ready.sem, 1)
                    for q in range(2):
                        i = (g * L + l) * 2 + q
                        pe.wait_ge(y_copied.sem, y_copied.at(i + 1))
                        for h in range(4):
                            XT = inverse[:, g, 4 * q + h, :]
                            nc.tensor.matmul(c.banks[:, 3 * q + 1, h * P:(h + 1) * P], XT, y[:, q, h, :], start=True, stop=True)
                        for h in range(4):
                            XT = inverse[:, g, 4 * q + h, :]
                            last = nc.tensor.matmul(c.banks[:, 3 * q + 2, h * P:(h + 1) * P], y[:, q, h, :], XT,
                                                    start=True, stop=True)
                        last.then_inc(x_ready.sem, 1)

        @block.scalar
        def _(act):
            for i in range(rounds * L * 2):
                act.wait_ge(y_ready.sem, y_ready.at(i + 1))
                nc.scalar.activation(y[:, i % 2], c.banks[:, 3 * (i % 2), :].rearrange("p (h s) -> p h s", h=4),
                                     ACT.Copy).then_inc(y_copied.sem, 1)

        @block.gpsimd
        def _(pool):
            for g in range(rounds):
                for l in range(L):
                    for q in range(2):
                        i = (g * L + l) * 2 + q
                        pool.wait_ge(nt_ready.sem, nt_ready.at(2 * g + q + 1))
                        if i >= 4:
                            pool.wait_ge(y_ready.sem, y_ready.at(i - 3))
                        nc.gpsimd.tensor_tensor(ntm[:, l % 2, q], nt[:, q], four(upper_of[:, l + 1, :]), ALU.mult).then_inc(joined.sem, 1)

        @block.vector
        def _(dve):
            for g in range(rounds):
                for q in range(2):
                    i = 2 * g + q
                    XT = inverse[:, g, 4 * q:4 * q + 4, :]
                    dve.wait_ge(n_ready.sem, n_ready.at(i + 1))
                    if g >= 1:
                        dve.wait_ge(joined.sem, joined.at(((g - 1) * L + L - 1) * 2 + q + 1))
                    for b in range(2):
                        nc.vector.tensor_tensor(n1[:, q, 2 * b:2 * b + 2, :], c.banks[:, 6:8, (2 + b) * P:(3 + b) * P],
                                                lower1.unsqueeze(1).broadcast_to([P, 2, P]), ALU.mult)
                        last = nc.vector.tensor_tensor(nt[:, q, 2 * b:2 * b + 2, :], c.banks[:, 6:8, b * P:(b + 1) * P],
                                                       c.upper_strict[:].unsqueeze(1).broadcast_to([P, 2, P]), ALU.mult)
                    last.then_inc(nt_ready.sem, 1)
                    dve.wait_ge(nt_ready.sem, nt_ready.at(i + 1))
                    nc.vector.tensor_tensor(X[:, q], n1[:, q], four(c.ident[:]), ALU.add).then_inc(taken.sem, 1)
                    c.dve(dve, nc.vector.tensor_tensor(XT, nt[:, q], four(upper_of[:, 0, :]), ALU.mult))
                    nc.vector.tensor_tensor(XT, XT, four(c.ident[:]), ALU.add).then_inc(x_updated.sem, 1)
                for l in range(L):
                    for q in range(2):
                        i = (g * L + l) * 2 + q
                        XT = inverse[:, g, 4 * q:4 * q + 4, :]
                        bank = lambda b: c.banks[:, b, :].rearrange("p (h s) -> p h s", h=4)
                        dve.wait_ge(x_ready.sem, x_ready.at(i + 1))
                        nc.vector.tensor_tensor(X[:, q], X[:, q], bank(3 * q + 1), ALU.add)
                        nc.vector.tensor_tensor(XT, XT, bank(3 * q + 2), ALU.add).then_inc(x_updated.sem, 1)

    n_ready.passed(2 * rounds)
    taken.passed(2 * rounds)
    nt_ready.passed(2 * rounds)
    x_updated.passed(2 * rounds * (L + 1))
    for signal in (y_ready, x_ready, y_copied, joined):
        signal.passed(2 * rounds * L)


def rwkv_scan(c, ar, bT, kT, inverse, v_tok, b_tok, k_tok, into, outof, bd, o_tok, free, work):
    nc = c.nc
    mats = free(2, 3, 2, RP * P)
    rhs = work(RW)
    u = work(RW)
    state = work(2, RP, P)
    mats_ready, masked, rhs_ready, act_done = c.products, c.att_masked, c.att_turned, c.act_done
    u_ready, u_copied, carried, s_ready, o_ready = c.att_out, c.dve_done, c.att_max, c.masks, c.extra
    with nc.Block("rwkv_scan") as block:

        @block.gpsimd
        def _(pool):
            nc.gpsimd.memset(state[:, 0], 0.0).then_inc(c.pool_ready.sem, 1)

        @block.tensor
        def _(pe):
            def products(t):
                s = slice(t * P, (t + 1) * P)
                if t >= 1:
                    pe.wait_ge(masked.sem, masked.at(t))
                for f in range(RP):
                    for j in range(2):
                        rows = slice(64 * j, 64 * j + 64)
                        both = ar[rows, f, t, :, :].rearrange("p k s -> p (k s)")
                        nc.tensor.matmul(c.banks[:, 2 * j + f // 2, (f % 2) * 2 * P:(f % 2 + 1) * 2 * P], kT[rows, f, s], both,
                                         start=True, stop=True)
                        last = nc.tensor.matmul(c.banks[:, 4 + j, f * P:(f + 1) * P], bT[rows, f, s], ar[rows, f, t, 1, :],
                                                start=True, stop=True)
                last.then_inc(mats_ready.sem, 1)

            products(0)
            for t in range(TT):
                heads = [(2 * f + j, f, j) for f in range(RP) for j in range(2)]
                mat = lambda kind, f, j: mats[:, t % 2, kind, j, f * P:(f + 1) * P]
                S = lambda f, j: state[:, t % 2, f, j * 64:(j + 1) * 64]
                pe.wait_ge(masked.sem, masked.at(t + 1))
                pe.wait_ge(carried.sem, carried.at(2 * t + 1))
                if t >= 1:
                    pe.wait_ge(act_done.sem, act_done.at(2 * t))
                for h, f, j in heads:
                    out = c.banks[:, 6, h * 64:(h + 1) * 64]
                    nc.tensor.matmul(out, ar[:, f, t, 0, :], S(f, j), start=True, stop=False)
                    last = nc.tensor.matmul(out, mat(0, f, j), v_tok[:, t, h * 64:(h + 1) * 64], start=False, stop=True)
                last.then_inc(rhs_ready.sem, 1)
                if t + 1 < TT:
                    products(t + 1)
                pe.wait_ge(act_done.sem, act_done.at(2 * t + 1))
                if t >= 1:
                    pe.wait_ge(carried.sem, carried.at(2 * t))
                for h, f, j in heads:
                    last = nc.tensor.matmul(c.banks[:, 7, h * 64:(h + 1) * 64], inverse[:, t, h, :], rhs[:, h * 64:(h + 1) * 64],
                                            start=True, stop=True)
                last.then_inc(u_ready.sem, 1)
                pe.wait_ge(u_copied.sem, u_copied.at(t + 1))
                for f in range(RP):
                    out, s = c.banks[:, 7, f * P:(f + 1) * P], slice(f * P, (f + 1) * P)
                    nc.tensor.matmul(out, b_tok[:, t, s], u[:, s], start=True, stop=False)
                    last = nc.tensor.matmul(out, k_tok[:, t, s], v_tok[:, t, s], start=False, stop=True)
                last.then_inc(s_ready.sem, 1)
                for h, f, j in heads:
                    out = c.banks[:, 6, h * 64:(h + 1) * 64]
                    nc.tensor.matmul(out, ar[:, f, t, 1, :], S(f, j), start=True, stop=False)
                    nc.tensor.matmul(out, mat(1, f, j), v_tok[:, t, h * 64:(h + 1) * 64], start=False, stop=False)
                    last = nc.tensor.matmul(out, mat(2, f, j), u[:, h * 64:(h + 1) * 64], start=False, stop=True)
                last.then_inc(o_ready.sem, 1)

        @block.scalar
        def _(act):
            for t in range(TT):
                act.wait_ge(rhs_ready.sem, rhs_ready.at(t + 1))
                nc.scalar.activation(rhs, c.banks[:, 6, :], ACT.Copy).then_inc(act_done.sem, 1)
                act.wait_ge(o_ready.sem, o_ready.at(t + 1))
                nc.scalar.activation(o_tok[:, t, :], c.banks[:, 6, :], ACT.Copy).then_inc(act_done.sem, 1)

        @block.vector
        def _(dve):
            def mask(t):
                dve.wait_ge(mats_ready.sem, mats_ready.at(t + 1))
                if t >= 2:
                    dve.wait_ge(o_ready.sem, o_ready.at(t - 1))
                for j in range(2):
                    four = lambda m: m[:].unsqueeze(1).broadcast_to([P, RP, P])
                    pairs = c.banks[:, 2 * j:2 * j + 2, :].rearrange("p b (i k s) -> p (b i) k s", i=2, k=2)
                    place = lambda kind: mats[:, t % 2, kind, j, :].rearrange("p (f s) -> p f s", f=RP)
                    nc.vector.tensor_tensor(place(0), pairs[:, :, 0, :], four(c.upper_strict), ALU.mult)
                    nc.vector.tensor_tensor(place(1), pairs[:, :, 1, :], four(c.upper), ALU.mult)
                    last = nc.vector.tensor_tensor(place(2), c.banks[:, 4 + j, :].rearrange("p (f s) -> p f s", f=RP),
                                                   four(c.upper), ALU.mult)
                last.then_inc(masked.sem, 1)

            along = lambda x, t: x[:, :, t:t + 1].broadcast_to([P, RP, P])
            dve.wait_ge(c.pool_ready.sem, c.pool_ready.at(1))
            mask(0)
            for t in range(TT):
                cur, nxt = state[:, t % 2], state[:, (t + 1) % 2]
                nc.vector.tensor_tensor(cur, cur, along(into, t), ALU.mult).then_inc(carried.sem, 1)
                if t + 1 < TT:
                    mask(t + 1)
                dve.wait_ge(u_ready.sem, u_ready.at(t + 1))
                if t >= 1:
                    dve.wait_ge(o_ready.sem, o_ready.at(t))
                nc.vector.tensor_copy(u, c.banks[:, 7, :]).then_inc(u_copied.sem, 1)
                dve.wait_ge(s_ready.sem, s_ready.at(t + 1))
                c.dve(dve, nc.vector.tensor_tensor(nxt, c.banks[:, 7, :].rearrange("p (f s) -> p f s", f=RP),
                                                   bd[:].unsqueeze(1).broadcast_to([P, RP, P]), ALU.mult))
                c.dve(dve, nc.vector.tensor_tensor(nxt, nxt, cur, ALU.add))
                nc.vector.tensor_tensor(nxt, nxt, along(outof, t), ALU.mult).then_inc(carried.sem, 1)
                dve.wait_ge(carried.sem, carried.at(2 * t + 2))

    c.pool_ready.passed(1)
    act_done.passed(2 * TT)
    carried.passed(2 * TT)
    for signal in (mats_ready, masked, rhs_ready, u_ready, u_copied, s_ready, o_ready):
        signal.passed(TT)


def mixed(c, A, h, part, ctx, gates, slots, plan):
    nc = c.nc

    def sb(name, shape, dt=F32):
        return ctx.enter_context(nc.sbuf_tensor(name, shape, dt))

    h_rows = nc.dram_tensor("h_rows", [SEQ, D], F32).ap()
    slot_tok = nc.dram_tensor("slot_tokens", [SLOTS + CAP, 1], I32).ap()
    vec = sb("mix_vectors", [P, 5, D])
    hT = sb("hT2", [P, DT, SEQ])
    with nc.Block("load_gate_1") as block:
        @block.sync
        def _(sp):
            sp.dma_start(vec[:, 4, :], over_partitions(part(2), D)).then_inc(c.loaded.sem, 16)
            sp.wait_ge(c.loaded.sem, c.loaded.at(1))
    c.loaded.passed(1)
    out_projection(c, "project_mix", A["w_o_2"].rearrange("a k n -> (a k) n"), h, hT, lambda t, n, b:
                   nc.vector.scalar_tensor_tensor(out=h[:, t, n * 512:(n + 1) * 512], in0=vec[:, 4, n * 512:(n + 1) * 512],
                                                  scalar=1.0, in1=b, op0=ALU.add, op1=ALU.mult))

    def residual(dve):
        for t in range(TT):
            last = nc.vector.scalar_tensor_tensor(out=h[:, t, :], in0=c.x[:, t, :], scalar=ALPHA, in1=h[:, t, :],
                                                  op0=ALU.mult, op1=ALU.add)
        c.dve(dve, last)

    def modulated(dve, t):
        c.dve(dve, nc.vector.scalar_tensor_tensor(out=h[:, t, :], in0=vec[:, 2, :], scalar=1.0, in1=c.x[:, t, :],
                                                  op0=ALU.add, op1=ALU.mult))
        nc.vector.tensor_tensor(h[:, t, :], h[:, t, :], vec[:, 3, :], ALU.add)

    layer_norm(c, "norm_1", lambda t: h[:, t, :], lambda t: c.x[:, t, :],
               [(vec[:, 0, :], A["ln1_g_2"].rearrange("a n -> (a n)")), (vec[:, 1, :], A["ln1_b_2"].rearrange("a n -> (a n)")),
                (vec[:, 2, :], part(4)), (vec[:, 3, :], part(3))], modulated, residual)
    turned(c, "turn_h2", lambda t, f: h[:, t, f * P:(f + 1) * P], lambda f: hT[:, f, :], DT, copied(c))

    rw = sb("router_w", [P, DT, E])
    rb = sb("router_b", [P, E])
    logits = sb("logits", [P, TT, E])
    top = sb("top_values", [P, TT, 8])
    top_i = sb("top_indices", [P, TT, 8], U32)
    top_f = sb("top_index_f", [P, TT, 8])
    neg = sb("neg_top", [P, TT])
    total = sb("gate_total", [P, TT])
    e_int = sb("expert_ids_i", [P, E], I32)
    e_id = sb("expert_ids", [P, E])
    hot = sb("one_hot", [P, TT, TOPK, E])
    member = sb("member", [P, TT, E])
    rank = sb("rank", [P, TT, E])
    count = sb("expert_count", [P, E])
    extra = sb("extra_blocks", [P, 2, E])
    cum = sb("extra_cum", [P, E])
    first = sb("extra_first", [P, E])
    over = sb("over_capacity", [P, TT, E])
    dest = sb("dest", [P, TT, TOPK])
    token_id = sb("token_id", [P, TT], I32)
    blk_i = sb("block_ids_i", [1, EXTRA], I32)
    blk = sb("block_ids", [1, EXTRA])
    before_blk = sb("experts_before", [1, EXTRA, E])
    plan_f = sb("plan_f", [1, 1 + EXTRA])
    zeros = sb("zero_ids", [SLOTS // CAP + 1, CAP], I32)
    with nc.Block("router") as block:

        @block.sync
        def _(sp):
            sp.dma_start(rw[:], A["router_w_2"].rearrange("a (k p) e -> p (a k) e", p=P)).then_inc(c.loaded.sem, 16)
            sp.dma_start(rb[:], over_partitions(A["router_b_2"].rearrange("a n -> (a n)"), E)).then_inc(c.loaded.sem, 16)
            sp.dma_start(h_rows.rearrange("(t p) d -> p t d", p=P), h[:]).then_inc(c.stored.sem, 16)
            sp.wait_ge(c.pool_ready.sem, c.pool_ready.at(1))
            sp.dma_start(slot_tok.rearrange("(b s) o -> b (s o)", s=CAP), zeros[:]).then_inc(c.stored.sem, 16)
            sp.wait_ge(c.stored.sem, c.stored.at(2))

        @block.gpsimd
        def _(pool):
            nc.gpsimd.memset(zeros[:], 0)
            nc.gpsimd.iota(token_id[:], pattern=[[P, TT]], base=0, channel_multiplier=1)
            nc.gpsimd.iota(blk_i[:], pattern=[[1, EXTRA]], base=0, channel_multiplier=0)
            nc.gpsimd.iota(e_int[:], pattern=[[1, E]], base=0, channel_multiplier=0).then_inc(c.pool_ready.sem, 1)

        @block.tensor
        def _(pe):
            pe.wait_ge(c.loaded.sem, c.loaded.at(2))
            for t in range(TT):
                for k in range(DT):
                    last = nc.tensor.matmul(c.banks[:, 0, t * E:(t + 1) * E], hT[:, k, t * P:(t + 1) * P], rw[:, k, :],
                                            start=(k == 0), stop=(k == DT - 1))
            last.then_inc(c.products.sem, 1)
            pe.wait_ge(c.dve_done.sem, c.dve_done.at(2))
            for t in range(TT):
                out = c.banks[:, 1, t * E:(t + 1) * E]
                for b in range(t):
                    nc.tensor.matmul(out, c.ones[:], member[:, b, :], start=(b == 0), stop=False)
                nc.tensor.matmul(out, c.upper_strict[:], member[:, t, :], start=(t == 0), stop=True)
            for b in range(TT):
                last = nc.tensor.matmul(c.banks[:, 1, TT * E:(TT + 1) * E], c.ones[:], member[:, b, :], start=(b == 0),
                                        stop=(b == TT - 1))
            last.then_inc(c.products.sem, 1)

        @block.scalar
        def _(act):
            act.wait_ge(c.dve_done.sem, c.dve_done.at(1))
            for t in range(TT):
                last = nc.scalar.activation(gates[:, t, :], top[:, t, 0:TOPK], ACT.Exp, bias=neg[:, t:t + 1],
                                            accum_out=total[:, t:t + 1])
            last.then_inc(c.act_done.sem, 1)

        @block.vector
        def _(dve):
            dve.wait_ge(c.loaded.sem, c.loaded.at(2))
            dve.wait_ge(c.pool_ready.sem, c.pool_ready.at(1))
            nc.vector.tensor_copy(blk[:], blk_i[:])
            nc.vector.tensor_copy(e_id[:], e_int[:])
            dve.wait_ge(c.products.sem, c.products.at(1))
            c.dve(dve, nc.vector.tensor_tensor(logits[:], c.banks[:, 0, 0:TT * E].rearrange("p (t e) -> p t e", t=TT),
                                               spread(rb[:], TT), ALU.add))
            for t in range(TT):
                last = nc.vector.max(top[:, t, :], logits[:, t, :])
            c.dve(dve, last)
            nc.vector.tensor_scalar(neg[:], top[:, :, 0], -1.0, None, ALU.mult).then_inc(c.dve_done.sem, 1)
            for t in range(TT):
                last = nc.vector.max_index(top_i[:, t, :], top[:, t, :], logits[:, t, :])
            c.dve(dve, last)
            c.dve(dve, nc.vector.tensor_copy(top_f[:], top_i[:]))
            for t in range(TT):
                for k in range(TOPK):
                    last = nc.vector.tensor_scalar(hot[:, t, k, :], e_id[:], top_f[:, t, k:k + 1], None, ALU.is_equal)
            c.dve(dve, last)
            nc.vector.tensor_reduce(member[:], hot[:].rearrange("p t k e -> p t e k"), AX.X, ALU.add).then_inc(c.dve_done.sem, 1)
            dve.wait_ge(c.act_done.sem, c.act_done.at(1))
            c.dve(dve, nc.vector.reciprocal(total[:], total[:]))
            nc.vector.tensor_tensor(gates[:], gates[:], total[:].unsqueeze(2).broadcast_to([P, TT, TOPK]), ALU.mult)
            dve.wait_ge(c.products.sem, c.products.at(2))
            nc.vector.tensor_copy(rank[:], c.banks[:, 1, 0:TT * E].rearrange("p (t e) -> p t e", t=TT))
            c.dve(dve, nc.vector.tensor_copy(count[:], c.banks[:, 1, TT * E:(TT + 1) * E]))
            c.dve(dve, nc.vector.tensor_scalar(extra[:, 0, :], count[:], float(CAP), None, ALU.is_gt))
            for m in range(2, SEQ // CAP):
                c.dve(dve, nc.vector.tensor_scalar(extra[:, 1, :], count[:], float(m * CAP), None, ALU.is_gt))
                c.dve(dve, nc.vector.tensor_tensor(extra[:, 0, :], extra[:, 0, :], extra[:, 1, :], ALU.add))
            c.dve(dve, nc.vector.tensor_tensor_scan(cum[:], c.ones[:, 0:E], extra[:, 0, :], 0.0, ALU.mult, ALU.add))
            c.dve(dve, nc.vector.tensor_tensor(first[:], cum[:], extra[:, 0, :], ALU.subtract))
            c.dve(dve, nc.vector.scalar_tensor_tensor(out=first[:], in0=first[:], scalar=float(E - 1), in1=e_id[:],
                                                      op0=ALU.add, op1=ALU.subtract))
            c.dve(dve, nc.vector.tensor_scalar(over[:], rank[:], float(CAP), None, ALU.is_ge))
            c.dve(dve, nc.vector.tensor_tensor(over[:], over[:], spread(first[:], TT), ALU.mult))
            c.dve(dve, nc.vector.tensor_tensor(over[:], over[:], spread(e_id[:], TT), ALU.add))
            c.dve(dve, nc.vector.scalar_tensor_tensor(out=rank[:], in0=over[:], scalar=float(CAP), in1=rank[:],
                                                      op0=ALU.mult, op1=ALU.add))
            for k in range(TOPK):
                last = nc.vector.tensor_tensor(hot[:, :, k, :], hot[:, :, k, :], rank[:], ALU.mult)
            c.dve(dve, last)
            c.dve(dve, nc.vector.tensor_reduce(dest[:], hot[:], AX.X, ALU.add))
            nc.vector.tensor_copy(slots[:], dest[:])
            for b in range(EXTRA):
                last = nc.vector.tensor_scalar(before_blk[:, b, :], cum[0:1, :], blk[:, b:b + 1], None, ALU.is_le)
            c.dve(dve, last)
            nc.vector.tensor_copy(plan_f[:, 0:1], cum[0:1, E - 1:E])
            c.dve(dve, nc.vector.tensor_reduce(plan_f[:, 1:1 + EXTRA], before_blk[:], AX.X, ALU.add))
            c.dve(dve, nc.vector.tensor_scalar(plan_f[:, 1:1 + EXTRA], plan_f[:, 1:1 + EXTRA], float(E - 1), None, ALU.min))
            nc.vector.tensor_copy(plan[:], plan_f[:])

    c.loaded.passed(2)
    c.stored.passed(2)
    c.pool_ready.passed(1)
    c.products.passed(2)
    c.dve_done.passed(2)
    c.act_done.passed(1)
    with nc.Block("fill_slots") as block:

        @block.gpsimd
        def _(pool):
            for t in range(TT):
                for k in range(TOPK):
                    nc.gpsimd.indirect_dma_start(slot_tok, bass.IndirectOffsetOnAxis(slots[:, t, k:k + 1], 0),
                                                 token_id[:, t:t + 1], None).then_inc(c.gathered.sem, 16)
                    pool.wait_ge(c.gathered.sem, c.gathered.at(t * TOPK + k + 1))

    c.gathered.passed(TT * TOPK)
    return h_rows, slot_tok


def experts(c, A, h_rows, slot_tok, plan, Y):
    nc = c.nc
    HALF = FF // 2
    w1 = A["exp_w1_2"].rearrange("a e (k p) n -> (a e) p k n", p=P)
    w2 = A["exp_w2_2"].rearrange("a e (k p) n -> (a e) p k n", p=P)
    bias_rows = nc.dram_tensor("bias_parts", [E, 3, 3 * FF], BF16).ap()
    with ExitStack() as ctx:
        def sb(name, shape, dt=F32):
            return ctx.enter_context(nc.sbuf_tensor(name, shape, dt))

        with ExitStack() as inner:
            b = inner.enter_context(nc.sbuf_tensor("expert_b", [E, 3 * FF], F32))
            parts = inner.enter_context(nc.sbuf_tensor("expert_b_parts", [E, 3, 3 * FF], BF16))
            with nc.Block("split_biases") as block:

                @block.sync
                def _(sp):
                    sp.dma_start(b[:, 0:2 * FF], A["exp_b1_2"].rearrange("a e n -> (a e) n")).then_inc(c.loaded.sem, 16)
                    sp.dma_start(b[:, 2 * FF:3 * FF], A["exp_b2_2"].rearrange("a e n -> (a e) n")).then_inc(c.loaded.sem, 16)
                    sp.wait_ge(c.dve_done.sem, c.dve_done.at(1))
                    sp.dma_start(bias_rows, parts[:]).then_inc(c.stored.sem, 16)
                    sp.wait_ge(c.stored.sem, c.stored.at(1))

                @block.vector
                def _(dve):
                    dve.wait_ge(c.loaded.sem, c.loaded.at(2))
                    for i in range(3):
                        last = nc.vector.tensor_copy(parts[:, i, :], b[:])
                        if i < 2:
                            c.dve(dve, last)
                            c.dve(dve, nc.vector.tensor_tensor(b[:], b[:], parts[:, i, :], ALU.subtract))
                    last.then_inc(c.dve_done.sem, 1)

            c.loaded.passed(2)
            c.stored.passed(1)
            c.dve_done.passed(1)

        ids = sb("block_tokens", [P, 1], I32)
        xg = sb("block_rows", [P, D])
        xT = sb("block_rows_T", [P, DT, P])
        brow = sb("bias_row", [3, 3 * FF], BF16)
        ones = sb("ones_bf", [3, P], BF16)
        glu = sb("glu", [P, 2, HALF])
        lin = sb("lin", [P, 2, HALF])
        sig = sb("sig", [P, 2, HALF])
        u = sb("u", [P, 2, HALF])
        uT = sb("uT", [P, DT, P])
        ysb = sb("y_rows", [P, D])
        own = lambda name, step=1: Signal(nc, name, step)
        used, bias_used, bias_in = own("chunks_used"), own("bias_used"), own("bias_in", 16)
        turned_x, turned_u, x_copied, u_copied = own("rows_turned"), own("u_turned"), own("rows_copied"), own("u_copied")
        glu_ready, step, sig_ready, u_ready = own("glu_ready"), own("swiglu_step"), own("sigmoid_ready"), own("u_ready")
        y_left, y_right, rows_in, ids_in, stored = (own("y_left_copied"), own("y_right_copied"), own("rows_in", 16),
                                                    own("ids_in", 16), own("y_stored", 16))
        fetches = own("block_fetches")
        per = 12
        out_rows = Y.rearrange("(b s) n -> b s n", s=CAP)
        slot_ids = slot_tok.rearrange("(b s) o -> b s o", s=CAP)

        def every_block(engine, body):
            with engine.Fori(0, E) as i:
                body(i, i)
            n = engine.value_load(plan[0:1, 0:1], min_val=0, max_val=EXTRA)
            with engine.If(n > 0):
                with engine.Fori(0, n) as j:
                    body(engine.snap(j + E), j)

        with nc.Block("experts") as block:

            @block.sync
            def _(sp):
                def weights(i, e, wait):
                    for ch in range(per):
                        if wait:
                            sp.wait_ge(used.sem, used.base + 1 + ch + (i - 1) * per)
                        if ch < 8:
                            half, k = ch // 4, 2 * (ch % 4)
                            src = w1[bass.ds(e, 1), :, k:k + 2, half * FF:(half + 1) * FF]
                        else:
                            k = 2 * (ch - 8)
                            src = w2[bass.ds(e, 1), :, k:k + 2, :]
                        sp.dma_start(c.ring[:, ch, :].rearrange("p (k n) -> p k n", k=2),
                                     src.rearrange("o p k n -> p (o k) n")).then_inc(c.landed[ch].sem, 16)
                    if wait:
                        sp.wait_ge(bias_used.sem, bias_used.base + i)
                    sp.dma_start(brow[:], bias_rows[bass.ds(e, 1), :, :].rearrange("o a n -> (o a) n")).then_inc(bias_in.sem, 16)

                weights(0, 0, False)
                with sp.Fori(1, E) as i:
                    weights(i, i, True)
                n = sp.value_load(plan[0:1, 0:1], min_val=0, max_val=EXTRA)
                with sp.If(n > 0):
                    with sp.Fori(0, n) as j:
                        e = sp.value_load(plan[0:1, bass.ds(j + 1, 1)], min_val=0, max_val=E - 1)
                        weights(sp.snap(j + E), e, True)

            @block.gpsimd
            def _(pool):
                nc.gpsimd.memset(ones[:], 1.0).then_inc(c.pool_ready.sem, 1)

                def fetch(i):
                    pool.dma_start(ids[:], slot_ids[bass.ds(i, 1), :, :].rearrange("b s o -> (b s) o"),
                                   allow_slow_non_contiguous=True).then_inc(ids_in.sem, 16)
                    pool.wait_ge(ids_in.sem, ids_in.base + 16 + i * 16)
                    pool.sem_inc(fetches.sem, 1)
                    nc.gpsimd.indirect_dma_start(xg[:], None, h_rows, bass.IndirectOffsetOnAxis(ids[:], 0)).then_inc(rows_in.sem, 16)
                    pool.wait_ge(rows_in.sem, rows_in.base + 16 + i * 16)

                fetch(0)

                def body(i, _):
                    pool.wait_ge(turned_x.sem, turned_x.base + 2 + i * 2)
                    fetch(i + 1)

                every_block(pool, body)
                n = pool.value_load(plan[0:1, 0:1], min_val=0, max_val=EXTRA)
                pool.wait_ge(stored.sem, stored.base + 16 * E + n * 16)

            @block.tensor
            def _(pe):
                def turn_x(i, half):
                    for k in range(4):
                        last = nc.tensor.transpose(c.banks[:, 5 - half, k * P:(k + 1) * P],
                                                   xg[:, (4 * half + k) * P:(4 * half + k + 1) * P], c.ident[:])
                    last.then_inc(turned_x.sem, 1)

                pe.wait_ge(c.pool_ready.sem, c.pool_ready.at(1))
                pe.wait_ge(rows_in.sem, rows_in.at(1))
                turn_x(0, 0)
                turn_x(0, 1)

                def body(i, _):
                    pe.wait_ge(x_copied.sem, x_copied.base + 2 + i * 2)
                    pe.wait_ge(bias_in.sem, bias_in.base + 16 + i * 16)
                    pe.wait_ge(step.sem, step.base + i * 4)
                    for half in range(2):
                        for n in range(2):
                            nc.tensor.matmul(c.banks[:, 2 * half + n, :], ones[:],
                                             brow[:, half * FF + n * 512:half * FF + (n + 1) * 512], start=True, stop=False)
                        for ch in range(4 * half, 4 * half + 4):
                            pe.wait_ge(c.landed[ch].sem, c.landed[ch].base + 16 + i * 16)
                            for kk in range(2):
                                k = 2 * (ch % 4) + kk
                                for n in range(2):
                                    last = nc.tensor.matmul(c.banks[:, 2 * half + n, :], xT[:, k, :],
                                                            c.ring[:, ch, kk * FF + n * 512:kk * FF + (n + 1) * 512],
                                                            start=False, stop=(k == DT - 1))
                            last.then_inc(used.sem, 1)
                    pe.wait_ge(u_ready.sem, u_ready.base + 1 + i * 2)
                    for k in range(4):
                        last = nc.tensor.transpose(c.banks[:, 4, k * P:(k + 1) * P], u[:, 0, k * P:(k + 1) * P], c.ident[:])
                    last.then_inc(turned_u.sem, 1)
                    pe.wait_ge(rows_in.sem, rows_in.base + 32 + i * 16)
                    turn_x(i, 0)
                    pe.wait_ge(y_left.sem, y_left.base + i)
                    pe.wait_ge(y_right.sem, y_right.base + i)
                    pe.wait_ge(u_copied.sem, u_copied.base + 1 + i * 2)
                    for n in range(2):
                        last = nc.tensor.matmul(c.banks[:, 6 + n, :], ones[:], brow[:, 2 * FF + n * 512:2 * FF + (n + 1) * 512],
                                                start=True, stop=False)
                    last.then_inc(bias_used.sem, 1)
                    for half in range(2):
                        if half:
                            turn_x(i, 1)
                            pe.wait_ge(u_ready.sem, u_ready.base + 2 + i * 2)
                            pe.wait_ge(x_copied.sem, x_copied.base + 3 + i * 2)
                            for k in range(4):
                                last = nc.tensor.transpose(c.banks[:, 5, k * P:(k + 1) * P], u[:, 1, k * P:(k + 1) * P], c.ident[:])
                            last.then_inc(turned_u.sem, 1)
                            pe.wait_ge(u_copied.sem, u_copied.base + 2 + i * 2)
                        for ch in range(8 + 2 * half, 10 + 2 * half):
                            pe.wait_ge(c.landed[ch].sem, c.landed[ch].base + 16 + i * 16)
                            for kk in range(2):
                                k = 2 * (ch - 8) + kk
                                for n in range(2):
                                    last = nc.tensor.matmul(c.banks[:, 6 + n, :], uT[:, k, :],
                                                            c.ring[:, ch, kk * FF + n * 512:kk * FF + (n + 1) * 512],
                                                            start=False, stop=(k == DT - 1))
                            last.then_inc(used.sem, 1)

                every_block(pe, body)

            @block.vector
            def _(dve):
                def body(i, _):
                    for half in range(2):
                        dve.wait_ge(used.sem, used.base + 4 * (half + 1) + i * per)
                        pair = c.banks[:, 2 * half:2 * half + 2, :].rearrange("p b (n two) -> p (b n) two", two=2)
                        nc.vector.tensor_scalar(glu[:, half, :], pair[:, :, 0], LIMIT, None, ALU.min).then_inc(glu_ready.sem, 1)
                        nc.vector.tensor_scalar(lin[:, half, :], pair[:, :, 1], LIMIT, -LIMIT, ALU.min,
                                                ALU.max).then_inc(step.sem, 1)
                        dve.wait_ge(glu_ready.sem, glu_ready.base + 1 + half + i * 2)
                        dve.wait_ge(step.sem, step.base + 1 + 2 * half + i * 4)
                        nc.vector.scalar_tensor_tensor(out=lin[:, half, :], in0=lin[:, half, :], scalar=1.0,
                                                       in1=glu[:, half, :], op0=ALU.add, op1=ALU.mult).then_inc(step.sem, 1)
                        dve.wait_ge(step.sem, step.base + 2 + 2 * half + i * 4)
                        dve.wait_ge(sig_ready.sem, sig_ready.base + 1 + half + i * 2)
                        nc.vector.tensor_tensor(u[:, half, :], lin[:, half, :], sig[:, half, :], ALU.mult).then_inc(u_ready.sem, 1)
                    dve.wait_ge(used.sem, used.base + per + i * per)
                    dve.wait_ge(stored.sem, stored.base + i * 16)
                    nc.vector.tensor_copy(ysb[:, 0:512], c.banks[:, 6, :]).then_inc(y_left.sem, 1)

                every_block(dve, body)

            @block.scalar
            def _(act):
                def copy_x(i, half):
                    act.wait_ge(turned_x.sem, turned_x.base + 1 + half + i * 2)
                    nc.scalar.activation(xT[:, 4 * half:4 * half + 4, :],
                                         c.banks[:, 5 - half, :].rearrange("p (k s) -> p k s", k=4), ACT.Copy).then_inc(x_copied.sem, 1)

                def copy_u(i, half):
                    act.wait_ge(turned_u.sem, turned_u.base + 1 + half + i * 2)
                    nc.scalar.activation(uT[:, 4 * half:4 * half + 4, :],
                                         c.banks[:, 4 + half, :].rearrange("p (k s) -> p k s", k=4), ACT.Copy).then_inc(u_copied.sem, 1)

                copy_x(0, 0)
                copy_x(0, 1)

                def body(i, _):
                    for half in range(2):
                        act.wait_ge(glu_ready.sem, glu_ready.base + 1 + half + i * 2)
                        nc.scalar.activation(sig[:, half, :], glu[:, half, :], ACT.Sigmoid, scale=SW_ALPHA).then_inc(sig_ready.sem, 1)
                    copy_u(i, 0)
                    copy_x(i + 1, 0)
                    copy_x(i + 1, 1)
                    copy_u(i, 1)
                    act.wait_ge(used.sem, used.base + per + i * per)
                    act.wait_ge(stored.sem, stored.base + i * 16)
                    nc.scalar.activation(ysb[:, 512:D], c.banks[:, 7, :], ACT.Copy).then_inc(y_right.sem, 1)
                    act.wait_ge(y_left.sem, y_left.base + 1 + i)
                    act.wait_ge(y_right.sem, y_right.base + 1 + i)
                    act.dma_start(out_rows[bass.ds(i, 1), :, :].rearrange("b s n -> (b s) n"), ysb[:]).then_inc(stored.sem, 16)

                every_block(act, body)


def combine(c, A, h, Y, gates, slots, part, out):
    nc = c.nc
    flat = c.ring[:].rearrange("p a b -> p (a b)")
    rows = Carve(flat)(TT, TOPK, D)
    came = [Signal(nc, f"rows_of_tile_{t}", 16) for t in range(TT)]
    with nc.sbuf_tensor("final_vectors", [P, 3, D], F32) as vec:
        with nc.Block("combine") as block:

            @block.sync
            def _(sp):
                sp.dma_start(vec[:, 2, :], over_partitions(part(5), D)).then_inc(c.final_loaded.sem, 16)
                sp.wait_ge(c.final_loaded.sem, 16)

            @block.gpsimd
            def _(pool):
                for t in range(TT):
                    for k in range(TOPK):
                        nc.gpsimd.indirect_dma_start(rows[:, t, k, :], None, Y,
                                                     bass.IndirectOffsetOnAxis(slots[:, t, k:k + 1], 0)).then_inc(came[t].sem, 16)

            @block.vector
            def _(dve):
                dve.wait_ge(c.final_loaded.sem, 16)
                for t in range(TT):
                    dve.wait_ge(came[t].sem, 16 * TOPK)
                    acc = h[:, t, :]
                    c.dve(dve, nc.vector.tensor_scalar(acc, rows[:, t, 0, :], gates[:, t, 0:1], None, ALU.mult))
                    for k in range(1, TOPK):
                        c.dve(dve, nc.vector.scalar_tensor_tensor(out=acc, in0=rows[:, t, k, :], scalar=gates[:, t, k:k + 1],
                                                                  in1=acc, op0=ALU.mult, op1=ALU.add))
                    c.dve(dve, nc.vector.scalar_tensor_tensor(out=acc, in0=vec[:, 2, :], scalar=1.0, in1=acc,
                                                              op0=ALU.add, op1=ALU.mult))
                    nc.vector.scalar_tensor_tensor(out=acc, in0=c.x[:, t, :], scalar=ALPHA, in1=acc, op0=ALU.mult, op1=ALU.add)

        layer_norm(c, "norm_2", lambda t: h[:, t, :], lambda t: c.x[:, t, :],
                   [(vec[:, 0, :], A["ln2_g_2"].rearrange("a n -> (a n)")), (vec[:, 1, :], A["ln2_b_2"].rearrange("a n -> (a n)"))],
                   lambda dve, t: None)
    with nc.Block("store") as block:

        @block.sync
        def _(sp):
            sp.dma_start(out.rearrange("a (t p) d -> p (a t) d", p=P), c.x[:]).then_inc(c.final_stored.sem, 16)
            sp.wait_ge(c.final_stored.sem, 16)


def hybrid_then_moe(nc, A, out):
    with ExitStack() as ctx:
        c = Core(nc, ctx)
        Y = nc.dram_tensor("slot_outputs", [SLOTS, D], F32).ap()
        constants(c, A["x"], Y)
        first_block(c, A)
        second_block(c, A, Y, out)


_INS = ["x", "norm_g", "w_in", "b_gates", "conv_w", "w_alpha", "b_alpha", "ml_norm_g", "gla_norm_g", "w_out",
        "final_g", "c_2", "positions_2", "emb_ln_g_2", "emb_ln_b_2", "ada_w_2", "ada_b_2", "w_in_2", "q_norm_g_2",
        "w_uq_2", "kv_norm_g_2", "w_uk_2", "w_uv_2", "mla_out_g_2", "rwkv_mu_2", "rwkv_w0_2", "rwkv_w2_2",
        "rwkv_a0_2", "rwkv_a2_2", "rwkv_g2_2", "rwkv_k_k_2", "rwkv_k_a_2", "rwkv_r_k_2", "rwkv_gn_g_2",
        "rwkv_gn_b_2", "w_o_2", "ln1_g_2", "ln1_b_2", "router_w_2", "router_b_2", "exp_w1_2", "exp_b1_2",
        "exp_w2_2", "exp_b2_2", "ln2_g_2", "ln2_b_2"]


def kernel(**inputs):
    import concourse.bacc as bacc
    from concourse.bass_utils import run_bass_kernel_spmd

    arrays = {name: np.ascontiguousarray(inputs[name]) for name in _INS}
    distance = np.arange(P)[:, None] + (SEQ - P) - np.arange(SEQ)[None, :]
    table = np.asarray(inputs["rel_bias"])[0]
    arrays["rel_rows"] = np.ascontiguousarray(table[:, np.clip(distance, -REL, REL) + REL])
    arrays["inv_freq"] = (10000.0 ** (-np.arange(0, ROPE, 2, dtype=np.float32) / np.float32(ROPE))).astype(np.float32)

    nc = bacc.Bacc("TRN2", target_bir_lowering=False, num_devices=1)
    A = {name: nc.dram_tensor(f"in_{name}", a.shape, mybir.dt.from_np(a.dtype), kind="ExternalInput").ap()
         for name, a in arrays.items()}
    out = nc.dram_tensor("out", (1, SEQ, D), F32, kind="ExternalOutput").ap()
    hybrid_then_moe(nc, A, out)
    result = run_bass_kernel_spmd(nc, [{f"in_{name}": a for name, a in arrays.items()}], core_ids=[0])
    return result.results[0]["out"]
```

```python
from contextlib import ExitStack

import concourse.bass as bass
import concourse.mybir as mybir
import numpy as np

ALU = mybir.AluOpType
ACT = mybir.ActivationFunctionType
AX = mybir.AxisListType
F32 = mybir.dt.float32
BF16 = mybir.dt.bfloat16
F32R = mybir.dt.float32r
I32 = mybir.dt.int32
U32 = mybir.dt.uint32

P = 128
SEQ = 512
D = 1024
TT = SEQ // P
DT = D // P
NEG = -1e30

CHUNK = 64
HD = 64
AW = 384
AH = AW // HD
REL = 128
MW = 384
MH = MW // HD
CONV = 4
GW = 256
GH = 4
GDV = 64
GDK = 32
GKW = GH * GDK
RANK = 16
TAU = 16.0
RMS_EPS = 1e-6

QL, KVL, ROPE, NOPE, VD = 256, 128, 32, 64, 64
QK = NOPE + ROPE
NH = 8
MLA_IN = QL + KVL + ROPE
RW = 512
RH = 8
RP = RH // 2
LORA_D, LORA_A, LORA_G = 64, 64, 128
RWKV_IN = 3 * RW + LORA_D + LORA_A + LORA_G
GN_EPS = 64e-5
LN_EPS = 1e-5
ALPHA = 2.0 ** 0.25
E = 32
TOPK = 4
FF = 1024
LIMIT = 7.0
SW_ALPHA = 1.702
CAP = 128
EXTRA = SEQ * TOPK // CAP - 1
SLOTS = (E + EXTRA) * CAP

NBANK = 8
RING = 12
RSLOT = 2048
RAW = 6
SPLIT = 4


class Signal:

    def __init__(self, nc, name, step=1):
        self.sem = nc.alloc_semaphore(name=name)
        self.step = step
        self.base = 0

    def at(self, n):
        return self.base + n * self.step

    def passed(self, n):
        self.base += n * self.step


class Chain:

    def __init__(self, nc, name):
        self.sem = nc.alloc_semaphore(name=name)
        self.n = 0

    def __call__(self, engine, instruction):
        self.n += 1
        instruction.then_inc(self.sem, 1)
        engine.wait_ge(self.sem, self.n)


class Core:

    def __init__(self, nc, ctx):
        self.nc = nc
        self.ctx = ctx
        self.banks = ctx.enter_context(nc.psum_tensor("banks", [P, NBANK, 512], F32))
        self.far = ExitStack()
        self.x = ctx.enter_context(nc.sbuf_tensor("x_tokens", [P, TT, D], F32))
        self.ident = ctx.enter_context(nc.sbuf_tensor("ident", [P, P], F32))
        self.upper = ctx.enter_context(nc.sbuf_tensor("upper", [P, P], F32))
        self.upper_strict = ctx.enter_context(nc.sbuf_tensor("upper_strict", [P, P], F32))
        self.zeros = ctx.enter_context(nc.sbuf_tensor("zeros", [P, 256], F32))
        self.ones = ctx.enter_context(nc.sbuf_tensor("ones", [P, P], F32))
        self.zero_filled = Signal(nc, "zero_filled", 16)
        self.products = Signal(nc, "products_ready")
        self.high_parts = Signal(nc, "high_parts_made")
        self.low_parts = Signal(nc, "low_parts_made")
        self.act_done = Signal(nc, "act_evacuated")
        self.dve_done = Signal(nc, "dve_evacuated")
        self.landed = [Signal(nc, f"landed_{i}", 16) for i in range(RING)]
        self.loaded = Signal(nc, "small_loads", 16)
        self.stored = Signal(nc, "stored", 16)
        self.dve = Chain(nc, "dve_chain")
        self.act = Chain(nc, "act_chain")
        self.pool = Chain(nc, "pool_chain")
        self.masks = Signal(nc, "masks_ready")
        self.gathered = Signal(nc, "gathered", 16)
        self.final_loaded = Signal(nc, "final_loaded", 16)
        self.final_stored = Signal(nc, "final_stored", 16)
        self.extra = Signal(nc, "outputs_ready")
        self.pool_ready = Signal(nc, "pool_ready")
        self.att_turned = Signal(nc, "probs_transposed")
        self.att_copied = Signal(nc, "transposed_copied")
        self.att_out = Signal(nc, "attention_out_ready")
        self.att_masked = Signal(nc, "scores_masked")
        self.att_max = Signal(nc, "row_max_ready")


def column(ap, tiles):
    return ap.rearrange("(t p) -> p t", t=tiles)


def over_partitions(ap, n):
    return ap.rearrange("(a n) -> a n", a=1).broadcast_to([P, n])


def projection(c, name, loads, units, beside=None, split=None, under_way=0):
    nc = c.nc
    products, landed = c.products, c.landed
    done = {"act": c.act_done, "dve": c.dve_done}
    order = []
    count = {"act": 0, "dve": 0}
    for u in units:
        count[u["engine"]] += 1
        order.append((u["engine"], count[u["engine"]]))
    nbank = beside["banks"] if beside else NBANK
    last_of = {}
    for u, unit in enumerate(units):
        last_of[unit["load"]] = u
    passes = ((0, 1), (0, 0), (1, 0)) if split else (None,)

    def other(engine, who, at):
        for place, piece in (beside[who] if beside else ()):
            if place == at:
                piece(engine)

    with nc.Block(name) as block:

        @block.sync
        def _(sp):
            for g, (dst, src, free_after) in enumerate(loads):
                other(sp, "sync", g)
                if g < under_way:
                    continue
                if split and g >= split["raws"]:
                    sp.wait_ge(c.low_parts.sem, c.low_parts.at(g - split["raws"] + 1))
                if free_after is not None:
                    sp.wait_ge(products.sem, products.at(free_after + 1))
                sp.dma_start(dst, src).then_inc(landed[g % RING].sem, 16)
            other(sp, "sync", len(loads))

        if beside:
            block.gpsimd(beside["gpsimd"])

        @block.tensor
        def _(pe):
            seen = -1
            for u, unit in enumerate(units):
                other(pe, "tensor", u)
                if unit["load"] > seen:
                    seen = unit["load"]
                    if split:
                        pe.wait_ge(c.low_parts.sem, c.low_parts.at(seen + 1))
                    else:
                        pe.wait_ge(landed[seen % RING].sem, landed[seen % RING].at(seen // RING + 1))
                if u >= nbank:
                    engine, n = order[u - nbank]
                    pe.wait_ge(done[engine].sem, done[engine].at(n))
                bank = c.banks[:, u % nbank, :]
                steps = [(k, p) for k in range(unit["k"]) for p in passes]
                for i, (k, p) in enumerate(steps):
                    left = unit["lhsT"](k, p[0]) if split else unit["lhsT"](k)
                    right = unit["rhs"](k, p[1]) if split else unit["rhs"](k)
                    last = nc.tensor.matmul(unit["out"](bank), left, right, start=(i == 0), stop=(i == len(steps) - 1))
                last.then_inc(products.sem, 1)
            other(pe, "tensor", len(units))

        def make_parts(engine, who, g):
            if who == "act":
                engine.wait_ge(landed[g % RING].sem, landed[g % RING].at(g // RING + 1))
                if g >= split["places"]:
                    engine.wait_ge(products.sem, products.at(last_of[g - split["places"]] + 1))
                nc.scalar.activation(split["part"](0, g), split["raw"](g), ACT.Copy).then_inc(c.high_parts.sem, 1)
            else:
                engine.wait_ge(c.high_parts.sem, c.high_parts.at(g + 1))
                nc.vector.tensor_tensor(split["part"](1, g), split["raw"](g), split["part"](0, g),
                                        ALU.subtract).then_inc(c.low_parts.sem, 1)

        def evacuate(engine, who):
            made = 0
            for u, unit in enumerate(units):
                while split and made < min(unit["load"] + 2, len(loads)):
                    make_parts(engine, who, made)
                    made += 1
                other(engine, who, u)
                if unit["engine"] == who:
                    engine.wait_ge(products.sem, products.at(u + 1))
                    unit["evac"](c.banks[:, u % nbank, :]).then_inc(done[who].sem, 1)
            other(engine, who, len(units))

        @block.scalar
        def _(act):
            evacuate(act, "act")

        @block.vector
        def _(dve):
            evacuate(dve, "dve")

    products.passed(len(units))
    if split:
        c.high_parts.passed(len(loads))
        c.low_parts.passed(len(loads))
    for who in ("act", "dve"):
        done[who].passed(count[who])
    for g in range(len(loads)):
        landed[g % RING].passed(1)


def turned(c, name, src, dst, tiles, evac):
    nc = c.nc
    with nc.Block(name) as block:

        @block.tensor
        def _(pe):
            for f in range(tiles):
                if f >= NBANK:
                    copied_by = c.act_done if f % 2 else c.dve_done
                    pe.wait_ge(copied_by.sem, copied_by.at((f - NBANK) // 2 + 1))
                for t in range(TT):
                    last = nc.tensor.transpose(c.banks[:, f % NBANK, t * P:(t + 1) * P], src(t, f), c.ident[:])
                last.then_inc(c.products.sem, 1)

        @block.scalar
        def _(act):
            for f in range(1, tiles, 2):
                act.wait_ge(c.products.sem, c.products.at(f + 1))
                evac("act", f, dst(f), c.banks[:, f % NBANK, :]).then_inc(c.act_done.sem, 1)

        @block.vector
        def _(dve):
            for f in range(0, tiles, 2):
                dve.wait_ge(c.products.sem, c.products.at(f + 1))
                evac("dve", f, dst(f), c.banks[:, f % NBANK, :]).then_inc(c.dve_done.sem, 1)

    c.products.passed(tiles)
    c.act_done.passed(tiles // 2)
    c.dve_done.passed((tiles + 1) // 2)


def turned_parts(c, name, src, parts, tiles, gain=None, loads=()):
    nc = c.nc
    assert tiles <= NBANK
    with nc.Block(name) as block:

        @block.sync
        def _(sp):
            for g, (dst, src_dram, _) in enumerate(loads):
                sp.dma_start(dst, src_dram).then_inc(c.landed[g].sem, 16)

        @block.tensor
        def _(pe):
            for f in range(tiles):
                for t in range(TT):
                    last = nc.tensor.transpose(c.banks[:, f, t * P:(t + 1) * P], src(t, f), c.ident[:])
                last.then_inc(c.products.sem, 1)

        @block.scalar
        def _(act):
            for f in range(tiles):
                act.wait_ge(c.products.sem, c.products.at(f + 1))
                nc.scalar.activation(parts[:, 0, f, :], c.banks[:, f, :], ACT.Copy,
                                     scale=1.0 if gain is None else gain[:, f:f + 1]).then_inc(c.high_parts.sem, 1)

        @block.vector
        def _(dve):
            for f in range(tiles):
                dve.wait_ge(c.high_parts.sem, c.high_parts.at(f + 1))
                if gain is None:
                    nc.vector.tensor_tensor(parts[:, 1, f, :], c.banks[:, f, :], parts[:, 0, f, :], ALU.subtract)
                else:
                    nc.vector.scalar_tensor_tensor(out=parts[:, 1, f, :], in0=c.banks[:, f, :], scalar=gain[:, f:f + 1],
                                                   in1=parts[:, 0, f, :], op0=ALU.mult, op1=ALU.subtract)

    c.products.passed(tiles)
    c.high_parts.passed(tiles)


def constants(c, A, bias_rows):
    nc = c.nc
    with ExitStack() as ctx:
        b = ctx.enter_context(nc.sbuf_tensor("expert_b", [E, 3 * FF], F32))[:]
        parts = ctx.enter_context(nc.sbuf_tensor("expert_b_parts", [E, 3, 3 * FF], BF16))
        block = ctx.enter_context(nc.Block("constants"))

        @block.sync
        def _(sp):
            sp.dma_start(b[:, 0:2 * FF], A["exp_b1_2"].rearrange("a e n -> (a e) n")).then_inc(c.loaded.sem, 16)
            sp.dma_start(b[:, 2 * FF:3 * FF], A["exp_b2_2"].rearrange("a e n -> (a e) n")).then_inc(c.loaded.sem, 16)
            sp.dma_start(c.x[:], A["x"].rearrange("a (t p) d -> p (a t) d", p=P)).then_inc(c.final_loaded.sem, 16)
            sp.wait_ge(c.dve_done.sem, c.dve_done.at(1))
            sp.dma_start(bias_rows, parts[:]).then_inc(c.stored.sem, 16)
            sp.wait_ge(c.stored.sem, c.stored.at(1))
            sp.wait_ge(c.final_loaded.sem, c.final_loaded.at(1))

        @block.vector
        def _(dve):
            dve.wait_ge(c.loaded.sem, c.loaded.at(2))
            for i in range(3):
                last = nc.vector.tensor_copy(parts[:, i, :], b)
                if i < 2:
                    c.dve(dve, last)
                    c.dve(dve, nc.vector.tensor_tensor(b, b, parts[:, i, :], ALU.subtract))
            last.then_inc(c.dve_done.sem, 1)

        @block.gpsimd
        def _(pool):
            nc.gpsimd.memset(c.zeros[:], 0.0).then_inc(c.masks.sem, 1)
            for m in (c.ident, c.upper, c.upper_strict):
                value = 0.0 if m is c.ident else 1.0
                nc.gpsimd.memset(m[:], value).then_inc(c.masks.sem, 1)
            nc.gpsimd.memset(c.ones[:], 1.0)
            pool.wait_ge(c.masks.sem, 4)
            nc.gpsimd.affine_select(out=c.ident[:], in_=c.ident[:], compare_op=ALU.not_equal, fill=1.0,
                                    base=0, pattern=[[-1, P]], channel_multiplier=1)
            nc.gpsimd.affine_select(out=c.upper[:], in_=c.upper[:], compare_op=ALU.is_ge, fill=0.0,
                                    base=0, pattern=[[1, P]], channel_multiplier=-1)
            nc.gpsimd.affine_select(out=c.upper_strict[:], in_=c.upper_strict[:], compare_op=ALU.is_gt, fill=0.0,
                                    base=0, pattern=[[1, P]], channel_multiplier=-1)

    c.loaded.passed(2)
    c.final_loaded.passed(1)
    c.masks.passed(4)
    c.stored.passed(1)
    c.dve_done.passed(1)


def rms_rows(c, name, src, dst, junk, stat, n, width, eps, also=None):
    nc = c.nc
    sums, root = stat[:, 0:n], stat[:, n:2 * n]
    with nc.Block(name) as block:

        @block.vector
        def _(dve):
            for i in range(n):
                last = nc.vector.tensor_tensor_reduce(out=junk(i), in0=src(i), in1=src(i), scale=1.0, scalar=0.0,
                                                      op0=ALU.mult, op1=ALU.add, accum_out=sums[:, i:i + 1])
            c.dve(dve, last)
            nc.vector.tensor_scalar(sums, sums, 1.0 / width, eps, ALU.mult, ALU.add).then_inc(c.dve_done.sem, 1)
            dve.wait_ge(c.act_done.sem, c.act_done.at(1))
            c.dve(dve, nc.vector.reciprocal(root, root))
            for i in range(n):
                last = nc.vector.tensor_scalar(dst(i), src(i), root[:, i:i + 1], None, ALU.mult)
                if also is not None:
                    c.dve(dve, last)
                    also(dve, i)

        @block.scalar
        def _(act):
            act.wait_ge(c.dve_done.sem, c.dve_done.at(1))
            nc.scalar.activation(root, sums, ACT.Sqrt).then_inc(c.act_done.sem, 1)

    c.act_done.passed(1)
    c.dve_done.passed(1)


def attention(c, name, heads, qT, kT, v, dv, scale, bias, bias_source, finish):
    nc = c.nc
    units = [(h, t) for h in range(heads) for t in range(TT)]
    n = len(units)
    scores_ready, turned_ready, out_ready = c.products, c.att_turned, c.att_out
    masked, probs_ready, probs_turned, used = c.att_masked, c.act_done, c.att_copied, c.dve_done
    with ExitStack() as ctx:
        s = ctx.enter_context(nc.sbuf_tensor(name + "_s", [P, 2, SEQ], F32))
        p = ctx.enter_context(nc.sbuf_tensor(name + "_p", [P, 2, SEQ], F32))
        pT = ctx.enter_context(nc.sbuf_tensor(name + "_pT", [P, 2, SEQ], F32))
        top = ctx.enter_context(nc.sbuf_tensor(name + "_top", [P, n], F32))
        total = ctx.enter_context(nc.sbuf_tensor(name + "_total", [P, n], F32))
        rinv = ctx.enter_context(nc.sbuf_tensor(name + "_rinv", [P, n], F32))
        with nc.Block(name) as block:

            @block.sync
            def _(sp):
                if bias_source is None:
                    return
                for h in range(heads):
                    if h >= 2:
                        sp.wait_ge(masked.sem, masked.at(TT * (h - 1)))
                    sp.dma_start(bias(h), bias_source[h, :, :]).then_inc(c.landed[h % 2].sem, 16)

            @block.gpsimd
            def _(pool):
                if bias_source is None:
                    return
                for h in range(heads):
                    landed = c.landed[h % 2]
                    pool.wait_ge(landed.sem, landed.at(h // 2 + 1))
                    nc.gpsimd.memset(bias(h)[0:CHUNK, SEQ - CHUNK:SEQ], NEG).then_inc(c.masks.sem, 1)

            @block.tensor
            def _(pe):
                for i in range(n + 2):
                    if i < n:
                        h, t = units[i]
                        if i >= 2:
                            pe.wait_ge(masked.sem, masked.at(i - 1))
                        nc.tensor.matmul(c.banks[:, i % 2, 0:(t + 1) * P], qT(h)[:, t * P:(t + 1) * P],
                                         kT(h)[:, 0:(t + 1) * P], start=True, stop=True).then_inc(scores_ready.sem, 1)
                    if 1 <= i <= n:
                        j = i - 1
                        t = units[j][1]
                        pe.wait_ge(probs_ready.sem, probs_ready.at(j + 1))
                        if j >= 2:
                            pe.wait_ge(probs_turned.sem, probs_turned.at(j - 1))
                        for b in range(t + 1):
                            last = nc.tensor.transpose(c.banks[:, 2 + j % 2, b * P:(b + 1) * P],
                                                       p[:, j % 2, b * P:(b + 1) * P], c.ident[:])
                        last.then_inc(turned_ready.sem, 1)
                    if i >= 2:
                        j = i - 2
                        h, t = units[j]
                        pe.wait_ge(probs_turned.sem, probs_turned.at(j + 1))
                        if j >= 2:
                            pe.wait_ge(used.sem, used.at(j - 1))
                        for b in range(t + 1):
                            last = nc.tensor.matmul(c.banks[:, 4 + j % 2, 0:dv], pT[:, j % 2, b * P:(b + 1) * P],
                                                    v(b, h), start=(b == 0), stop=(b == t))
                        last.then_inc(out_ready.sem, 1)

            @block.scalar
            def _(act):
                for i in range(n + 1):
                    if i < n:
                        t = units[i][1]
                        act.wait_ge(c.att_max.sem, c.att_max.at(i + 1))
                        if i >= 2:
                            act.wait_ge(turned_ready.sem, turned_ready.at(i - 1))
                        nc.scalar.activation(p[:, i % 2, 0:(t + 1) * P], s[:, i % 2, 0:(t + 1) * P], ACT.Exp,
                                             bias=top[:, i:i + 1], accum_out=total[:, i:i + 1]).then_inc(probs_ready.sem, 1)
                    if i >= 1:
                        j = i - 1
                        t = units[j][1]
                        act.wait_ge(turned_ready.sem, turned_ready.at(j + 1))
                        if j >= 2:
                            act.wait_ge(out_ready.sem, out_ready.at(j - 1))
                        nc.scalar.activation(pT[:, j % 2, 0:(t + 1) * P], c.banks[:, 2 + j % 2, 0:(t + 1) * P],
                                             ACT.Copy).then_inc(probs_turned.sem, 1)

            @block.vector
            def _(dve):
                for i in range(n + 2):
                    if i < n:
                        h, t = units[i]
                        w = (t + 1) * P
                        if t == 0 and bias_source is not None:
                            dve.wait_ge(c.masks.sem, c.masks.at(h + 1))
                        dve.wait_ge(scores_ready.sem, scores_ready.at(i + 1))
                        if i >= 2:
                            dve.wait_ge(probs_ready.sem, probs_ready.at(i - 1))
                        nc.vector.scalar_tensor_tensor(out=s[:, i % 2, 0:w], in0=c.banks[:, i % 2, 0:w], scalar=scale,
                                                       in1=bias(h)[:, SEQ - w:SEQ], op0=ALU.mult,
                                                       op1=ALU.add).then_inc(masked.sem, 1)
                        dve.wait_ge(masked.sem, masked.at(i + 1))
                        nc.vector.tensor_reduce(top[:, i:i + 1], s[:, i % 2, 0:w], AX.X, ALU.max,
                                                negate=True).then_inc(c.att_max.sem, 1)
                    if i >= 2:
                        j = i - 2
                        h, t = units[j]
                        dve.wait_ge(probs_ready.sem, probs_ready.at(j + 1))
                        c.dve(dve, nc.vector.reciprocal(rinv[:, j:j + 1], total[:, j:j + 1]))
                        dve.wait_ge(out_ready.sem, out_ready.at(j + 1))
                        finish(h, t, c.banks[:, 4 + j % 2, 0:dv], rinv[:, j:j + 1]).then_inc(used.sem, 1)

    for signal in (scores_ready, turned_ready, out_ready, masked, probs_ready, probs_turned, used, c.att_max):
        signal.passed(n)
    if bias_source is not None:
        c.masks.passed(heads)
        c.landed[0].passed((heads + 1) // 2)
        c.landed[1].passed(heads // 2)


def first_attention(c, A, qk, v, y):
    nc = c.nc
    with nc.sbuf_tensor("rel_bias_rows", [P, 2, SEQ], F32) as bias:
        def finish(h, t, product, rinv):
            place = y[:, t, h * HD:(h + 1) * HD]
            return nc.vector.scalar_tensor_tensor(out=place, in0=product, scalar=rinv, in1=place,
                                                  op0=ALU.mult, op1=ALU.mult)

        def head(base):
            return lambda h: qk[(h % 2) * HD:(h % 2 + 1) * HD, base + h // 2, :]

        attention(c, "band_attention", AH, head(0), head(3), lambda b, h: v[:, b, h * HD:(h + 1) * HD], HD,
                  HD ** -0.5, lambda h: bias[:, h % 2, :], A["rel_rows"], finish)


def first_block(c, A, mod, Y):
    nc = c.nc
    with ExitStack() as ctx:
        def sb(name, shape, dt=F32):
            return ctx.enter_context(nc.sbuf_tensor(name, shape, dt))

        y = sb("y", [P, TT, D])
        qk_m = sb("ml_qk", [P, 6, SEQ])
        v_m = sb("ml_v", [P, TT, MH, HD + 1])
        gate_m = sb("ml_gate", [P, TT, MW])
        pre_if = sb("ml_if", [P, TT, 2 * MH])
        qk_g = sb("gla_qk", [P, 2, SEQ])
        v_g = sb("gla_v", [P, TT, GW])
        rank_g = sb("gla_rank", [RANK, SEQ])
        stat = sb("stat_a", [P, 64])
        g_col = sb("norm_col", [P, DT])
        attention_only = ExitStack()
        qk_a = attention_only.enter_context(nc.sbuf_tensor("att_qk", [P, 6, SEQ], F32))
        v_a = attention_only.enter_context(nc.sbuf_tensor("att_v", [P, TT, AW], F32))
        with ExitStack() as projecting:
            hn = projecting.enter_context(nc.sbuf_tensor("hnT_parts", [P, 2, DT, SEQ], F32R))
            def load_g():
                with nc.Block("load_norm_g") as block:
                    @block.sync
                    def _(sp):
                        sp.dma_start(g_col[:], column(A["norm_g"].rearrange("a d -> (a d)"), DT), allow_slow_non_contiguous=True).then_inc(c.loaded.sem, 16)
                        sp.wait_ge(c.loaded.sem, c.loaded.at(1))
                    @block.gpsimd
                    def _(pool):
                        nc.gpsimd.memset(v_m[:, :, :, HD:HD + 1], 1.0)
                c.loaded.passed(1)
            load_g()
            rms_rows(c, "rms_in", lambda i: c.x[:, i, :], lambda i: y[:, i, :], lambda i: y[:, i, :], stat, TT, D, RMS_EPS)

            w_in = A["w_in"].rearrange("a (k p) n -> p (a k) n", p=P)
            groups = [(0, 256), (256, 256), (512, 256), (768, 256), (1024, 256), (1280, 256),
                      (1536, 256), (1792, 256), (2048, 256), (2304, 256), (2560, 256), (2816, 256),
                      (3072, 204), (3276, 192), (3468, 256), (3724, 272), (3996, 256)]
            slot, raws, places = DT * 272, 3, 2
            raw = projecting.enter_context(nc.sbuf_tensor("w_in_landing", [P, raws, slot], F32))
            parts = projecting.enter_context(nc.sbuf_tensor("w_in_parts", [P, 2, places, slot], F32R))
            modulating = projecting.enter_context(nc.sbuf_tensor("modulation_scratch", [P, 2 * DT * 256 + 4 * 256 + DT], F32))
            scratch = Carve(modulating[:])

            def raw_of(g):
                return raw[:, g % raws, 0:DT * groups[g][1]]

            def part_of(p, g):
                return parts[:, p, g % places, 0:DT * groups[g][1]]

            def weights_of(p, g):
                return part_of(p, g).rearrange("p (k n) -> p k n", k=DT)

            units = []

            def feature_unit(g, off, n, dst):
                engine = "dve" if len(units) % 2 else "act"
                units.append(dict(load=g, k=DT, width=SEQ, lhsT=lambda k, p: weights_of(p, g)[:, k, off:off + n],
                                  rhs=lambda k, p: hn[:, p, k, :], out=lambda b: b[0:n, :], engine=engine,
                                  evac=(lambda b: nc.vector.tensor_copy(dst, b[0:n, :])) if engine == "dve"
                                  else (lambda b: nc.scalar.activation(dst, b[0:n, :], ACT.Copy))))

            def token_units(g, off, n, engine, evac):
                for t in range(TT):
                    units.append(dict(load=g, k=DT, width=n, lhsT=lambda k, p, t=t: hn[:, p, k, t * P:(t + 1) * P],
                                      rhs=lambda k, p: weights_of(p, g)[:, k, off:off + n], out=lambda b: b[:, 0:n],
                                      engine=engine, evac=lambda b, t=t: evac(t, b[:, 0:n])))

            def gate(place, function):
                return lambda t, b: nc.scalar.activation(place(t), b, function)

            half, quarter = 2 * P, P
            for g in range(3):
                for f in range(2):
                    feature_unit(g, f * P, P, qk_a[:, 2 * g + f, :])
            token_units(3, 0, half, "dve", lambda t, b: nc.vector.tensor_copy(v_a[:, t, 0:half], b))

            def values_and_gate(t, b):
                nc.scalar.activation(v_a[:, t, half:AW], b[:, 0:quarter], ACT.Copy)
                return nc.scalar.activation(y[:, t, 0:quarter], b[:, quarter:half], ACT.Silu)

            token_units(4, 0, half, "act", values_and_gate)
            token_units(5, 0, half, "act", gate(lambda t: y[:, t, quarter:AW], ACT.Silu))
            for g in range(3):
                for f in range(2):
                    feature_unit(6 + g, f * P, P, qk_m[:, 2 * g + f, :])
            by_head = lambda b: b.rearrange("p (h d) -> p h d", d=HD)
            token_units(9, 0, half, "dve", lambda t, b: nc.vector.tensor_copy(v_m[:, t, 0:4, 0:HD], by_head(b)))

            def values_and_output_gate(t, b):
                nc.scalar.activation(v_m[:, t, 4:MH, 0:HD], by_head(b[:, 0:quarter]), ACT.Copy)
                return nc.scalar.activation(gate_m[:, t, 0:quarter], b[:, quarter:half], ACT.Sigmoid)

            token_units(10, 0, half, "act", values_and_output_gate)
            token_units(11, 0, half, "act", gate(lambda t: gate_m[:, t, quarter:MW], ACT.Sigmoid))
            token_units(12, 0, 2 * MH, "dve", lambda t, b: nc.vector.tensor_copy(pre_if[:, t, :], b))
            rest = MW // 2
            for i in range(2):
                token_units(12 + i, 0 if i else 2 * MH, rest, "act",
                            gate(lambda t, i=i: y[:, t, AW + i * rest:AW + (i + 1) * rest], ACT.Silu))
            for f in range(2):
                feature_unit(14, f * P, P, qk_g[:, f, :])
            token_units(15, 0, GW, "dve", lambda t, b: nc.vector.tensor_copy(v_g[:, t, :], b))
            feature_unit(15, GW, RANK, rank_g[:, :])
            token_units(16, 0, GW, "act", gate(lambda t: y[:, t, AW + MW:D], ACT.Silu))
            loads = [(raw_of(g).rearrange("p (k n) -> p k n", k=DT), w_in[:, :, a:a + n], None)
                     for g, (a, n) in enumerate(groups)]
            first_unit = [next(i for i, u in enumerate(units) if u["load"] == g) for g in range(len(groups))]
            widths = [u["width"] for u in units]
            keys = [first_unit[g - raws] if g >= raws else 0 for g in range(len(groups))]
            turned_parts(c, "turn_in", lambda t, f: y[:, t, f * P:(f + 1) * P], hn, DT, g_col, loads[0:raws])
            projection(c, "project_in", loads, units, modulation(c, A, mod, Y, scratch, widths, len(loads), keys),
                       dict(raws=raws, places=places, raw=raw_of, part=part_of), raws)
        first_attention(c, A, qk_a, v_a, y)
        attention_only.close()
        first_mlstm(c, A, qk_m, v_m, gate_m, pre_if, y)
        first_gla(c, A, qk_g, v_g, rank_g, y)
        out_projection(c, "project_out", A["w_out"].rearrange("a k n -> (a k) n"), y, lambda t, n, b:
                       nc.vector.tensor_tensor(c.x[:, t, n * 512:(n + 1) * 512], c.x[:, t, n * 512:(n + 1) * 512], b, ALU.add))


def log_sigmoid(c, dve, act_ready, act_done, x, t1, t2, out):
    nc = c.nc
    c.dve(dve, nc.vector.scalar_tensor_tensor(out=t1, in0=x, scalar=-1.0, in1=x, op0=ALU.mult, op1=ALU.max))
    nc.vector.tensor_scalar(out, x, 0.0, None, ALU.min).then_inc(act_ready.sem, 1)
    dve.wait_ge(act_done.sem, act_done.at(1))
    c.dve(dve, nc.vector.tensor_tensor(out, out, t2, ALU.subtract))


def log_sigmoid_act(c, act, act_ready, act_done, t1, t2):
    nc = c.nc
    act.wait_ge(act_ready.sem, act_ready.at(1))
    c.act(act, nc.scalar.activation(t2, t1, ACT.Exp, scale=-1.0))
    nc.scalar.activation(t2, t2, ACT.Ln, bias=1.0).then_inc(act_done.sem, 1)


def first_mlstm(c, A, qk, v, gate_o, pre_if, y):
    nc = c.nc
    H = MH
    with ExitStack() as ctx:
        def sb(name, shape, dt=F32):
            return ctx.enter_context(nc.sbuf_tensor(name, shape, dt))

        a_row = sb("a_rows", [H, SEQ])
        pick = sb("pick_head", [H, H, P])
        b_col = sb("b_cols", [P, TT, H])
        em_col = sb("em_cols", [P, TT, H])
        ml_g = sb("ml_norm", [P, MW])
        stat = sb("ml_stat", [P, 2, TT * H])
        hout = sb("ml_out", [P, TT, MW])
        early = ExitStack()
        gi, gf, t1, t2, lf, F, m, onerow, b_row = (
            early.enter_context(nc.sbuf_tensor(name, [H, SEQ], F32)) for name in
            ("gate_i", "gate_f", "mt1", "mt2", "log_f", "cum_f", "stabiliser", "one_rows", "b_rows"))
        taps = early.enter_context(nc.sbuf_tensor("conv_taps", [P, CONV, 6], F32))
        bias_if = early.enter_context(nc.sbuf_tensor("bias_if", [H, 2], F32))
        acc = early.enter_context(nc.sbuf_tensor("conv_acc", [P, 2, SEQ], F32))

        with nc.Block("mlstm_gates") as block:

            @block.sync
            def _(sp):
                sp.dma_start(taps[:], A["conv_w"].rearrange("a j (f p) -> p (a j) f", p=P), allow_slow_non_contiguous=True).then_inc(c.loaded.sem, 16)
                sp.dma_start(bias_if[:], A["b_gates"].rearrange("a (g h) -> h (a g)", g=2), allow_slow_non_contiguous=True).then_inc(c.loaded.sem, 16)
                sp.dma_start(ml_g[:], over_partitions(A["ml_norm_g"].rearrange("a n -> (a n)"), MW)).then_inc(c.loaded.sem, 16)

            @block.tensor
            def _(pe):
                for g in range(2):
                    for t in range(TT):
                        last = nc.tensor.transpose(c.banks[0:H, g, t * P:(t + 1) * P],
                                                   pre_if[:, t, g * H:(g + 1) * H], c.ident[:])
                last.then_inc(c.products.sem, 1)

            @block.gpsimd
            def _(pool):
                nc.gpsimd.memset(onerow[:], 1.0)
                c.pool(pool, nc.gpsimd.memset(pick[:], 0.0))
                nc.gpsimd.affine_select(out=pick[:], in_=pick[:], compare_op=ALU.not_equal, fill=1.0, base=0,
                                        pattern=[[-1, H], [0, P]], channel_multiplier=1)

            @block.vector
            def _(dve):
                dve.wait_ge(c.loaded.sem, c.loaded.at(3))
                for f in range(6):
                    x, o = qk[:, f, :], acc[:, f % 2, :]
                    if f >= 2:
                        dve.wait_ge(c.act_done.sem, c.act_done.at(f - 1))
                    c.dve(dve, nc.vector.tensor_scalar(o, x, taps[:, CONV - 1, f:f + 1], None, ALU.mult))
                    for back in range(1, CONV):
                        last = nc.vector.scalar_tensor_tensor(
                            out=o[:, back:SEQ], in0=x[:, 0:SEQ - back], scalar=taps[:, CONV - 1 - back, f:f + 1],
                            in1=o[:, back:SEQ], op0=ALU.mult, op1=ALU.add)
                        if back < CONV - 1:
                            c.dve(dve, last)
                    last.then_inc(c.dve_done.sem, 1)
                dve.wait_ge(c.products.sem, c.products.at(1))
                nc.vector.tensor_scalar(gi[:], c.banks[0:H, 0, :], bias_if[:, 0:1], None, ALU.add)
                c.dve(dve, nc.vector.tensor_scalar(gf[:], c.banks[0:H, 1, :], bias_if[:, 1:2], None, ALU.add))

            @block.scalar
            def _(act):
                for f in range(6):
                    act.wait_ge(c.dve_done.sem, c.dve_done.at(f + 1))
                    nc.scalar.activation(qk[:, f, :], acc[:, f % 2, :], ACT.Silu).then_inc(c.act_done.sem, 1)

        c.products.passed(1)
        c.dve_done.passed(6)
        c.act_done.passed(6)
        c.loaded.passed(3)

        with nc.Block("mlstm_scans") as block:

            @block.vector
            def _(dve):
                log_sigmoid(c, dve, c.dve_done, c.act_done, gf[:], t1[:], t2[:], lf[:])
                nc.vector.tensor_tensor_scan(F[:], onerow[:], lf[:], 0.0, ALU.mult, ALU.add)
                c.dve(dve, nc.vector.tensor_tensor_scan(m[:], lf[:], gi[:], 0.0, ALU.add, ALU.max))
                nc.vector.tensor_tensor(a_row[:], F[:], m[:], ALU.subtract)
                nc.vector.tensor_tensor(b_row[:], gi[:], F[:], ALU.subtract).then_inc(c.dve_done.sem, 1)
                dve.wait_ge(c.products.sem, c.products.at(1))
                nc.vector.tensor_copy(b_col[:], c.banks[:, 0, 0:TT * H].rearrange("p (t h) -> p t h", t=TT))
                nc.vector.tensor_copy(em_col[:], c.banks[:, 1, 0:TT * H].rearrange("p (t h) -> p t h", t=TT))

            @block.scalar
            def _(act):
                log_sigmoid_act(c, act, c.dve_done, c.act_done, t1[:], t2[:])
                act.wait_ge(c.dve_done.sem, c.dve_done.at(2))
                nc.scalar.activation(t1[:], m[:], ACT.Exp, scale=-1.0).then_inc(c.act_done.sem, 1)

            @block.tensor
            def _(pe):
                pe.wait_ge(c.dve_done.sem, c.dve_done.at(2))
                pe.wait_ge(c.act_done.sem, c.act_done.at(2))
                for bank, rows in ((0, b_row), (1, t1)):
                    for t in range(TT):
                        last = nc.tensor.transpose(c.banks[:, bank, t * H:(t + 1) * H], rows[:, t * P:(t + 1) * P],
                                                   c.ident[0:H, 0:H])
                last.then_inc(c.products.sem, 1)

        c.products.passed(1)
        c.dve_done.passed(2)
        c.act_done.passed(2)

        early.close()
        with ExitStack() as inner:
            expo = inner.enter_context(nc.sbuf_tensor("decay_exp", [P, 2, SEQ], F32))
            dec = inner.enter_context(nc.sbuf_tensor("decay", [P, 2, SEQ], F32))
            start = [sum((TT - i) * P for i in range(j)) for j in range(TT)]
            sd = inner.enter_context(nc.sbuf_tensor("scores_decayed", [P, 2, sum((TT - j) * P for j in range(TT))], F32))
            den = inner.enter_context(nc.sbuf_tensor("ml_den", [P, 2, TT], F32))
            units = [(h, j) for h in range(H) for j in range(TT)]
            n = len(units)
            rows_ready, s_ready, out_ready = c.products, c.att_turned, c.att_out
            expo_ready, decay_ready, masked_ready, sd_ready, used = c.att_max, c.act_done, c.masks, c.att_masked, c.dve_done
            with nc.Block("mlstm_attention") as block:

                @block.tensor
                def _(pe):
                    for h in range(H + 1):
                        if h < H:
                            if h >= 2:
                                pe.wait_ge(expo_ready.sem, expo_ready.at(TT * (h - 1)))
                            nc.tensor.matmul(c.banks[:, h % 2, :], pick[:, h, :], a_row[:], start=True,
                                             stop=True).then_inc(rows_ready.sem, 1)
                            lo = (h % 2) * HD
                            for j in range(TT):
                                i = TT * h + j
                                if i >= 2:
                                    pe.wait_ge(sd_ready.sem, sd_ready.at(i - 1))
                                nc.tensor.matmul(c.banks[:, 2 + i % 2, j * P:SEQ],
                                                 qk[lo:lo + HD, 3 + h // 2, j * P:(j + 1) * P],
                                                 qk[lo:lo + HD, h // 2, j * P:SEQ], start=True,
                                                 stop=True).then_inc(s_ready.sem, 1)
                        if h >= 1:
                            g = h - 1
                            pe.wait_ge(sd_ready.sem, sd_ready.at(TT * (g + 1)))
                            if g >= 2:
                                pe.wait_ge(used.sem, used.at(g - 1))
                            for t in range(TT):
                                for j in range(t + 1):
                                    last = nc.tensor.matmul(c.banks[:, 4 + g % 2, t * (HD + 1):(t + 1) * (HD + 1)],
                                                            sd[:, g % 2, start[j] + (t - j) * P:start[j] + (t - j + 1) * P], v[:, j, g, :],
                                                            start=(j == 0), stop=(j == t))
                            last.then_inc(out_ready.sem, 1)

                def take(dve, h):
                    dve.wait_ge(out_ready.sem, out_ready.at(h + 1))
                    o = c.banks[:, 4 + h % 2, 0:TT * (HD + 1)].rearrange("p (t d) -> p t d", t=TT)
                    d = den[:, h % 2, :]
                    c.dve(dve, nc.vector.tensor_scalar(d, o[:, :, HD], -1.0, None, ALU.mult))
                    c.dve(dve, nc.vector.tensor_tensor(d, d, o[:, :, HD], ALU.max))
                    c.dve(dve, nc.vector.tensor_tensor(d, d, em_col[:, :, h], ALU.max))
                    c.dve(dve, nc.vector.reciprocal(d, d))
                    for t in range(TT):
                        last = nc.vector.tensor_scalar(hout[:, t, h * HD:(h + 1) * HD], o[:, t, 0:HD], d[:, t:t + 1],
                                                       None, ALU.mult)
                    last.then_inc(used.sem, 1)

                @block.vector
                def _(dve):
                    def exponent(i):
                        h, j = units[i]
                        if j == 0:
                            dve.wait_ge(rows_ready.sem, rows_ready.at(h + 1))
                        if i >= 2:
                            dve.wait_ge(decay_ready.sem, decay_ready.at(i - 1))
                        nc.vector.tensor_scalar(expo[:, i % 2, j * P:SEQ], c.banks[:, h % 2, j * P:SEQ],
                                                b_col[:, j, h:h + 1], 0.0, ALU.add, ALU.min).then_inc(expo_ready.sem, 1)

                    exponent(0)
                    for i in range(n):
                        h, j = units[i]
                        if i + 1 < n:
                            exponent(i + 1)
                        dve.wait_ge(masked_ready.sem, masked_ready.at(i + 1))
                        dve.wait_ge(s_ready.sem, s_ready.at(i + 1))
                        if h >= 2:
                            dve.wait_ge(out_ready.sem, out_ready.at(h - 1))
                        nc.vector.scalar_tensor_tensor(out=sd[:, h % 2, start[j]:start[j] + SEQ - j * P], in0=c.banks[:, 2 + i % 2, j * P:SEQ],
                                                       scalar=HD ** -0.5, in1=dec[:, i % 2, j * P:SEQ], op0=ALU.mult,
                                                       op1=ALU.mult).then_inc(sd_ready.sem, 1)
                        if j == 1 and h >= 1:
                            take(dve, h - 1)
                    take(dve, H - 1)

                @block.scalar
                def _(act):
                    for i in range(n):
                        h, j = units[i]
                        act.wait_ge(expo_ready.sem, expo_ready.at(i + 1))
                        if i >= 2:
                            act.wait_ge(sd_ready.sem, sd_ready.at(i - 1))
                        nc.scalar.activation(dec[:, i % 2, j * P:SEQ], expo[:, i % 2, j * P:SEQ],
                                             ACT.Exp).then_inc(decay_ready.sem, 1)

                @block.gpsimd
                def _(pool):
                    for i in range(n):
                        j = units[i][1]
                        pool.wait_ge(decay_ready.sem, decay_ready.at(i + 1))
                        diag = dec[:, i % 2, j * P:(j + 1) * P]
                        nc.gpsimd.tensor_tensor(diag, diag, c.upper[:], ALU.mult).then_inc(masked_ready.sem, 1)

            rows_ready.passed(H)
            out_ready.passed(H)
            used.passed(H)
            for signal in (s_ready, expo_ready, decay_ready, masked_ready, sd_ready):
                signal.passed(n)

        def gated(dve):
            place = y[:, :, AW:AW + MW]
            c.dve(dve, nc.vector.tensor_tensor(hout[:], hout[:], ml_g[:].unsqueeze(1).broadcast_to([P, TT, MW]), ALU.mult))
            c.dve(dve, nc.vector.tensor_tensor(place, place, gate_o[:], ALU.mult))
            nc.vector.tensor_tensor(place, place, hout[:], ALU.mult)

        with nc.sbuf_tensor("ml_square", [P, TT * H, HD], F32) as square:
            head_norm(c, "mlstm_norm", hout[:].rearrange("p t (h d) -> p (t h) d", h=H), square[:], stat[:], TT * H, HD,
                      RMS_EPS, False, gated)


def head_norm(c, name, x3, square, stat, n, width, eps, centered, after):
    nc = c.nc
    s, r = stat[:, 0, :], stat[:, 1, :]
    with nc.Block(name) as block:

        @block.vector
        def _(dve):
            if centered:
                c.dve(dve, nc.vector.tensor_reduce(s, x3, AX.X, ALU.add))
                c.dve(dve, nc.vector.tensor_scalar(s, s, 1.0 / width, None, ALU.mult))
                c.dve(dve, nc.vector.tensor_tensor(x3, x3, s.unsqueeze(2).broadcast_to([P, n, width]), ALU.subtract))
            c.dve(dve, nc.vector.tensor_tensor(square, x3, x3, ALU.mult))
            c.dve(dve, nc.vector.tensor_reduce(s, square, AX.X, ALU.add))
            nc.vector.tensor_scalar(s, s, 1.0 / width, eps, ALU.mult, ALU.add).then_inc(c.dve_done.sem, 1)
            dve.wait_ge(c.act_done.sem, c.act_done.at(1))
            c.dve(dve, nc.vector.reciprocal(r, r))
            c.dve(dve, nc.vector.tensor_tensor(x3, x3, r.unsqueeze(2).broadcast_to([P, n, width]), ALU.mult))
            after(dve)

        @block.scalar
        def _(act):
            act.wait_ge(c.dve_done.sem, c.dve_done.at(1))
            nc.scalar.activation(r, s, ACT.Sqrt).then_inc(c.act_done.sem, 1)

    c.dve_done.passed(1)
    c.act_done.passed(1)


def first_gla(c, A, qk, v, rank, y):
    nc = c.nc
    MID = P // 2 - 1
    CLAMP = 40.0
    with ExitStack() as ctx:
        def sb(name, shape, dt=F32):
            return ctx.enter_context(nc.sbuf_tensor(name, shape, dt))

        wa = sb("w_alpha_s", [RANK, GKW])
        ba = sb("b_alpha_s", [P, 1])
        la = sb("log_alpha", [P, SEQ])
        xa = sb("alpha_x", [P, SEQ])
        t1 = sb("gt1", [P, SEQ])
        t2 = sb("gt2", [P, SEQ])
        F = sb("cum_alpha", [P, SEQ])
        onerow = sb("gla_ones", [P, P])
        bd = sb("gla_blocks", [P, GW])
        diff = sb("gla_diff", [P, TT])
        into = sb("gla_into", [P, TT])
        outof = sb("gla_outof", [P, TT])
        ktok = sb("gla_ktok", [P, TT, P])
        at = sb("gla_at", [P, 2, SEQ])
        state = sb("gla_state", [P, 2, GW])
        hout = sb("gla_out", [P, TT, GW])
        square = sb("gla_square", [P, TT * GH, GDV])
        stat = sb("gla_stat", [P, 2, TT * GH])
        gg = sb("gla_norm", [P, GW])
        q, k = qk[:, 0, :], qk[:, 1, :]

        with nc.Block("gla_decays") as block:

            @block.sync
            def _(sp):
                sp.dma_start(wa[:], A["w_alpha"].rearrange("a r k -> (a r) k")).then_inc(c.loaded.sem, 16)
                sp.dma_start(ba[:], column(A["b_alpha"].rearrange("a n -> (a n)"), 1), allow_slow_non_contiguous=True).then_inc(c.loaded.sem, 16)
                sp.dma_start(gg[:], over_partitions(A["gla_norm_g"].rearrange("a n -> (a n)"), GW)).then_inc(c.loaded.sem, 16)
                sp.wait_ge(c.loaded.sem, c.loaded.at(3))

            @block.gpsimd
            def _(pool):
                nc.gpsimd.memset(onerow[:], 1.0)
                nc.gpsimd.memset(state[:], 0.0)
                c.pool(pool, nc.gpsimd.memset(bd[:], 0.0))
                for h in range(GH):
                    nc.gpsimd.memset(bd[h * GDK:(h + 1) * GDK, h * GDV:(h + 1) * GDV], 1.0)

            @block.tensor
            def _(pe):
                pe.wait_ge(c.loaded.sem, c.loaded.at(3))
                nc.tensor.matmul(c.banks[:, 0, :], wa[:], rank[:], start=True, stop=True).then_inc(c.products.sem, 1)

            @block.vector
            def _(dve):
                dve.wait_ge(c.loaded.sem, c.loaded.at(3))
                dve.wait_ge(c.products.sem, c.products.at(1))
                c.dve(dve, nc.vector.tensor_scalar(xa[:], c.banks[:, 0, :], ba[:], None, ALU.add))
                log_sigmoid(c, dve, c.dve_done, c.act_done, xa[:], t1[:], t2[:], la[:])
                c.dve(dve, nc.vector.tensor_scalar(la[:], la[:], 1.0 / TAU, None, ALU.mult))

            @block.scalar
            def _(act):
                log_sigmoid_act(c, act, c.dve_done, c.act_done, t1[:], t2[:])

        c.loaded.passed(3)
        c.products.passed(1)
        c.dve_done.passed(1)
        c.act_done.passed(1)

        with nc.Block("gla_scaled") as block:

            @block.vector
            def _(dve):
                for t in range(TT):
                    s = slice(t * P, (t + 1) * P)
                    last = nc.vector.tensor_tensor_scan(F[:, s], onerow[:], la[:, s], 0.0, ALU.mult, ALU.add)
                c.dve(dve, last)
                ends = F[:].rearrange("p (t s) -> p t s", t=TT)
                nc.vector.tensor_tensor(diff[:], ends[:, :, P - 1], ends[:, :, MID], ALU.subtract)
                for t in range(TT):
                    s, mid = slice(t * P, (t + 1) * P), F[:, t * P + MID:t * P + MID + 1]
                    nc.vector.tensor_scalar(t1[:, s], F[:, s], mid, CLAMP, ALU.subtract, ALU.min)
                    last = nc.vector.tensor_scalar(t2[:, s], F[:, s], mid, -CLAMP, ALU.subtract, ALU.max)
                last.then_inc(c.dve_done.sem, 1)
                dve.wait_ge(c.act_done.sem, c.act_done.at(1))
                nc.vector.scalar_tensor_tensor(out=q, in0=q, scalar=GDK ** -0.5, in1=t1[:], op0=ALU.mult, op1=ALU.mult)
                nc.vector.tensor_tensor(k, k, t2[:], ALU.mult).then_inc(c.dve_done.sem, 1)
                dve.wait_ge(c.products.sem, c.products.at(1))
                nc.vector.tensor_copy(ktok[:], c.banks[:, 0, :].rearrange("p (t s) -> p t s", t=TT))

            @block.scalar
            def _(act):
                act.wait_ge(c.dve_done.sem, c.dve_done.at(1))
                nc.scalar.activation(t1[:], t1[:], ACT.Exp)
                nc.scalar.activation(into[:], F[:].rearrange("p (t s) -> p t s", t=TT)[:, :, MID], ACT.Exp)
                nc.scalar.activation(outof[:], diff[:], ACT.Exp)
                nc.scalar.activation(t2[:], t2[:], ACT.Exp, scale=-1.0).then_inc(c.act_done.sem, 1)

            @block.tensor
            def _(pe):
                pe.wait_ge(c.dve_done.sem, c.dve_done.at(2))
                for t in range(TT):
                    last = nc.tensor.transpose(c.banks[:, 0, t * P:(t + 1) * P], k[:, t * P:(t + 1) * P], c.ident[:])
                last.then_inc(c.products.sem, 1)

        c.products.passed(1)
        c.dve_done.passed(2)
        c.act_done.passed(1)

        masked, out_ready, used, state_ready = c.att_masked, c.att_out, c.dve_done, c.att_max
        with nc.Block("gla_tiles") as block:

            @block.tensor
            def _(pe):
                for t in range(TT):
                    s = slice(t * P, (t + 1) * P)
                    for h in range(GH):
                        r = slice(h * GDK, (h + 1) * GDK)
                        last = nc.tensor.matmul(c.banks[:, h, s], k[r, s], q[r, s], start=True, stop=True)
                last.then_inc(c.products.sem, 1)
                for t in range(TT):
                    s = slice(t * P, (t + 1) * P)
                    if t >= 2:
                        pe.wait_ge(used.sem, used.at(t - 1))
                        pe.wait_ge(state_ready.sem, state_ready.at(2 * (t - 1)))
                    nc.tensor.matmul(c.banks[:, 6 + t % 2, 0:GW], ktok[:, t, :], v[:, t, :], start=True,
                                     stop=True).then_inc(c.att_turned.sem, 1)
                    pe.wait_ge(masked.sem, masked.at(t + 1))
                    pe.wait_ge(state_ready.sem, state_ready.at(2 * t + 1))
                    for h in range(GH):
                        o = c.banks[:, 4 + t % 2, h * GDV:(h + 1) * GDV]
                        nc.tensor.matmul(o, q[:, s], state[:, t % 2, h * GDV:(h + 1) * GDV], start=True, stop=False)
                        last = nc.tensor.matmul(o, at[:, t % 2, h * P:(h + 1) * P], v[:, t, h * GDV:(h + 1) * GDV],
                                                start=False, stop=True)
                    last.then_inc(out_ready.sem, 1)

            @block.vector
            def _(dve):
                dve.wait_ge(c.products.sem, c.products.at(1))
                for t in range(TT):
                    if t >= 2:
                        dve.wait_ge(out_ready.sem, out_ready.at(t - 1))
                    nc.vector.tensor_tensor(at[:, t % 2, :].rearrange("p (h s) -> p h s", h=GH),
                                            c.banks[:, 0:GH, t * P:(t + 1) * P],
                                            c.upper[:].unsqueeze(1).broadcast_to([P, GH, P]), ALU.mult).then_inc(masked.sem, 1)
                    cur, nxt = state[:, t % 2, :], state[:, (t + 1) % 2, :]
                    nc.vector.tensor_scalar(cur, cur, into[:, t:t + 1], None, ALU.mult).then_inc(state_ready.sem, 1)
                    dve.wait_ge(c.att_turned.sem, c.att_turned.at(t + 1))
                    if t >= 1:
                        dve.wait_ge(out_ready.sem, out_ready.at(t))
                    c.dve(dve, nc.vector.tensor_tensor(nxt, c.banks[:, 6 + t % 2, 0:GW], bd[:], ALU.mult))
                    c.dve(dve, nc.vector.tensor_tensor(nxt, nxt, cur, ALU.add))
                    nc.vector.tensor_scalar(nxt, nxt, outof[:, t:t + 1], None, ALU.mult).then_inc(state_ready.sem, 1)
                    dve.wait_ge(state_ready.sem, state_ready.at(2 * (t + 1)))
                    dve.wait_ge(out_ready.sem, out_ready.at(t + 1))
                    nc.vector.tensor_copy(hout[:, t, :], c.banks[:, 4 + t % 2, 0:GW]).then_inc(used.sem, 1)

        c.products.passed(1)
        for signal in (masked, out_ready, used, c.att_turned):
            signal.passed(TT)
        state_ready.passed(2 * TT)

        def gated(dve):
            place = y[:, :, AW + MW:D]
            c.dve(dve, nc.vector.tensor_tensor(hout[:], hout[:], gg[:].unsqueeze(1).broadcast_to([P, TT, GW]), ALU.mult))
            nc.vector.tensor_tensor(place, place, hout[:], ALU.mult)

        head_norm(c, "gla_norm", hout[:].rearrange("p t (h d) -> p (t h) d", h=GH), square[:], stat[:], TT * GH, GDV,
                  RMS_EPS, False, gated)


def copied(c):
    nc = c.nc

    def evac(who, f, dst, src):
        if who == "act":
            return nc.scalar.activation(dst, src, ACT.Copy)
        return nc.vector.tensor_copy(dst, src)

    return evac


def out_projection(c, name, weights, y, evac):
    nc = c.nc
    half = D // 2
    with ExitStack() as ctx:
        c.far.close()
        yT = ctx.enter_context(nc.sbuf_tensor(name + "_yT", [P, 2, DT, SEQ], F32R))
        raw = ctx.enter_context(nc.sbuf_tensor(name + "_landing", [P, 2, DT, half], F32, side="right"))
        parts = ctx.enter_context(nc.sbuf_tensor(name + "_parts", [P, 2, 2, DT, half], F32R, side="right"))
        w = weights.rearrange("(k p) n -> p k n", p=P)
        loads = [(raw[:, g], w[:, :, g * half:(g + 1) * half], None) for g in range(2)]
        turned_parts(c, name + "_turn", lambda t, f: y[:, t, f * P:(f + 1) * P], yT, DT, loads=loads)
        units = [dict(load=n, k=DT, lhsT=lambda k, p, t=t: yT[:, p, k, t * P:(t + 1) * P],
                      rhs=lambda k, p, n=n: parts[:, p, n, k, :], out=lambda b: b, engine="dve",
                      evac=lambda b, t=t, n=n: evac(t, n, b)) for n in range(2) for t in range(TT)]
        projection(c, name, loads, units, under_way=2,
                   split=dict(raws=2, places=2, raw=lambda g: raw[:, g], part=lambda p, g: parts[:, p, g]))


class Carve:

    def __init__(self, flat):
        self.flat = flat
        self.at = 0

    def __call__(self, *shape):
        n = 1
        for d in shape:
            n *= d
        piece = self.flat[:, self.at:self.at + n]
        self.at += n
        assert self.at <= self.flat.shape[1], self.at
        if len(shape) == 1:
            return piece
        names = " ".join("abcde"[i] for i in range(len(shape)))
        sizes = {"abcde"[i]: d for i, d in enumerate(shape[1:], 1)}
        return piece.rearrange(f"p ({names}) -> p {names}", **sizes)


def spread(v, n):
    return v.unsqueeze(1).broadcast_to([P, n, v.shape[-1]])


def modulation(c, A, mod, Y, scratch, widths, loads, load_key):
    nc = c.nc
    wide, places = 256, 2
    sections = 6 * D // wide
    ada = A["ada_w_2"].rearrange("a (k p) n -> p (a k) n", p=P)
    bias = A["ada_b_2"]
    out = mod.rearrange("(a n) -> a n", a=1)
    w = [scratch(DT, wide) for _ in range(places)]
    acc = scratch(2, wide)
    row = scratch(2, wide)[0:1]
    col = scratch(DT)
    own = lambda name, step=1: Signal(nc, name, step)
    ada_in = [own(f"ada_in_{i}", 16) for i in range(places)]
    c_in, c_ready, added, summed = own("c_in", 16), own("silu_c_ready"), own("tiles_added"), own("partitions_added")
    bias_in, rows_done, row_stored = own("ada_b_in", 16), own("mod_rows_ready"), own("mod_stored", 16)
    until = np.cumsum(widths)
    unit_of = [int(np.searchsorted(until, (q + 1) / (sections + 2) * until[-1])) for q in range(sections + 1)]

    def load(q):
        def piece(sp):
            if q >= places:
                sp.wait_ge(added.sem, q - places + 1)
            sp.dma_start(w[q % places], ada[:, :, q * wide:(q + 1) * wide]).then_inc(ada_in[q % places].sem, 16)
        return piece

    def add_tiles(q):
        def piece(dve):
            dve.wait_ge(ada_in[q % places].sem, 16 * (q // places + 1))
            if q == 0:
                dve.wait_ge(c_ready.sem, 1)
            if q >= 2:
                dve.wait_ge(summed.sem, q - 1)
            c.dve(dve, nc.vector.tensor_scalar(acc[:, q % 2, :], w[q % places][:, 0, :], col[:, 0:1], None, ALU.mult))
            for k in range(1, DT):
                last = nc.vector.scalar_tensor_tensor(out=acc[:, q % 2, :], in0=w[q % places][:, k, :], scalar=col[:, k:k + 1],
                                                      in1=acc[:, q % 2, :], op0=ALU.mult, op1=ALU.add)
                if k < DT - 1:
                    c.dve(dve, last)
            last.then_inc(added.sem, 1)
        return piece

    def add_partitions(q):
        def piece(pe):
            pe.wait_ge(added.sem, q + 1)
            if q >= 1:
                pe.wait_ge(rows_done.sem, q)
            nc.tensor.matmul(c.banks[0:1, NBANK - 1, 0:wide], c.ones[:, 0:1], acc[:, q % 2, :], start=True,
                             stop=True).then_inc(summed.sem, 1)
        return piece

    def add_bias(q):
        def piece(dve):
            dve.wait_ge(summed.sem, q + 1)
            dve.wait_ge(bias_in.sem, 16 * (q + 1))
            nc.vector.tensor_tensor(row[:, q % 2, :], c.banks[0:1, NBANK - 1, 0:wide], row[:, q % 2, :],
                                    ALU.add).then_inc(rows_done.sem, 1)
        return piece

    def silu(act):
        act.wait_ge(c_in.sem, 16)
        nc.scalar.activation(col, col, ACT.Silu).then_inc(c_ready.sem, 1)

    def fill_zeros(sp):
        for n in range(D // wide):
            sp.dma_start(Y[E * CAP:SLOTS, n * wide:(n + 1) * wide].rearrange("(b s) n -> s b n", s=CAP),
                         c.zeros[:].unsqueeze(1).broadcast_to([P, EXTRA, wide])).then_inc(c.zero_filled.sem, 16)

    def pool_program(pool):
        def load_bias(q):
            pool.dma_start(row[:, q % 2, :], bias[:, q * wide:(q + 1) * wide]).then_inc(bias_in.sem, 16)

        pool.dma_start(col, column(A["c_2"].rearrange("a d -> (a d)"), DT),
                       allow_slow_non_contiguous=True).then_inc(c_in.sem, 16)
        load_bias(0)
        for q in range(sections):
            if q + 1 < sections:
                if q >= 1:
                    pool.wait_ge(row_stored.sem, 16 * q)
                pool.wait_ge(bias_in.sem, 16 * (q + 1))
                load_bias(q + 1)
            pool.wait_ge(rows_done.sem, q + 1)
            pool.dma_start(out[:, q * wide:(q + 1) * wide], row[:, q % 2, :]).then_inc(row_stored.sem, 16)
        pool.wait_ge(row_stored.sem, 16 * sections)

    vector, tensor, sync = [], [], []
    for q in range(sections):
        vector += [(unit_of[q], add_tiles(q))] + ([(unit_of[q], add_bias(q - 1))] if q else [])
        tensor.append((unit_of[q + 1], add_partitions(q)))
        free = unit_of[q - places] if q >= places else 0
        sync.append((next((g for g in range(1, loads) if load_key[g] > free), loads), load(q)))
    vector.append((unit_of[sections], add_bias(sections - 1)))
    sync.append((loads, fill_zeros))
    return dict(banks=NBANK - 1, sync=sync, dve=vector, act=[(0, silu)], tensor=tensor, gpsimd=pool_program)


def layer_norm(c, name, src, dst, vectors, then, before=None):
    nc = c.nc
    with ExitStack() as ctx:
        stats = ctx.enter_context(nc.sbuf_tensor(name + "_stats", [P, TT, 2, 6], F32))
        mv = ctx.enter_context(nc.sbuf_tensor(name + "_mv", [P, TT, 2], F32))
        rstd = ctx.enter_context(nc.sbuf_tensor(name + "_rstd", [P, TT], F32))
        g, b = vectors[0][0], vectors[1][0]
        with nc.Block(name) as block:

            @block.sync
            def _(sp):
                for place, vector in vectors:
                    sp.dma_start(place, over_partitions(vector, D)).then_inc(c.loaded.sem, 16)

            @block.vector
            def _(dve):
                if before is not None:
                    before(dve)
                for t in range(TT):
                    for half in range(2):
                        last = nc.vector.bn_stats(stats[:, t, half, :], src(t)[:, half * 512:(half + 1) * 512])
                c.dve(dve, last)
                for t in range(TT):
                    last = nc.vector.bn_aggr(mv[:, t, :], stats[:, t, :, :].rearrange("p a b -> p (a b)"))
                c.dve(dve, last)
                nc.vector.tensor_scalar(rstd[:], mv[:, :, 1], LN_EPS, None, ALU.add).then_inc(c.dve_done.sem, 1)
                dve.wait_ge(c.act_done.sem, c.act_done.at(1))
                c.dve(dve, nc.vector.reciprocal(rstd[:], rstd[:]))
                dve.wait_ge(c.loaded.sem, c.loaded.at(len(vectors)))
                for t in range(TT):
                    c.dve(dve, nc.vector.tensor_scalar(dst(t), src(t), mv[:, t, 0:1], rstd[:, t:t + 1],
                                                       ALU.subtract, ALU.mult))
                    c.dve(dve, nc.vector.tensor_tensor(dst(t), dst(t), g, ALU.mult))
                    c.dve(dve, nc.vector.tensor_tensor(dst(t), dst(t), b, ALU.add))
                    then(dve, t)

            @block.scalar
            def _(act):
                act.wait_ge(c.dve_done.sem, c.dve_done.at(1))
                nc.scalar.activation(rstd[:], rstd[:], ACT.Sqrt).then_inc(c.act_done.sem, 1)

    c.loaded.passed(len(vectors))
    c.dve_done.passed(1)
    c.act_done.passed(1)


def second_block(c, A, mod, bias_rows, Y, out):
    nc = c.nc
    part = lambda i: mod[i * D:(i + 1) * D]
    with ExitStack() as ctx:
        h = ctx.enter_context(nc.sbuf_tensor("h_mix", [P, TT, D], F32))
        hT = c.far.enter_context(nc.sbuf_tensor("hT_parts", [P, 2, DT, SEQ], F32R, side="right"))
        with ExitStack() as raw_free:
            with ExitStack() as inner:
                vec = inner.enter_context(nc.sbuf_tensor("enter_vectors", [P, 5, D], F32))
                stat = inner.enter_context(nc.sbuf_tensor("final_stat", [P, 2 * TT], F32))
                with nc.Block("load_final_g") as block:
                    @block.sync
                    def _(sp):
                        sp.dma_start(vec[:, 4, :], over_partitions(A["final_g"], D)).then_inc(c.loaded.sem, 16)
                        sp.wait_ge(c.loaded.sem, c.loaded.at(1))
                c.loaded.passed(1)
                rms_rows(c, "rms_final", lambda i: c.x[:, i, :], lambda i: h[:, i, :], lambda i: h[:, i, :], stat, TT, D,
                         RMS_EPS, lambda dve, i: c.dve(dve, nc.vector.tensor_tensor(h[:, i, :], h[:, i, :], vec[:, 4, :], ALU.mult)))

                def modulated(dve, t):
                    c.dve(dve, nc.vector.scalar_tensor_tensor(out=h[:, t, :], in0=vec[:, 2, :], scalar=1.0, in1=c.x[:, t, :],
                                                              op0=ALU.add, op1=ALU.mult))
                    nc.vector.tensor_tensor(h[:, t, :], h[:, t, :], vec[:, 3, :], ALU.add)

                layer_norm(c, "embedding_norm", lambda t: h[:, t, :], lambda t: c.x[:, t, :],
                           [(vec[:, 0, :], A["emb_ln_g_2"]), (vec[:, 1, :], A["emb_ln_b_2"]),
                            (vec[:, 2, :], part(1)), (vec[:, 3, :], part(0))], modulated)
            with nc.sbuf_tensor("latent_stages", [P, 15744], F32, side="right") as latent:
                w_a = latent[:, 0:DT * MLA_IN].rearrange("p (k n) -> p k n", k=DT)
                w_in = A["w_in_2"].rearrange("a (k p) n -> p (a k) n", p=P)
                turned_parts(c, "turn_h", lambda t, f: h[:, t, f * P:(f + 1) * P], hT, DT,
                             loads=[(w_a, w_in[:, :, 0:MLA_IN], None)])
                latent_attention(c, A, hT, h, latent[:])
            raw_free = ExitStack()
            raw = raw_free.enter_context(nc.sbuf_tensor("rwkv_raw", [P, RWKV_IN // P * (SEQ + 1)], F32))
            rwkv_projection(c, A, hT, raw)
        c.far.close()
        ring = c.far.enter_context(nc.sbuf_tensor("rwkv_room", [P, RING * RSLOT], F32, side="right"))
        rwkv(c, A, raw, h, ring[:])
        raw_free.close()
        gates = ctx.enter_context(nc.sbuf_tensor("gates", [P, TT, TOPK], F32))
        slots = ctx.enter_context(nc.sbuf_tensor("token_slots", [P, TT, TOPK], I32))
        plan = ctx.enter_context(nc.sbuf_tensor("extra_plan", [1, 2 + EXTRA], I32))
        with ExitStack() as inner:
            h_rows, slot_tok = mixed(c, A, h, part, inner, gates, slots, plan)
        experts(c, A, h, h_rows, slot_tok, bias_rows, plan, Y)
        combine(c, A, h, Y, gates, slots, part, out)


def latent_attention(c, A, hT, mix, flat):
    nc = c.nc
    w = Carve(flat)
    w_a = w(DT, MLA_IN)
    uq = w(2, NH * QK)
    uk = w(NH * NOPE)
    uv = w(NH * VD)
    lat = w(TT, MLA_IN)
    latn = w(TT, QL + KVL)
    latT = w(3, SEQ)
    q_tok = w(TT, NH, QK)
    v_tok = w(TT, NH * VD)
    with ExitStack() as ctx:
        def sb(name, shape, dt=F32):
            return ctx.enter_context(nc.sbuf_tensor(name, shape, dt))

        qT = sb("mla_qT", [QK, NH, SEQ])
        kT = sb("mla_kT", [QK, NH, SEQ])
        gcol = sb("lat_g", [P, 3])
        stat = sb("lat_stat", [P, 2 * TT])
        out_g = sb("mla_out_gain", [P, NH * VD])
        mask = sb("causal_bias", [P, SEQ])
        small = ExitStack()
        pos_i = small.enter_context(nc.sbuf_tensor("pos_i", [P, TT], I32))
        pos = small.enter_context(nc.sbuf_tensor("pos_f", [P, TT], F32))
        inv = small.enter_context(nc.sbuf_tensor("inv_freq_rows", [P, ROPE // 2], F32))
        ang = small.enter_context(nc.sbuf_tensor("angle", [P, 2, TT, ROPE // 2], F32))
        turns = small.enter_context(nc.sbuf_tensor("turns", [P, 2, TT, ROPE // 2], F32))
        turns_i = small.enter_context(nc.sbuf_tensor("turns_i", [P, 2, TT, ROPE // 2], I32))
        krot = small.enter_context(nc.sbuf_tensor("k_rotated", [P, TT, ROPE], F32))
        r4 = small.enter_context(nc.sbuf_tensor("rope_parts", [P, 4, NH, ROPE // 2], F32))
        k_tok = q_tok

        w_in = A["w_in_2"].rearrange("a (k p) n -> p (a k) n", p=P)
        with nc.sbuf_tensor("w_latent_parts", [P, 2, DT, MLA_IN], F32R, side="right") as w_p:
            projection(c, "project_latents", [(w_a, w_in[:, :, 0:MLA_IN], None)],
                       [dict(load=0, k=DT, lhsT=lambda k, p, t=t: hT[:, p, k, t * P:(t + 1) * P],
                             rhs=lambda k, p: w_p[:, p, k, :], out=lambda b: b[:, 0:MLA_IN], engine="dve",
                             evac=lambda b, t=t: nc.vector.tensor_copy(lat[:, t, :], b[:, 0:MLA_IN])) for t in range(TT)],
                       split=dict(raws=1, places=1, raw=lambda g: w_a, part=lambda p, g: w_p[:, p]), under_way=1)

        with nc.Block("rotary_tables") as block:

            @block.sync
            def _(sp):
                slow = dict(allow_slow_non_contiguous=True)
                sp.dma_start(pos_i[:], column(A["positions_2"].rearrange("a s -> (a s)"), TT), **slow).then_inc(c.loaded.sem, 16)
                sp.dma_start(inv[:], over_partitions(A["inv_freq"], ROPE // 2)).then_inc(c.loaded.sem, 16)
                sp.dma_start(gcol[:, 0:2], column(A["q_norm_g_2"].rearrange("a n -> (a n)"), 2), **slow).then_inc(c.loaded.sem, 16)
                sp.dma_start(gcol[:, 2:3], column(A["kv_norm_g_2"].rearrange("a n -> (a n)"), 1), **slow).then_inc(c.loaded.sem, 16)
                sp.dma_start(out_g[:], over_partitions(A["mla_out_g_2"].rearrange("a n -> (a n)"), NH * VD)).then_inc(c.loaded.sem, 16)
                sp.dma_start(uq, A["w_uq_2"].rearrange("a (k p) n -> p (a k) n", p=P)).then_inc(c.loaded.sem, 16)
                sp.dma_start(uk, A["w_uk_2"].rearrange("a k n -> (a k) n")).then_inc(c.loaded.sem, 16)
                sp.dma_start(uv, A["w_uv_2"].rearrange("a k n -> (a k) n")).then_inc(c.loaded.sem, 16)
                sp.wait_ge(c.loaded.sem, c.loaded.at(8))

            @block.gpsimd
            def _(pool):
                c.pool(pool, nc.gpsimd.memset(mask[:], 0.0))
                nc.gpsimd.affine_select(out=mask[:, SEQ - P:SEQ], in_=mask[:, SEQ - P:SEQ], compare_op=ALU.is_ge,
                                        fill=NEG, base=0, pattern=[[-1, P]], channel_multiplier=1)

            @block.vector
            def _(dve):
                pi = float(np.pi)
                limit = 3.1415925
                dve.wait_ge(c.loaded.sem, c.loaded.at(8))
                c.dve(dve, nc.vector.tensor_copy(pos[:], pos_i[:]))
                for t in range(TT):
                    last = nc.vector.tensor_scalar(ang[:, 0, t, :], inv[:], pos[:, t:t + 1], None, ALU.mult)
                c.dve(dve, last)
                c.dve(dve, nc.vector.tensor_scalar(turns[:, 0], ang[:, 0], 1.0 / (2 * pi), None, ALU.mult))
                c.dve(dve, nc.vector.tensor_copy(turns_i[:, 0], turns[:, 0]))
                c.dve(dve, nc.vector.tensor_copy(turns[:, 0], turns_i[:, 0]))
                for part in (-6.28125, -(2 * pi - 6.28125)):
                    c.dve(dve, nc.vector.scalar_tensor_tensor(out=ang[:, 0], in0=turns[:, 0], scalar=part, in1=ang[:, 0],
                                                              op0=ALU.mult, op1=ALU.add))
                c.dve(dve, nc.vector.tensor_scalar(ang[:, 1], ang[:, 0], pi / 2, None, ALU.add))
                for compare, turn in ((ALU.is_gt, -2 * pi), (ALU.is_lt, 2 * pi)):
                    edge = pi if compare == ALU.is_gt else -pi
                    c.dve(dve, nc.vector.tensor_scalar(turns[:], ang[:], edge, turn, compare, ALU.mult))
                    c.dve(dve, nc.vector.tensor_tensor(ang[:], ang[:], turns[:], ALU.add))
                nc.vector.tensor_scalar(ang[:], ang[:], limit, -limit, ALU.min, ALU.max).then_inc(c.dve_done.sem, 1)

            @block.scalar
            def _(act):
                act.wait_ge(c.dve_done.sem, c.dve_done.at(1))
                nc.scalar.activation(ang[:], ang[:], ACT.Sin).then_inc(c.act_done.sem, 1)

        c.loaded.passed(8)
        c.dve_done.passed(1)
        c.act_done.passed(1)

        rms_rows(c, "rms_q", lambda i: lat[:, i, 0:QL], lambda i: latn[:, i, 0:QL], lambda i: latn[:, i, 0:QL], stat, TT, QL, RMS_EPS)
        rms_rows(c, "rms_kv", lambda i: lat[:, i, QL:QL + KVL], lambda i: latn[:, i, QL:QL + KVL],
                 lambda i: latn[:, i, QL:QL + KVL], stat, TT, KVL, RMS_EPS)

        def scaled(who, f, dst, src):
            if who == "act":
                return nc.scalar.activation(dst, src, ACT.Copy, scale=gcol[:, f:f + 1])
            return nc.vector.tensor_scalar(dst, src, gcol[:, f:f + 1], None, ALU.mult)

        turned(c, "turn_latents", lambda t, f: latn[:, t, f * P:(f + 1) * P], lambda f: latT[:, f, :], 3, scaled)

        half = NH * QK // 2
        units = [dict(load=-1, k=2, lhsT=lambda k, t=t: latT[:, k, t * P:(t + 1) * P],
                      rhs=lambda k, n=n: uq[:, k, n * half:(n + 1) * half], out=lambda b: b[:, 0:half],
                      engine=("act", "dve")[n],
                      evac=(lambda b, t=t: nc.scalar.activation(q_tok[:, t, 0:NH // 2, :], b[:, 0:half].rearrange("p (h d) -> p h d", d=QK), ACT.Copy),
                            lambda b, t=t: nc.vector.tensor_copy(q_tok[:, t, NH // 2:NH, :], b[:, 0:half].rearrange("p (h d) -> p h d", d=QK)))[n])
                 for t in range(TT) for n in range(2)]
        projection(c, "queries", [], units)

        def rotate(dve, x, heads, t, dst=None):
            sin = ang[:, 0, t, :].unsqueeze(1).broadcast_to([P, heads, ROPE // 2])
            cos = ang[:, 1, t, :].unsqueeze(1).broadcast_to([P, heads, ROPE // 2])
            even, odd = x[:, :, 0:ROPE:2], x[:, :, 1:ROPE:2]
            for i, (a, b) in enumerate(((even, cos), (odd, sin), (even, sin), (odd, cos))):
                last = nc.vector.tensor_tensor(r4[:, i, 0:heads, :], a, b, ALU.mult)
            c.dve(dve, last)
            dst = x if dst is None else dst
            nc.vector.tensor_tensor(dst[:, :, 0:ROPE:2], r4[:, 0, 0:heads, :], r4[:, 1, 0:heads, :], ALU.subtract)
            c.dve(dve, nc.vector.tensor_tensor(dst[:, :, 1:ROPE:2], r4[:, 2, 0:heads, :], r4[:, 3, 0:heads, :], ALU.add))

        with nc.Block("rotate_queries") as block:

            @block.vector
            def _(dve):
                for t in range(TT):
                    rotate(dve, q_tok[:, t, :, NOPE:QK], NH, t)
                    rotate(dve, lat[:, t:t + 1, QL + KVL:MLA_IN], 1, t, krot[:, t:t + 1, :])

        def head_turn(name, dst):
            with nc.Block(name) as block:

                @block.tensor
                def _(pe):
                    for f in range(NH):
                        for t in range(TT):
                            last = nc.tensor.transpose(c.banks[0:QK, f, t * P:(t + 1) * P], q_tok[:, t, f, :], c.ident[:])
                        last.then_inc(c.products.sem, 1)

                @block.scalar
                def _(act):
                    for f in range(0, NH, 2):
                        act.wait_ge(c.products.sem, c.products.at(f + 1))
                        nc.scalar.activation(dst[:, f, :], c.banks[0:QK, f, :], ACT.Copy)

                @block.vector
                def _(dve):
                    for f in range(1, NH, 2):
                        dve.wait_ge(c.products.sem, c.products.at(f + 1))
                        nc.vector.tensor_copy(dst[:, f, :], c.banks[0:QK, f, :])

            c.products.passed(NH)

        head_turn("turn_queries", qT)
        units = []
        for t in range(TT):
            units.append(dict(load=-1, k=1, lhsT=lambda k, t=t: latT[:, 2, t * P:(t + 1) * P], rhs=lambda k: uk,
                              out=lambda b: b, engine="dve",
                              evac=lambda b, t=t: nc.vector.tensor_copy(k_tok[:, t, :, 0:NOPE], b.rearrange("p (h d) -> p h d", h=NH))))
            units.append(dict(load=-1, k=1, lhsT=lambda k, t=t: latT[:, 2, t * P:(t + 1) * P], rhs=lambda k: uv,
                              out=lambda b: b, engine="act",
                              evac=lambda b, t=t: nc.scalar.activation(v_tok[:, t, :], b, ACT.Copy)))
        projection(c, "keys_values", [], units)
        with nc.Block("shared_rotary_key") as block:

            @block.vector
            def _(dve):
                for t in range(TT):
                    nc.vector.tensor_copy(k_tok[:, t, :, NOPE:QK], krot[:, t, :].unsqueeze(1).broadcast_to([P, NH, ROPE]))

        head_turn("turn_keys", kT)
        small.close()

        def finish(h, t, product, rinv):
            return nc.vector.tensor_scalar(mix[:, t, h * VD:(h + 1) * VD], product, rinv, None, ALU.mult)

        attention(c, "causal_attention", NH, lambda h: qT[:, h, :], lambda h: kT[:, h, :],
                  lambda b, h: v_tok[:, b, h * VD:(h + 1) * VD], VD, QK ** -0.5, lambda h: mask[:], None, finish)

        W = NH * VD
        junk = Carve(flat)(TT, W)
        rms_rows(c, "rms_mla", lambda i: mix[:, i, 0:W], lambda i: mix[:, i, 0:W], lambda i: junk[:, i, :], stat, TT, W,
                 RMS_EPS, lambda dve, i: c.dve(dve, nc.vector.tensor_tensor(mix[:, i, 0:W], mix[:, i, 0:W], out_g[:], ALU.mult)))


def rwkv_projection(c, A, hT, raw):
    nc = c.nc
    tiles = RWKV_IN // P
    p = raw[:].rearrange("p (f s) -> p f s", f=tiles)
    w_in = A["w_in_2"].rearrange("a (k p) n -> p (a k) n", p=P)
    raws, places, groups = 4, 2, tiles // 2
    with ExitStack() as ctx:
        landing = ctx.enter_context(nc.sbuf_tensor("w_rwkv_landing", [P, raws, DT, 2 * P], F32, side="right"))
        parts = ctx.enter_context(nc.sbuf_tensor("w_rwkv_parts", [P, 2, places, DT, 2 * P], F32R, side="right"))
        loads = [(landing[:, g % raws], w_in[:, :, MLA_IN + g * 2 * P:MLA_IN + (g + 1) * 2 * P], None)
                 for g in range(groups)]
        units = [dict(load=f // 2, k=DT, lhsT=lambda k, q, f=f: parts[:, q, f // 2 % places, k, (f % 2) * P:(f % 2 + 1) * P],
                      rhs=lambda k, q: hT[:, q, k, :], out=lambda b: b, engine=("act", "dve")[f % 2],
                      evac=(lambda b, f=f: nc.scalar.activation(p[:, f, 1:SEQ + 1], b, ACT.Copy),
                            lambda b, f=f: nc.vector.tensor_copy(p[:, f, 1:SEQ + 1], b))[f % 2]) for f in range(tiles)]
        projection(c, "project_rwkv", loads, units,
                   split=dict(raws=raws, places=places, raw=lambda g: landing[:, g % raws],
                              part=lambda q, g: parts[:, q, g % places]))
    with ExitStack() as ctx:
        mu = ctx.enter_context(nc.sbuf_tensor("rwkv_mu_col", [P, tiles], F32))
        d = ctx.enter_context(nc.sbuf_tensor("rwkv_step", [P, 2, SEQ], F32))
        with nc.Block("token_shift") as block:

            @block.sync
            def _(sp):
                sp.dma_start(mu[:], column(A["rwkv_mu_2"].rearrange("a n -> (a n)"), tiles),
                             allow_slow_non_contiguous=True).then_inc(c.loaded.sem, 16)

            @block.gpsimd
            def _(pool):
                c.pool(pool, nc.gpsimd.memset(p[:, :, 0:1], 0.0))
                for f in range(tiles):
                    if f >= 2:
                        pool.wait_ge(c.dve_done.sem, c.dve_done.at(f - 1))
                    nc.gpsimd.tensor_tensor(d[:, f % 2, :], p[:, f, 0:SEQ], p[:, f, 1:SEQ + 1],
                                            ALU.subtract).then_inc(c.masks.sem, 1)

            @block.vector
            def _(dve):
                dve.wait_ge(c.loaded.sem, c.loaded.at(1))
                for f in range(tiles):
                    dve.wait_ge(c.masks.sem, c.masks.at(f + 1))
                    nc.vector.scalar_tensor_tensor(out=p[:, f, 1:SEQ + 1], in0=d[:, f % 2, :], scalar=mu[:, f:f + 1],
                                                   in1=p[:, f, 1:SEQ + 1], op0=ALU.mult, op1=ALU.add).then_inc(c.dve_done.sem, 1)

    c.loaded.passed(1)
    c.masks.passed(tiles)
    c.dve_done.passed(tiles)


def rwkv(c, A, raw, mix, flat):
    nc = c.nc
    tiles = RWKV_IN // P
    MID = P // 2 - 1
    p = raw[:].rearrange("p (f s) -> p f s", f=tiles)[:, :, 1:SEQ + 1]
    r, k, v = p[:, 0:RP, :], p[:, RP:2 * RP, :], p[:, 2 * RP:3 * RP, :]
    lora, gate_in = p[:, 3 * RP, :], p[:, 3 * RP + 1, :]
    w = Carve(flat)
    ar = w(RP, TT, 2, P)
    bT = w(RP, SEQ)
    kT = w(RP, SEQ)
    inverse = w(TT, RH, P)
    a = w(RP, SEQ)
    F = w(RP, SEQ)
    kk = w(RP, SEQ)
    e = w(RP, SEQ)
    with ExitStack() as ctx:
        def sb(name, shape, dt=F32):
            return ctx.enter_context(nc.sbuf_tensor(name, shape, dt))

        tok = sb("rwkv_tok", [P, 3, TT, RW])
        v_tok, b_tok, k_tok = tok[:, 0], tok[:, 1], tok[:, 2]
        into = sb("rwkv_into", [P, RP, TT])
        outof = sb("rwkv_outof", [P, RP, TT])
        bonus = sb("rwkv_bonus", [P, TT, RH])
        bd = sb("pair_blocks", [P, P])
        g2 = sb("rwkv_g2", [P, RW])
        with ExitStack() as inner:
            cols = inner.enter_context(nc.sbuf_tensor("rwkv_cols", [P, 6, RP], F32))
            w0, a0, k_k, k_a, r_k, omka = (cols[:, i, :] for i in range(6))
            wa2 = inner.enter_context(nc.sbuf_tensor("lora_w", [P, RW], F32))
            head_sum = inner.enter_context(nc.sbuf_tensor("pair_select", [P, 2], F32))

            with nc.Block("rwkv_gates") as block:

                @block.sync
                def _(sp):
                    for place, name in ((w0, "rwkv_w0_2"), (a0, "rwkv_a0_2"), (k_k, "rwkv_k_k_2"), (k_a, "rwkv_k_a_2")):
                        sp.dma_start(place, column(A[name].rearrange("a n -> (a n)"), RP),
                                     allow_slow_non_contiguous=True).then_inc(c.loaded.sem, 16)
                    sp.dma_start(r_k, column(A["rwkv_r_k_2"].rearrange("a h d -> (a h d)"), RP),
                                 allow_slow_non_contiguous=True).then_inc(c.loaded.sem, 16)
                    sp.dma_start(wa2[0:LORA_D, :], A["rwkv_w2_2"].rearrange("a k n -> (a k) n")).then_inc(c.loaded.sem, 16)
                    sp.dma_start(wa2[LORA_D:P, :], A["rwkv_a2_2"].rearrange("a k n -> (a k) n")).then_inc(c.loaded.sem, 16)
                    sp.dma_start(g2[:], A["rwkv_g2_2"].rearrange("a k n -> (a k) n")).then_inc(c.loaded.sem, 16)
                    sp.wait_ge(c.loaded.sem, c.loaded.at(8))

                @block.gpsimd
                def _(pool):
                    nc.gpsimd.memset(head_sum[:], 0.0)
                    c.pool(pool, nc.gpsimd.memset(bd[:], 0.0))
                    for j in range(2):
                        nc.gpsimd.memset(head_sum[j * 64:(j + 1) * 64, j:j + 1], 1.0)
                        nc.gpsimd.memset(bd[j * 64:(j + 1) * 64, j * 64:(j + 1) * 64], 1.0)

                @block.scalar
                def _(act):
                    nc.scalar.activation(lora[0:LORA_D, :], lora[0:LORA_D, :], ACT.Tanh).then_inc(c.act_done.sem, 1)
                    nc.scalar.activation(gate_in, gate_in, ACT.Sigmoid)
                    act.wait_ge(c.loaded.sem, c.loaded.at(8))
                    for f in range(RP):
                        act.wait_ge(c.products.sem, c.products.at(f + 1))
                        nc.scalar.activation(e[:, f, :], c.banks[:, f, :], ACT.Sigmoid, bias=w0[:, f:f + 1])
                        nc.scalar.activation(a[:, f, :], c.banks[:, 4 + f, :], ACT.Sigmoid, bias=a0[:, f:f + 1])

                @block.tensor
                def _(pe):
                    pe.wait_ge(c.loaded.sem, c.loaded.at(8))
                    pe.wait_ge(c.act_done.sem, c.act_done.at(1))
                    for f in range(RP):
                        nc.tensor.matmul(c.banks[:, f, :], wa2[0:LORA_D, f * P:(f + 1) * P], lora[0:LORA_D, :], start=True, stop=True)
                        nc.tensor.matmul(c.banks[:, 4 + f, :], wa2[LORA_D:P, f * P:(f + 1) * P], lora[LORA_D:P, :],
                                         start=True, stop=True).then_inc(c.products.sem, 1)

                @block.vector
                def _(dve):
                    dve.wait_ge(c.loaded.sem, c.loaded.at(8))
                    nc.vector.tensor_scalar(omka, k_a, -1.0, 1.0, ALU.mult, ALU.add)
                    for f in range(RP):
                        nc.vector.tensor_scalar(kk[:, f, :], k[:, f, :], k_k[:, f:f + 1], None, ALU.mult)

            c.loaded.passed(8)
            c.act_done.passed(1)
            c.products.passed(RP)

            by_tile = lambda x: x.rearrange("p f (t s) -> p (f t) s", t=TT)
            all_of = lambda x: x.rearrange("p f s -> p (f s)")
            decay_scale = -float(np.exp(-0.5))
            kk2 = ar.rearrange("p f t k s -> p (f t k s)")[:, 0:RP * SEQ]
            kk2f = kk2.rearrange("p (f s) -> p f s", f=RP)
            with nc.Block("rwkv_decays") as block:

                @block.tensor
                def _(pe):
                    pe.wait_ge(c.dve_done.sem, c.dve_done.at(1))
                    for f in range(RP):
                        last = nc.tensor.matmul(c.banks[:, f, :], bd[:], kk2f[:, f, :], start=True, stop=True)
                    last.then_inc(c.products.sem, 1)
                    pe.wait_ge(c.dve_done.sem, c.dve_done.at(2))
                    for t in range(TT):
                        for f in range(RP):
                            last = nc.tensor.matmul(c.banks[:, 4, t * RH + 2 * f:t * RH + 2 * f + 2],
                                                    bT[:, f, t * P:(t + 1) * P], head_sum[:], start=True, stop=True)
                    last.then_inc(c.products.sem, 1)

                @block.scalar
                def _(act):
                    act.wait_ge(c.products.sem, c.products.at(1))
                    for f in range(RP):
                        last = nc.scalar.activation(kT[:, f, :], c.banks[:, f, :], ACT.Sqrt)
                    last.then_inc(c.act_done.sem, 1)

                @block.vector
                def _(dve):
                    nc.vector.tensor_tensor(kk2, all_of(kk), all_of(kk), ALU.mult).then_inc(c.dve_done.sem, 1)
                    c.dve(dve, nc.vector.tensor_scalar(all_of(e), all_of(e), decay_scale, None, ALU.mult))
                    for f in range(RP):
                        nc.vector.tensor_scalar(inverse.rearrange("p t h s -> p (t h s)")[:, f * SEQ:(f + 1) * SEQ], a[:, f, :],
                                                k_a[:, f:f + 1], omka[:, f:f + 1], ALU.mult, ALU.add)
                        for t in range(TT):
                            s = slice(t * P, (t + 1) * P)
                            last = nc.vector.tensor_tensor_scan(F[:, f, s], c.ones[:], e[:, f, s], 0.0, ALU.mult, ALU.add)
                    c.dve(dve, last)
                    c.dve(dve, nc.vector.tensor_tensor(k, k, inverse.rearrange("p t h s -> p (t h s)")[:, 0:RP * SEQ].rearrange(
                        "p (f s) -> p f s", f=RP), ALU.mult))
                    for f in range(RP):
                        last = nc.vector.scalar_tensor_tensor(out=bT[:, f, :], in0=r[:, f, :], scalar=r_k[:, f:f + 1],
                                                              in1=k[:, f, :], op0=ALU.mult, op1=ALU.mult)
                    last.then_inc(c.dve_done.sem, 1)
                    dve.wait_ge(c.act_done.sem, c.act_done.at(1))
                    c.dve(dve, nc.vector.tensor_scalar(all_of(kT), all_of(kT), 1e-12, None, ALU.max))
                    c.dve(dve, nc.vector.reciprocal(all_of(kT), all_of(kT)))
                    c.dve(dve, nc.vector.tensor_tensor(all_of(kk), all_of(kk), all_of(kT), ALU.mult))
                    dve.wait_ge(c.products.sem, c.products.at(2))
                    nc.vector.tensor_copy(bonus[:].rearrange("p t h -> p (t h)"), c.banks[:, 4, 0:TT * RH])

            c.products.passed(2)
            c.dve_done.passed(2)
            c.act_done.passed(1)

            Fm = by_tile(F)
            ends = into[:].rearrange("p f t -> p (f t)")
            with nc.Block("rwkv_scaled") as block:

                @block.vector
                def _(dve):
                    nc.vector.tensor_copy(into[:].rearrange("p f t -> p (f t)"), Fm[:, :, MID])
                    c.dve(dve, nc.vector.tensor_tensor(outof[:].rearrange("p f t -> p (f t)"), Fm[:, :, P - 1], Fm[:, :, MID],
                                                       ALU.subtract))
                    c.dve(dve, nc.vector.tensor_tensor(Fm, Fm, ends.unsqueeze(2).broadcast_to([P, RP * TT, P]), ALU.subtract))
                    nc.vector.tensor_tensor(all_of(e), all_of(F), all_of(e), ALU.subtract).then_inc(c.dve_done.sem, 1)
                    dve.wait_ge(c.act_done.sem, c.act_done.at(2))
                    for f in range(RP):
                        nc.vector.scalar_tensor_tensor(out=ar[:, f, :, 0, :], in0=kk[:, f, :].rearrange("p (t s) -> p t s", t=TT),
                                                       scalar=-1.0, in1=e[:, f, :].rearrange("p (t s) -> p t s", t=TT),
                                                       op0=ALU.mult, op1=ALU.mult)
                        nc.vector.tensor_tensor(ar[:, f, :, 1, :], r[:, f, :].rearrange("p (t s) -> p t s", t=TT),
                                                ar[:, f, :, 1, :], ALU.mult)
                    c.dve(dve, nc.vector.tensor_tensor(all_of(bT), all_of(kk), all_of(a), ALU.mult))
                    dve.wait_ge(c.act_done.sem, c.act_done.at(3))
                    nc.vector.tensor_tensor(all_of(bT), all_of(bT), all_of(F), ALU.mult)
                    c.dve(dve, nc.vector.tensor_tensor(kT, k, F, ALU.mult))

                @block.scalar
                def _(act):
                    act.wait_ge(c.dve_done.sem, c.dve_done.at(1))
                    nc.scalar.activation(all_of(e), all_of(e), ACT.Exp).then_inc(c.act_done.sem, 1)
                    for f in range(RP):
                        last = nc.scalar.activation(ar[:, f, :, 1, :], F[:, f, :].rearrange("p (t s) -> p t s", t=TT), ACT.Exp)
                    last.then_inc(c.act_done.sem, 1)
                    act.wait_ge(c.act_done.sem, c.act_done.at(2))
                    nc.scalar.activation(all_of(F), all_of(F), ACT.Exp, scale=-1.0).then_inc(c.act_done.sem, 1)
                    nc.scalar.activation(into[:], into[:], ACT.Exp)
                    nc.scalar.activation(outof[:], outof[:], ACT.Exp)

            c.dve_done.passed(1)
            c.act_done.passed(3)

            def token_rows(name, x, dst):
                turned(c, name, lambda s, f: x[:, s, f * P:(f + 1) * P], lambda f: dst[:, f, :], TT, copied(c))

            token_rows("turn_values", v, v_tok)
            token_rows("turn_b", bT, b_tok)
            token_rows("turn_k", kT, k_tok)

        free = Carve(raw[:, 0:3 * RP * (SEQ + 1)])
        w2 = Carve(flat)
        w2.at = 4 * RP * SEQ + TT * RH * P
        rwkv_inverse(c, ar, bT, inverse, free, w2)
        free = Carve(raw[:, 0:3 * RP * (SEQ + 1)])
        w2 = Carve(flat)
        w2.at = 4 * RP * SEQ + TT * RH * P
        o_tok = w2(TT, RW)
        rwkv_scan(c, ar, bT, kT, inverse, v_tok, b_tok, k_tok, into, outof, bd, o_tok, free, w2)

        square = w2(TT * RH, 64)
        gain = w2(2, RW)
        stat = sb("gn_stat", [P, 2, TT * RH])
        with nc.Block("rwkv_gate") as block:

            @block.sync
            def _(sp):
                sp.dma_start(gain[:, 0, :], over_partitions(A["rwkv_gn_g_2"].rearrange("a n -> (a n)"), RW)).then_inc(c.loaded.sem, 16)
                sp.dma_start(gain[:, 1, :], over_partitions(A["rwkv_gn_b_2"].rearrange("a n -> (a n)"), RW)).then_inc(c.loaded.sem, 16)
                sp.wait_ge(c.loaded.sem, c.loaded.at(2))

            @block.tensor
            def _(pe):
                for t in range(TT):
                    last = nc.tensor.matmul(c.banks[:, t, :], gate_in[:, t * P:(t + 1) * P], g2[:], start=True, stop=True)

        c.loaded.passed(2)

        def gated(dve):
            place = mix[:, :, D - RW:D]
            heads = lambda x: x.rearrange("p t (h d) -> p (t h) d", h=RH)
            c.dve(dve, nc.vector.tensor_tensor(o_tok, o_tok, spread(gain[:, 0, :], TT), ALU.mult))
            c.dve(dve, nc.vector.tensor_tensor(o_tok, o_tok, spread(gain[:, 1, :], TT), ALU.add))
            c.dve(dve, nc.vector.tensor_tensor(square, heads(v_tok), bonus[:].rearrange("p t h -> p (t h)").unsqueeze(2)
                                               .broadcast_to([P, TT * RH, 64]), ALU.mult))
            c.dve(dve, nc.vector.tensor_tensor(heads(o_tok), heads(o_tok), square, ALU.add))
            nc.vector.tensor_tensor(place, o_tok, c.banks[:, 0:TT, :], ALU.mult)

        head_norm(c, "rwkv_norm", o_tok.rearrange("p t (h d) -> p (t h) d", h=RH), square, stat[:], TT * RH, 64, GN_EPS,
                  True, gated)


def rwkv_inverse(c, ar, bT, inverse, free, work):
    nc = c.nc
    levels = [2 ** i for i in range(1, 7)]
    L = len(levels)
    upper_of = free(L + 1, P)
    lower1 = free(P)
    nt = free(2, 4, P)
    n1 = free(2, 4, P)
    ntm = free(2, 2, 4, P)
    X = free(2, 4, P)
    y = work(2, 4, P)
    rounds = TT
    with nc.Block("join_masks") as block:

        @block.gpsimd
        def _(pool):
            c.pool(pool, nc.gpsimd.memset(upper_of, 1.0))
            for i in range(L + 1):
                m = 2 ** i
                blocks = P // (2 * m)
                view = upper_of[:, i, :].rearrange("p (b h m) -> p b h m", b=blocks, h=2)
                c.pool(pool, nc.gpsimd.affine_select(out=view, in_=view, compare_op=ALU.is_ge, fill=0.0, base=0,
                                                     pattern=[[-2 * m, blocks], [0, 2], [0, m]], channel_multiplier=1))
                c.pool(pool, nc.gpsimd.affine_select(out=view, in_=view, compare_op=ALU.is_ge, fill=0.0, base=m - 1,
                                                     pattern=[[2 * m, blocks], [0, 2], [0, m]], channel_multiplier=-1))
                c.pool(pool, nc.gpsimd.affine_select(out=view, in_=view, compare_op=ALU.is_gt, fill=0.0, base=0,
                                                     pattern=[[0, blocks], [1, 2], [0, m]], channel_multiplier=0))

        @block.tensor
        def _(pe):
            pe.wait_ge(c.pool.sem, c.pool.n)
            nc.tensor.transpose(c.banks[:, 0, 0:P], upper_of[:, 0, :], c.ident[:]).then_inc(c.products.sem, 1)

        @block.vector
        def _(dve):
            dve.wait_ge(c.products.sem, c.products.at(1))
            nc.vector.tensor_copy(lower1, c.banks[:, 0, 0:P])

    c.products.passed(1)

    n_ready, y_ready, x_ready = c.products, c.att_turned, c.att_out
    taken, nt_ready, y_copied, x_updated, joined = c.dve_done, c.att_masked, c.act_done, c.att_max, c.masks
    four = lambda x: x.unsqueeze(1).broadcast_to([P, 4, P])
    with nc.Block("rwkv_inverse") as block:

        @block.tensor
        def _(pe):
            for g in range(rounds):
                for q in range(2):
                    i = 2 * g + q
                    if i >= 1:
                        pe.wait_ge(taken.sem, taken.at(i))
                    for b in range(2):
                        for j in range(2):
                            rows, f = slice(64 * j, 64 * j + 64), 2 * q + b
                            A_, B_ = ar[rows, f, g, 0, :], bT[rows, f, g * P:(g + 1) * P]
                            nc.tensor.matmul(c.banks[:, 6 + j, b * P:(b + 1) * P], B_, A_, start=True, stop=True)
                            last = nc.tensor.matmul(c.banks[:, 6 + j, (2 + b) * P:(3 + b) * P], A_, B_, start=True, stop=True)
                    last.then_inc(n_ready.sem, 1)
                for l in range(L):
                    for q in range(2):
                        i = (g * L + l) * 2 + q
                        pe.wait_ge(joined.sem, joined.at(i + 1))
                        pe.wait_ge(x_updated.sem, x_updated.at((g * (L + 1) + l) * 2 + q + 1))
                        for h in range(4):
                            last = nc.tensor.matmul(c.banks[:, 3 * q, h * P:(h + 1) * P], ntm[:, l % 2, q, h, :], X[:, q, h, :],
                                                    start=True, stop=True)
                        last.then_inc(y_ready.sem, 1)
                    for q in range(2):
                        i = (g * L + l) * 2 + q
                        pe.wait_ge(y_copied.sem, y_copied.at(i + 1))
                        for h in range(4 if l < L - 1 else 0):
                            XT = inverse[:, g, 4 * q + h, :]
                            nc.tensor.matmul(c.banks[:, 3 * q + 1, h * P:(h + 1) * P], XT, y[:, q, h, :], start=True, stop=True)
                        for h in range(4):
                            XT = inverse[:, g, 4 * q + h, :]
                            last = nc.tensor.matmul(c.banks[:, 3 * q + 2, h * P:(h + 1) * P], y[:, q, h, :], XT,
                                                    start=True, stop=True)
                        last.then_inc(x_ready.sem, 1)

        @block.scalar
        def _(act):
            for i in range(rounds * L * 2):
                act.wait_ge(y_ready.sem, y_ready.at(i + 1))
                nc.scalar.activation(y[:, i % 2], c.banks[:, 3 * (i % 2), :].rearrange("p (h s) -> p h s", h=4),
                                     ACT.Copy).then_inc(y_copied.sem, 1)

        @block.gpsimd
        def _(pool):
            for g in range(rounds):
                for l in range(L):
                    for q in range(2):
                        i = (g * L + l) * 2 + q
                        pool.wait_ge(nt_ready.sem, nt_ready.at(2 * g + q + 1))
                        if i >= 4:
                            pool.wait_ge(y_ready.sem, y_ready.at(i - 3))
                        nc.gpsimd.tensor_tensor(ntm[:, l % 2, q], nt[:, q], four(upper_of[:, l + 1, :]), ALU.mult).then_inc(joined.sem, 1)

        @block.vector
        def _(dve):
            for g in range(rounds):
                for q in range(2):
                    i = 2 * g + q
                    XT = inverse[:, g, 4 * q:4 * q + 4, :]
                    dve.wait_ge(n_ready.sem, n_ready.at(i + 1))
                    if g >= 1:
                        dve.wait_ge(joined.sem, joined.at(((g - 1) * L + L - 1) * 2 + q + 1))
                    for b in range(2):
                        nc.vector.tensor_tensor(n1[:, q, 2 * b:2 * b + 2, :], c.banks[:, 6:8, (2 + b) * P:(3 + b) * P],
                                                lower1.unsqueeze(1).broadcast_to([P, 2, P]), ALU.mult)
                        last = nc.vector.tensor_tensor(nt[:, q, 2 * b:2 * b + 2, :], c.banks[:, 6:8, b * P:(b + 1) * P],
                                                       c.upper_strict[:].unsqueeze(1).broadcast_to([P, 2, P]), ALU.mult)
                    last.then_inc(nt_ready.sem, 1)
                    dve.wait_ge(nt_ready.sem, nt_ready.at(i + 1))
                    nc.vector.tensor_tensor(X[:, q], n1[:, q], four(c.ident[:]), ALU.add).then_inc(taken.sem, 1)
                    c.dve(dve, nc.vector.tensor_tensor(XT, nt[:, q], four(upper_of[:, 0, :]), ALU.mult))
                    nc.vector.tensor_tensor(XT, XT, four(c.ident[:]), ALU.add).then_inc(x_updated.sem, 1)
                for l in range(L):
                    for q in range(2):
                        i = (g * L + l) * 2 + q
                        XT = inverse[:, g, 4 * q:4 * q + 4, :]
                        bank = lambda b: c.banks[:, b, :].rearrange("p (h s) -> p h s", h=4)
                        dve.wait_ge(x_ready.sem, x_ready.at(i + 1))
                        if l < L - 1:
                            nc.vector.tensor_tensor(X[:, q], X[:, q], bank(3 * q + 1), ALU.add)
                        nc.vector.tensor_tensor(XT, XT, bank(3 * q + 2), ALU.add).then_inc(x_updated.sem, 1)

    n_ready.passed(2 * rounds)
    taken.passed(2 * rounds)
    nt_ready.passed(2 * rounds)
    x_updated.passed(2 * rounds * (L + 1))
    for signal in (y_ready, x_ready, y_copied, joined):
        signal.passed(2 * rounds * L)


def rwkv_scan(c, ar, bT, kT, inverse, v_tok, b_tok, k_tok, into, outof, bd, o_tok, free, work):
    nc = c.nc
    mats = free(2, 3, 2, RP * P)
    rhs = work(RW)
    u = work(RW)
    state = work(2, RP, P)
    mats_ready, masked, rhs_ready, act_done = c.products, c.att_masked, c.att_turned, c.act_done
    u_ready, u_copied, carried, s_ready, o_ready = c.att_out, c.dve_done, c.att_max, c.masks, c.extra
    with nc.Block("rwkv_scan") as block:

        @block.gpsimd
        def _(pool):
            nc.gpsimd.memset(state[:, 0], 0.0).then_inc(c.pool_ready.sem, 1)

        @block.tensor
        def _(pe):
            def products(t):
                s = slice(t * P, (t + 1) * P)
                if t >= 1:
                    pe.wait_ge(masked.sem, masked.at(t))
                for f in range(RP):
                    for j in range(2):
                        rows = slice(64 * j, 64 * j + 64)
                        both = ar[rows, f, t, :, :].rearrange("p k s -> p (k s)")
                        nc.tensor.matmul(c.banks[:, 2 * j + f // 2, (f % 2) * 2 * P:(f % 2 + 1) * 2 * P], kT[rows, f, s], both,
                                         start=True, stop=True)
                        last = nc.tensor.matmul(c.banks[:, 4 + j, f * P:(f + 1) * P], bT[rows, f, s], ar[rows, f, t, 1, :],
                                                start=True, stop=True)
                last.then_inc(mats_ready.sem, 1)

            products(0)
            for t in range(TT):
                heads = [(2 * f + j, f, j) for f in range(RP) for j in range(2)]
                mat = lambda kind, f, j: mats[:, t % 2, kind, j, f * P:(f + 1) * P]
                S = lambda f, j: state[:, t % 2, f, j * 64:(j + 1) * 64]
                pe.wait_ge(masked.sem, masked.at(t + 1))
                pe.wait_ge(carried.sem, carried.at(2 * t + 1))
                if t >= 1:
                    pe.wait_ge(act_done.sem, act_done.at(2 * t))
                for h, f, j in heads:
                    out = c.banks[:, 6, h * 64:(h + 1) * 64]
                    nc.tensor.matmul(out, ar[:, f, t, 0, :], S(f, j), start=True, stop=False)
                    last = nc.tensor.matmul(out, mat(0, f, j), v_tok[:, t, h * 64:(h + 1) * 64], start=False, stop=True)
                last.then_inc(rhs_ready.sem, 1)
                if t + 1 < TT:
                    products(t + 1)
                pe.wait_ge(act_done.sem, act_done.at(2 * t + 1))
                if t >= 1:
                    pe.wait_ge(carried.sem, carried.at(2 * t))
                for h, f, j in heads:
                    last = nc.tensor.matmul(c.banks[:, 7, h * 64:(h + 1) * 64], inverse[:, t, h, :], rhs[:, h * 64:(h + 1) * 64],
                                            start=True, stop=True)
                last.then_inc(u_ready.sem, 1)
                pe.wait_ge(u_copied.sem, u_copied.at(t + 1))
                for f in range(RP):
                    out, s = c.banks[:, 7, f * P:(f + 1) * P], slice(f * P, (f + 1) * P)
                    nc.tensor.matmul(out, b_tok[:, t, s], u[:, s], start=True, stop=False)
                    last = nc.tensor.matmul(out, k_tok[:, t, s], v_tok[:, t, s], start=False, stop=True)
                last.then_inc(s_ready.sem, 1)
                for h, f, j in heads:
                    out = c.banks[:, 6, h * 64:(h + 1) * 64]
                    nc.tensor.matmul(out, ar[:, f, t, 1, :], S(f, j), start=True, stop=False)
                    nc.tensor.matmul(out, mat(1, f, j), v_tok[:, t, h * 64:(h + 1) * 64], start=False, stop=False)
                    last = nc.tensor.matmul(out, mat(2, f, j), u[:, h * 64:(h + 1) * 64], start=False, stop=True)
                last.then_inc(o_ready.sem, 1)

        @block.scalar
        def _(act):
            for t in range(TT):
                act.wait_ge(rhs_ready.sem, rhs_ready.at(t + 1))
                nc.scalar.activation(rhs, c.banks[:, 6, :], ACT.Copy).then_inc(act_done.sem, 1)
                act.wait_ge(o_ready.sem, o_ready.at(t + 1))
                nc.scalar.activation(o_tok[:, t, :], c.banks[:, 6, :], ACT.Copy).then_inc(act_done.sem, 1)

        @block.vector
        def _(dve):
            def mask(t):
                dve.wait_ge(mats_ready.sem, mats_ready.at(t + 1))
                if t >= 2:
                    dve.wait_ge(o_ready.sem, o_ready.at(t - 1))
                for j in range(2):
                    four = lambda m: m[:].unsqueeze(1).broadcast_to([P, RP, P])
                    pairs = c.banks[:, 2 * j:2 * j + 2, :].rearrange("p b (i k s) -> p (b i) k s", i=2, k=2)
                    place = lambda kind: mats[:, t % 2, kind, j, :].rearrange("p (f s) -> p f s", f=RP)
                    nc.vector.tensor_tensor(place(0), pairs[:, :, 0, :], four(c.upper_strict), ALU.mult)
                    nc.vector.tensor_tensor(place(1), pairs[:, :, 1, :], four(c.upper), ALU.mult)
                    last = nc.vector.tensor_tensor(place(2), c.banks[:, 4 + j, :].rearrange("p (f s) -> p f s", f=RP),
                                                   four(c.upper), ALU.mult)
                last.then_inc(masked.sem, 1)

            along = lambda x, t: x[:, :, t:t + 1].broadcast_to([P, RP, P])
            dve.wait_ge(c.pool_ready.sem, c.pool_ready.at(1))
            mask(0)
            for t in range(TT):
                cur, nxt = state[:, t % 2], state[:, (t + 1) % 2]
                nc.vector.tensor_tensor(cur, cur, along(into, t), ALU.mult).then_inc(carried.sem, 1)
                if t + 1 < TT:
                    mask(t + 1)
                dve.wait_ge(u_ready.sem, u_ready.at(t + 1))
                if t >= 1:
                    dve.wait_ge(o_ready.sem, o_ready.at(t))
                nc.vector.tensor_copy(u, c.banks[:, 7, :]).then_inc(u_copied.sem, 1)
                dve.wait_ge(s_ready.sem, s_ready.at(t + 1))
                c.dve(dve, nc.vector.tensor_tensor(nxt, c.banks[:, 7, :].rearrange("p (f s) -> p f s", f=RP),
                                                   bd[:].unsqueeze(1).broadcast_to([P, RP, P]), ALU.mult))
                c.dve(dve, nc.vector.tensor_tensor(nxt, nxt, cur, ALU.add))
                nc.vector.tensor_tensor(nxt, nxt, along(outof, t), ALU.mult).then_inc(carried.sem, 1)
                dve.wait_ge(carried.sem, carried.at(2 * t + 2))

    c.pool_ready.passed(1)
    act_done.passed(2 * TT)
    carried.passed(2 * TT)
    for signal in (mats_ready, masked, rhs_ready, u_ready, u_copied, s_ready, o_ready):
        signal.passed(TT)


def mixed(c, A, h, part, ctx, gates, slots, plan):
    nc = c.nc

    def sb(name, shape, dt=F32):
        return ctx.enter_context(nc.sbuf_tensor(name, shape, dt))

    h_rows = nc.dram_tensor("h_rows", [SEQ, D], F32).ap()
    slot_tok = nc.dram_tensor("slot_tokens", [SLOTS + CAP, 1], I32).ap()
    vec = sb("mix_vectors", [P, 5, D])
    with nc.Block("load_gate_1") as block:
        @block.sync
        def _(sp):
            sp.dma_start(vec[:, 4, :], over_partitions(part(2), D)).then_inc(c.loaded.sem, 16)
            sp.wait_ge(c.loaded.sem, c.loaded.at(1))
    c.loaded.passed(1)
    out_projection(c, "project_mix", A["w_o_2"].rearrange("a k n -> (a k) n"), h, lambda t, n, b:
                   nc.vector.scalar_tensor_tensor(out=h[:, t, n * 512:(n + 1) * 512], in0=vec[:, 4, n * 512:(n + 1) * 512],
                                                  scalar=1.0, in1=b, op0=ALU.add, op1=ALU.mult))

    def residual(dve):
        for t in range(TT):
            last = nc.vector.scalar_tensor_tensor(out=h[:, t, :], in0=c.x[:, t, :], scalar=ALPHA, in1=h[:, t, :],
                                                  op0=ALU.mult, op1=ALU.add)
        c.dve(dve, last)

    def modulated(dve, t):
        c.dve(dve, nc.vector.scalar_tensor_tensor(out=h[:, t, :], in0=vec[:, 2, :], scalar=1.0, in1=c.x[:, t, :],
                                                  op0=ALU.add, op1=ALU.mult))
        nc.vector.tensor_tensor(h[:, t, :], h[:, t, :], vec[:, 3, :], ALU.add)

    layer_norm(c, "norm_1", lambda t: h[:, t, :], lambda t: c.x[:, t, :],
               [(vec[:, 0, :], A["ln1_g_2"].rearrange("a n -> (a n)")), (vec[:, 1, :], A["ln1_b_2"].rearrange("a n -> (a n)")),
                (vec[:, 2, :], part(4)), (vec[:, 3, :], part(3))], modulated, residual)
    c.raw = c.far.enter_context(nc.sbuf_tensor("expert_weights", [P, RAW, RSLOT], F32, side="right"))
    hT = sb("hT2", [P, DT, SEQ])
    turned(c, "turn_h2", lambda t, f: h[:, t, f * P:(f + 1) * P], lambda f: hT[:, f, :], DT, copied(c))

    rw = sb("router_w", [P, DT, E])
    rb = sb("router_b", [P, E])
    logits = sb("logits", [P, TT, E])
    top = sb("top_values", [P, TT, 8])
    top_i = sb("top_indices", [P, TT, 8], U32)
    top_f = sb("top_index_f", [P, TT, 8])
    neg = sb("neg_top", [P, TT])
    total = sb("gate_total", [P, TT])
    e_int = sb("expert_ids_i", [P, E], I32)
    e_id = sb("expert_ids", [P, E])
    hot = sb("one_hot", [P, TT, TOPK, E])
    member = sb("member", [P, TT, E])
    rank = sb("rank", [P, TT, E])
    count = sb("expert_count", [P, E])
    extra = sb("extra_blocks", [P, 2, E])
    cum = sb("extra_cum", [P, E])
    first = sb("extra_first", [P, E])
    over = sb("over_capacity", [P, TT, E])
    dest = sb("dest", [P, TT, TOPK])
    token_id = sb("token_id", [P, TT], I32)
    blk_i = sb("block_ids_i", [1, EXTRA], I32)
    blk = sb("block_ids", [1, EXTRA])
    before_blk = sb("experts_before", [1, EXTRA, E])
    plan_f = sb("plan_f", [1, 2 + EXTRA])
    zeros = sb("zero_ids", [SLOTS // CAP + 1, CAP], I32)
    with nc.Block("router") as block:

        @block.sync
        def _(sp):
            sp.dma_start(rw[:], A["router_w_2"].rearrange("a (k p) e -> p (a k) e", p=P)).then_inc(c.loaded.sem, 16)
            sp.dma_start(rb[:], over_partitions(A["router_b_2"].rearrange("a n -> (a n)"), E)).then_inc(c.loaded.sem, 16)
            sp.dma_start(h_rows.rearrange("(t p) d -> p t d", p=P), h[:]).then_inc(c.stored.sem, 16)
            sp.wait_ge(c.pool_ready.sem, c.pool_ready.at(1))
            sp.dma_start(slot_tok.rearrange("(b s) o -> b (s o)", s=CAP), zeros[:]).then_inc(c.stored.sem, 16)
            for ch in range(RAW):
                load_expert_chunk(c, A, sp, 0, ch)
            sp.wait_ge(c.stored.sem, c.stored.at(2))

        @block.gpsimd
        def _(pool):
            nc.gpsimd.memset(zeros[:], 0)
            nc.gpsimd.iota(token_id[:], pattern=[[P, TT]], base=0, channel_multiplier=1)
            nc.gpsimd.iota(blk_i[:], pattern=[[1, EXTRA]], base=0, channel_multiplier=0)
            nc.gpsimd.iota(e_int[:], pattern=[[1, E]], base=0, channel_multiplier=0).then_inc(c.pool_ready.sem, 1)

        @block.tensor
        def _(pe):
            pe.wait_ge(c.loaded.sem, c.loaded.at(2))
            for t in range(TT):
                for k in range(DT):
                    last = nc.tensor.matmul(c.banks[:, 0, t * E:(t + 1) * E], hT[:, k, t * P:(t + 1) * P], rw[:, k, :],
                                            start=(k == 0), stop=(k == DT - 1))
            last.then_inc(c.products.sem, 1)
            pe.wait_ge(c.dve_done.sem, c.dve_done.at(2))
            for t in range(TT):
                out = c.banks[:, 1, t * E:(t + 1) * E]
                for b in range(t):
                    nc.tensor.matmul(out, c.ones[:], member[:, b, :], start=(b == 0), stop=False)
                nc.tensor.matmul(out, c.upper_strict[:], member[:, t, :], start=(t == 0), stop=True)
            for b in range(TT):
                last = nc.tensor.matmul(c.banks[:, 1, TT * E:(TT + 1) * E], c.ones[:], member[:, b, :], start=(b == 0),
                                        stop=(b == TT - 1))
            last.then_inc(c.products.sem, 1)

        @block.scalar
        def _(act):
            act.wait_ge(c.dve_done.sem, c.dve_done.at(1))
            for t in range(TT):
                last = nc.scalar.activation(gates[:, t, :], top[:, t, 0:TOPK], ACT.Exp, bias=neg[:, t:t + 1],
                                            accum_out=total[:, t:t + 1])
            last.then_inc(c.act_done.sem, 1)

        @block.vector
        def _(dve):
            dve.wait_ge(c.loaded.sem, c.loaded.at(2))
            dve.wait_ge(c.pool_ready.sem, c.pool_ready.at(1))
            nc.vector.tensor_copy(blk[:], blk_i[:])
            nc.vector.tensor_copy(e_id[:], e_int[:])
            dve.wait_ge(c.products.sem, c.products.at(1))
            c.dve(dve, nc.vector.tensor_tensor(logits[:], c.banks[:, 0, 0:TT * E].rearrange("p (t e) -> p t e", t=TT),
                                               spread(rb[:], TT), ALU.add))
            for t in range(TT):
                last = nc.vector.max(top[:, t, :], logits[:, t, :])
            c.dve(dve, last)
            nc.vector.tensor_scalar(neg[:], top[:, :, 0], -1.0, None, ALU.mult).then_inc(c.dve_done.sem, 1)
            for t in range(TT):
                last = nc.vector.max_index(top_i[:, t, :], top[:, t, :], logits[:, t, :])
            c.dve(dve, last)
            c.dve(dve, nc.vector.tensor_copy(top_f[:], top_i[:]))
            for t in range(TT):
                for k in range(TOPK):
                    last = nc.vector.tensor_scalar(hot[:, t, k, :], e_id[:], top_f[:, t, k:k + 1], None, ALU.is_equal)
            c.dve(dve, last)
            nc.vector.tensor_reduce(member[:], hot[:].rearrange("p t k e -> p t e k"), AX.X, ALU.add).then_inc(c.dve_done.sem, 1)
            dve.wait_ge(c.act_done.sem, c.act_done.at(1))
            c.dve(dve, nc.vector.reciprocal(total[:], total[:]))
            nc.vector.tensor_tensor(gates[:], gates[:], total[:].unsqueeze(2).broadcast_to([P, TT, TOPK]), ALU.mult)
            dve.wait_ge(c.products.sem, c.products.at(2))
            nc.vector.tensor_copy(rank[:], c.banks[:, 1, 0:TT * E].rearrange("p (t e) -> p t e", t=TT))
            c.dve(dve, nc.vector.tensor_copy(count[:], c.banks[:, 1, TT * E:(TT + 1) * E]))
            c.dve(dve, nc.vector.tensor_scalar(extra[:, 0, :], count[:], float(CAP), None, ALU.is_gt))
            for m in range(2, SEQ // CAP):
                c.dve(dve, nc.vector.tensor_scalar(extra[:, 1, :], count[:], float(m * CAP), None, ALU.is_gt))
                c.dve(dve, nc.vector.tensor_tensor(extra[:, 0, :], extra[:, 0, :], extra[:, 1, :], ALU.add))
            c.dve(dve, nc.vector.tensor_tensor_scan(cum[:], c.ones[:, 0:E], extra[:, 0, :], 0.0, ALU.mult, ALU.add))
            c.dve(dve, nc.vector.tensor_tensor(first[:], cum[:], extra[:, 0, :], ALU.subtract))
            c.dve(dve, nc.vector.scalar_tensor_tensor(out=first[:], in0=first[:], scalar=float(E - 1), in1=e_id[:],
                                                      op0=ALU.add, op1=ALU.subtract))
            c.dve(dve, nc.vector.tensor_scalar(over[:], rank[:], float(CAP), None, ALU.is_ge))
            c.dve(dve, nc.vector.tensor_tensor(over[:], over[:], spread(first[:], TT), ALU.mult))
            c.dve(dve, nc.vector.tensor_tensor(over[:], over[:], spread(e_id[:], TT), ALU.add))
            c.dve(dve, nc.vector.scalar_tensor_tensor(out=rank[:], in0=over[:], scalar=float(CAP), in1=rank[:],
                                                      op0=ALU.mult, op1=ALU.add))
            for k in range(TOPK):
                last = nc.vector.tensor_tensor(hot[:, :, k, :], hot[:, :, k, :], rank[:], ALU.mult)
            c.dve(dve, last)
            c.dve(dve, nc.vector.tensor_reduce(dest[:], hot[:], AX.X, ALU.add))
            nc.vector.tensor_copy(slots[:], dest[:])
            for b in range(EXTRA):
                last = nc.vector.tensor_scalar(before_blk[:, b, :], cum[0:1, :], blk[:, b:b + 1], None, ALU.is_le)
            c.dve(dve, last)
            nc.vector.memset(plan_f[:, 0:1], float(E - 1))
            nc.vector.tensor_copy(plan_f[:, 1 + EXTRA:2 + EXTRA], cum[0:1, E - 1:E])
            c.dve(dve, nc.vector.tensor_reduce(plan_f[:, 1:1 + EXTRA], before_blk[:], AX.X, ALU.add))
            c.dve(dve, nc.vector.tensor_scalar(plan_f[:, 1:1 + EXTRA], plan_f[:, 1:1 + EXTRA], float(E - 1), None, ALU.min))
            nc.vector.tensor_copy(plan[:], plan_f[:])

    c.loaded.passed(2)
    c.stored.passed(2)
    c.pool_ready.passed(1)
    c.products.passed(2)
    c.dve_done.passed(2)
    c.act_done.passed(1)
    with nc.Block("fill_slots") as block:

        @block.gpsimd
        def _(pool):
            for t in range(TT):
                for k in range(TOPK):
                    nc.gpsimd.indirect_dma_start(slot_tok, bass.IndirectOffsetOnAxis(slots[:, t, k:k + 1], 0),
                                                 token_id[:, t:t + 1], None).then_inc(c.gathered.sem, 16)
            pool.wait_ge(c.gathered.sem, c.gathered.at(TT * TOPK))

    c.gathered.passed(TT * TOPK)
    return h_rows, slot_tok


def load_expert_chunk(c, A, engine, e, ch):
    if ch < 8:
        half, k = ch // 4, 2 * (ch % 4)
        src = A["exp_w1_2"].rearrange("a e (k p) n -> (a e) p k n", p=P)[bass.ds(e, 1), :, k:k + 2, half * FF:(half + 1) * FF]
    else:
        k = 2 * (ch - 8)
        src = A["exp_w2_2"].rearrange("a e (k p) n -> (a e) p k n", p=P)[bass.ds(e, 1), :, k:k + 2, :]
    engine.dma_start(c.raw[:, ch % RAW, :].rearrange("p (k n) -> p k n", k=2),
                     src.rearrange("o p k n -> p (o k) n")).then_inc(c.landed[ch].sem, 16)


def experts(c, A, h, h_rows, slot_tok, bias_rows, plan, Y):
    nc = c.nc
    HALF = FF // 2
    with ExitStack() as ctx:
        def sb(name, shape, dt=F32):
            return ctx.enter_context(nc.sbuf_tensor(name, shape, dt))

        xg, u, ysb = h[:, 0, :], h[:, 1, :], h[:, 2, :]
        ids = sb("block_tokens", [P, 1], I32)
        w_hi, w_lo = sb("weights_hi", [P, SPLIT, RSLOT], F32R), sb("weights_lo", [P, SPLIT, RSLOT], F32R)
        x_hi, x_lo = sb("rows_hi", [P, DT, P], F32R), sb("rows_lo", [P, DT, P], F32R)
        u_hi, u_lo = sb("u_hi", [P, DT, P], F32R), sb("u_lo", [P, DT, P], F32R)
        b1row, b2row = sb("bias_1_row", [3, 2 * FF], BF16), sb("bias_2_row", [3, FF], BF16)
        ones = sb("ones_bf", [3, P], BF16)
        glu, lin, sig = sb("glu", [P, 2, HALF]), sb("lin", [P, 2, HALF]), sb("sig", [P, 2, HALF])
        own = lambda name, step=1: Signal(nc, name, step)
        hi_ready, lo_ready, used = own("hi_ready"), own("lo_ready"), own("chunks_used")
        b1_in, b2_in, b1_used, b2_used = own("b1_in", 16), own("b2_in", 16), own("b1_used"), own("b2_used")
        rows_in, ids_in, fetches = own("rows_in", 16), own("ids_in", 16), own("block_fetches")
        turned_x, turned_u = own("rows_turned"), own("u_turned")
        x_hi_in, x_lo_in, u_hi_in, u_lo_in = own("x_hi_copied"), own("x_lo_copied"), own("u_hi_copied"), own("u_lo_copied")
        glu_ready, lin_ready, product_ready, sig_ready, u_ready = (own("glu_ready"), own("lin_ready"), own("product_ready"),
                                                                   own("sigmoid_ready"), own("u_ready"))
        y_taken, y_stored = own("y_copied"), own("y_stored", 16)
        out_rows = Y.rearrange("(b s) n -> b s n", s=CAP)
        slot_ids = slot_tok.rearrange("(b s) o -> b s o", s=CAP)
        turned_bank = c.banks[:, 4:6, :].rearrange("p b (k s) -> p (b k) s", k=4)
        y_bank = c.banks[:, 6:8, :].rearrange("p b n -> p (b n)")

        def first_chunk(i):
            return i * 12 - 4

        def further(engine, step, last, start=1):
            with engine.Fori(start, E) as i:
                step(i)
            n = engine.value_load(plan[0:1, 1 + EXTRA:2 + EXTRA], min_val=0, max_val=EXTRA)
            with engine.If(n > 0):
                with engine.Fori(0, n) as j:
                    step(engine.snap(j + E))
            last(engine.snap(n + (E - 1)))

        with nc.Block("experts") as block:

            @block.sync
            def _(sp):
                def expert(place):
                    return sp.value_load(plan[0:1, bass.ds(place, 1)], min_val=0, max_val=E - 1)

                def bias_1(e):
                    sp.dma_start(b1row[:], bias_rows[bass.ds(e, 1), :, 0:2 * FF].rearrange("o a n -> (o a) n")).then_inc(b1_in.sem, 16)

                def bias_2(e):
                    sp.dma_start(b2row[:], bias_rows[bass.ds(e, 1), :, 2 * FF:].rearrange("o a n -> (o a) n")).then_inc(b2_in.sem, 16)

                def first_layer(i, e, s0):
                    for k in range(8):
                        if k == 4:
                            sp.wait_ge(b1_used.sem, i)
                            bias_1(e)
                        sp.wait_ge(lo_ready.sem, s0 + k - RAW + 1)
                        load_expert_chunk(c, A, sp, e, k)

                def second_layer(i, e):
                    sp.wait_ge(b2_used.sem, i)
                    bias_2(e)
                    for k in range(4):
                        sp.wait_ge(lo_ready.sem, 12 * i + 16 + k - RAW + 1)
                        load_expert_chunk(c, A, sp, e, 8 + k)

                bias_1(0)
                bias_2(0)
                for k in range(RAW, 8):
                    sp.wait_ge(lo_ready.sem, k - RAW + 1)
                    load_expert_chunk(c, A, sp, 0, k)
                for k in range(8):
                    if k == 4:
                        sp.wait_ge(b1_used.sem, 1)
                        bias_1(1)
                    sp.wait_ge(lo_ready.sem, 7 + k if k < 2 else 8 + k - RAW + 1)
                    load_expert_chunk(c, A, sp, 1, k)
                for k in range(4):
                    sp.wait_ge(lo_ready.sem, 16 + k - RAW + 1)
                    load_expert_chunk(c, A, sp, 0, 8 + k)

                with sp.Fori(2, E) as i:
                    first_layer(i, i, first_chunk(i))
                    second_layer(i - 1, i - 1)
                n = sp.value_load(plan[0:1, 1 + EXTRA:2 + EXTRA], min_val=0, max_val=EXTRA)
                with sp.If(n > 0):
                    with sp.Fori(0, n) as j:
                        first_layer(sp.snap(j + E), expert(j + 1), first_chunk(j + E))
                        second_layer(j + (E - 1), expert(j))
                b = sp.snap(n + (E - 1))
                e = expert(n)
                sp.wait_ge(b2_used.sem, b)
                bias_2(e)
                for k in range(4):
                    sp.wait_ge(lo_ready.sem, b * 12 + 5 + k)
                    load_expert_chunk(c, A, sp, e, 8 + k)

            @block.gpsimd
            def _(pool):
                nc.gpsimd.memset(ones[:], 1.0).then_inc(c.pool_ready.sem, 1)

                def fetch(i):
                    pool.dma_start(ids[:], slot_ids[bass.ds(i, 1), :, :].rearrange("b s o -> (b s) o"),
                                   allow_slow_non_contiguous=True).then_inc(ids_in.sem, 16)
                    pool.wait_ge(ids_in.sem, 16 + i * 16)
                    pool.sem_inc(fetches.sem, 1)
                    nc.gpsimd.indirect_dma_start(xg, None, h_rows, bass.IndirectOffsetOnAxis(ids[:], 0)).then_inc(rows_in.sem, 16)
                    pool.wait_ge(rows_in.sem, 16 + i * 16)

                fetch(0)
                pool.wait_ge(turned_x.sem, 1)
                fetch(1)

                def step(i):
                    pool.wait_ge(turned_x.sem, 1 + i)
                    fetch(i + 1)

                further(pool, step, lambda i: pool.wait_ge(y_stored.sem, 32 + i * 16))

            @block.tensor
            def _(pe):
                def turn(src, done):
                    for k in range(DT):
                        last = nc.tensor.transpose(turned_bank[:, k, :], src[:, k * P:(k + 1) * P], c.ident[:])
                    last.then_inc(done.sem, 1)

                def bias(row, bank, at):
                    for n in range(2):
                        last = nc.tensor.matmul(c.banks[:, bank + n, :], ones[:], row[:, at + n * 512:at + (n + 1) * 512],
                                                start=True, stop=False)
                    return last

                def chunks(bank, hi, lo, s0):
                    for q in range(4):
                        pe.wait_ge(lo_ready.sem, s0 + 1 + q)
                        for kk in range(2):
                            k = 2 * q + kk
                            end = k == DT - 1
                            for left, right, stop in ((hi, w_lo, False), (hi, w_hi, False), (lo, w_hi, end)):
                                for n in range(2):
                                    last = nc.tensor.matmul(c.banks[:, bank + n, :], left[:, k, :],
                                                            right[:, q, kk * FF + n * 512:kk * FF + (n + 1) * 512],
                                                            start=False, stop=stop)
                        last.then_inc(used.sem, 1)

                def first_layer(i, s0, later):
                    pe.wait_ge(x_hi_in.sem, 1 + i)
                    pe.wait_ge(x_lo_in.sem, 1 + i)
                    pe.wait_ge(b1_in.sem, 16 + i * 16)
                    for half in range(2):
                        if later:
                            pe.wait_ge(lin_ready.sem, i * 2 + half - 1)
                        last = bias(b1row, 2 * half, half * FF)
                        if half:
                            last.then_inc(b1_used.sem, 1)
                        chunks(2 * half, x_hi, x_lo, s0 + 4 * half)

                def turn_next_rows(i, later):
                    pe.wait_ge(rows_in.sem, 32 + i * 16)
                    if later:
                        pe.wait_ge(u_hi_in.sem, i)
                        pe.wait_ge(u_lo_in.sem, i)
                    turn(xg, turned_x)

                def turn_own_u(i):
                    pe.wait_ge(u_ready.sem, 2 + i * 2)
                    pe.wait_ge(x_hi_in.sem, 2 + i)
                    pe.wait_ge(x_lo_in.sem, 2 + i)
                    turn(u, turned_u)

                def second_layer(i, s0):
                    pe.wait_ge(y_taken.sem, i)
                    pe.wait_ge(u_hi_in.sem, i)
                    pe.wait_ge(u_lo_in.sem, i)
                    pe.wait_ge(b2_in.sem, i * 16)
                    bias(b2row, 6, 0).then_inc(b2_used.sem, 1)
                    chunks(6, u_hi, u_lo, s0)

                pe.wait_ge(c.pool_ready.sem, c.pool_ready.at(1))
                pe.wait_ge(rows_in.sem, 16)
                turn(xg, turned_x)
                pe.sem_inc(y_taken.sem, 1)
                first_layer(0, 0, False)
                turn_next_rows(0, False)
                turn_own_u(0)

                def step(i):
                    first_layer(i, first_chunk(i), True)
                    turn_next_rows(i, True)
                    second_layer(i, first_chunk(i) + 8)
                    turn_own_u(i)

                further(pe, step, lambda i: second_layer(pe.snap(i + 1), i * 12 + 8))

            @block.vector
            def _(dve):
                def low(ch, s):
                    dve.wait_ge(hi_ready.sem, 1 + s)
                    nc.vector.tensor_tensor(w_lo[:, ch % SPLIT, :], c.raw[:, ch % RAW, :], w_hi[:, ch % SPLIT, :],
                                            ALU.subtract).then_inc(lo_ready.sem, 1)

                def swiglu(i, half, s0, later):
                    dve.wait_ge(used.sem, s0 + 4 * (half + 1))
                    pair = c.banks[:, 2 * half:2 * half + 2, :].rearrange("p b (n two) -> p (b n) two", two=2)
                    nc.vector.tensor_scalar(glu[:, half, :], pair[:, :, 0], LIMIT, None, ALU.min).then_inc(glu_ready.sem, 1)
                    nc.vector.tensor_scalar(lin[:, half, :], pair[:, :, 1], LIMIT, -LIMIT, ALU.min, ALU.max).then_inc(lin_ready.sem, 1)
                    dve.wait_ge(glu_ready.sem, 1 + half + i * 2)
                    dve.wait_ge(lin_ready.sem, 1 + half + i * 2)
                    nc.vector.scalar_tensor_tensor(out=lin[:, half, :], in0=lin[:, half, :], scalar=1.0,
                                                   in1=glu[:, half, :], op0=ALU.add, op1=ALU.mult).then_inc(product_ready.sem, 1)
                    dve.wait_ge(product_ready.sem, 1 + half + i * 2)
                    dve.wait_ge(sig_ready.sem, 1 + half + i * 2)
                    if later:
                        dve.wait_ge(turned_u.sem, i)
                    nc.vector.tensor_tensor(u[:, half * HALF:(half + 1) * HALF], lin[:, half, :], sig[:, half, :],
                                            ALU.mult).then_inc(u_ready.sem, 1)

                def low_rows(i):
                    dve.wait_ge(x_hi_in.sem, 1 + i)
                    nc.vector.tensor_tensor(x_lo[:], turned_bank, x_hi[:], ALU.subtract).then_inc(x_lo_in.sem, 1)

                def low_u(i):
                    dve.wait_ge(u_hi_in.sem, 1 + i)
                    nc.vector.tensor_tensor(u_lo[:], turned_bank, u_hi[:], ALU.subtract).then_inc(u_lo_in.sem, 1)

                low_rows(0)
                for k in range(7):
                    low(k, k)
                swiglu(0, 0, 0, False)
                low(7, 7)
                swiglu(0, 1, 0, False)
                low_rows(1)

                def step(i):
                    s0 = first_chunk(i)
                    for k in range(4):
                        low(k, s0 + k)
                    low_u(i - 1)
                    for k in range(4, 7):
                        low(k, s0 + k)
                    swiglu(i, 0, s0, True)
                    for k in range(7, 11):
                        low(k, s0 + k)
                    swiglu(i, 1, s0, True)
                    low(11, s0 + 11)
                    low_rows(i + 1)

                def last(i):
                    low_u(i)
                    for k in range(4):
                        low(8 + k, i * 12 + 8 + k)

                further(dve, step, last)

            @block.scalar
            def _(act):
                def high(ch, s, landed, later):
                    act.wait_ge(c.landed[ch].sem, landed)
                    if later:
                        act.wait_ge(used.sem, s - SPLIT + 1)
                    nc.scalar.activation(w_hi[:, ch % SPLIT, :], c.raw[:, ch % RAW, :], ACT.Copy).then_inc(hi_ready.sem, 1)

                def sigmoid(i, half):
                    act.wait_ge(glu_ready.sem, 1 + half + i * 2)
                    nc.scalar.activation(sig[:, half, :], glu[:, half, :], ACT.Sigmoid, scale=SW_ALPHA).then_inc(sig_ready.sem, 1)

                def high_rows(i):
                    act.wait_ge(turned_x.sem, 1 + i)
                    nc.scalar.activation(x_hi[:], turned_bank, ACT.Copy).then_inc(x_hi_in.sem, 1)

                def high_u(i):
                    act.wait_ge(turned_u.sem, 1 + i)
                    nc.scalar.activation(u_hi[:], turned_bank, ACT.Copy).then_inc(u_hi_in.sem, 1)

                def put_y(b, finished):
                    act.wait_ge(used.sem, finished)
                    act.wait_ge(y_stored.sem, 16 + b * 16)
                    nc.scalar.activation(ysb, y_bank, ACT.Copy).then_inc(y_taken.sem, 1)
                    act.wait_ge(y_taken.sem, 2 + b)
                    act.dma_start(out_rows[bass.ds(b, 1), :, :].rearrange("b s n -> (b s) n"), ysb).then_inc(y_stored.sem, 16)

                act.wait_ge(c.zero_filled.sem, 16 * (D // 256))
                landed = lambda ch, i: c.landed[ch].base + 16 + i * 16
                high_rows(0)
                for k in range(8):
                    high(k, k, landed(k, 0), k >= SPLIT)
                    if k == 6:
                        sigmoid(0, 0)
                sigmoid(0, 1)
                high_rows(1)

                act.sem_inc(y_stored.sem, 16)

                def step(i, any_y=True):
                    s0 = first_chunk(i)
                    for k in range(4):
                        high(k, s0 + k, landed(k, i), True)
                    if any_y:
                        put_y(i - 2, s0)
                    high_u(i - 1)
                    for k in range(4, 7):
                        high(k, s0 + k, landed(k, i), True)
                    sigmoid(i, 0)
                    high(7, s0 + 7, landed(7, i), True)
                    for k in range(8, 11):
                        high(k, s0 + k, landed(k, i - 1), True)
                    sigmoid(i, 1)
                    high(11, s0 + 11, landed(11, i - 1), True)
                    high_rows(i + 1)

                def last(i):
                    put_y(i - 1, first_chunk(i) + 12)
                    high_u(i)
                    for k in range(8, 12):
                        high(k, i * 12 + k, landed(k, i), True)
                    put_y(i, i * 12 + 12)

                step(1, False)
                further(act, step, last, 2)

        c.pool_ready.passed(1)


def combine(c, A, h, Y, gates, slots, part, out):
    nc = c.nc
    c.far.close()
    rows = c.far.enter_context(nc.sbuf_tensor("gathered_rows", [P, TT, TOPK, D], F32, side="right"))
    came = [Signal(nc, f"rows_of_tile_{t}", 16) for t in range(TT)]
    with nc.sbuf_tensor("final_vectors", [P, 3, D], F32) as vec:
        with nc.Block("combine") as block:

            @block.sync
            def _(sp):
                sp.dma_start(vec[:, 2, :], over_partitions(part(5), D)).then_inc(c.final_loaded.sem, 16)
                sp.wait_ge(c.final_loaded.sem, c.final_loaded.at(1))

            @block.gpsimd
            def _(pool):
                for t in range(TT):
                    for k in range(TOPK):
                        nc.gpsimd.indirect_dma_start(rows[:, t, k, :], None, Y,
                                                     bass.IndirectOffsetOnAxis(slots[:, t, k:k + 1], 0)).then_inc(came[t].sem, 16)

            @block.vector
            def _(dve):
                dve.wait_ge(c.final_loaded.sem, c.final_loaded.at(1))
                for t in range(TT):
                    dve.wait_ge(came[t].sem, 16 * TOPK)
                    acc = h[:, t, :]
                    c.dve(dve, nc.vector.tensor_scalar(acc, rows[:, t, 0, :], gates[:, t, 0:1], None, ALU.mult))
                    for k in range(1, TOPK):
                        c.dve(dve, nc.vector.scalar_tensor_tensor(out=acc, in0=rows[:, t, k, :], scalar=gates[:, t, k:k + 1],
                                                                  in1=acc, op0=ALU.mult, op1=ALU.add))
                    c.dve(dve, nc.vector.scalar_tensor_tensor(out=acc, in0=vec[:, 2, :], scalar=1.0, in1=acc,
                                                              op0=ALU.add, op1=ALU.mult))
                    nc.vector.scalar_tensor_tensor(out=acc, in0=c.x[:, t, :], scalar=ALPHA, in1=acc, op0=ALU.mult, op1=ALU.add)

        layer_norm(c, "norm_2", lambda t: h[:, t, :], lambda t: c.x[:, t, :],
                   [(vec[:, 0, :], A["ln2_g_2"].rearrange("a n -> (a n)")), (vec[:, 1, :], A["ln2_b_2"].rearrange("a n -> (a n)"))],
                   lambda dve, t: None)
    with nc.Block("store") as block:

        @block.sync
        def _(sp):
            sp.dma_start(out.rearrange("a (t p) d -> p (a t) d", p=P), c.x[:]).then_inc(c.final_stored.sem, 16)
            sp.wait_ge(c.final_stored.sem, 16)


def hybrid_then_moe(nc, A, out):
    with ExitStack() as ctx:
        c = Core(nc, ctx)
        Y = nc.dram_tensor("slot_outputs", [SLOTS, D], F32).ap()
        ctx.callback(c.far.close)
        mod = nc.dram_tensor("mod_scratch", [6 * D], F32).ap()
        bias_rows = nc.dram_tensor("bias_parts", [E, 3, 3 * FF], BF16).ap()
        constants(c, A, bias_rows)
        first_block(c, A, mod, Y)
        second_block(c, A, mod, bias_rows, Y, out)


_INS = ["x", "norm_g", "w_in", "b_gates", "conv_w", "w_alpha", "b_alpha", "ml_norm_g", "gla_norm_g", "w_out",
        "final_g", "c_2", "positions_2", "emb_ln_g_2", "emb_ln_b_2", "ada_w_2", "ada_b_2", "w_in_2", "q_norm_g_2",
        "w_uq_2", "kv_norm_g_2", "w_uk_2", "w_uv_2", "mla_out_g_2", "rwkv_mu_2", "rwkv_w0_2", "rwkv_w2_2",
        "rwkv_a0_2", "rwkv_a2_2", "rwkv_g2_2", "rwkv_k_k_2", "rwkv_k_a_2", "rwkv_r_k_2", "rwkv_gn_g_2",
        "rwkv_gn_b_2", "w_o_2", "ln1_g_2", "ln1_b_2", "router_w_2", "router_b_2", "exp_w1_2", "exp_b1_2",
        "exp_w2_2", "exp_b2_2", "ln2_g_2", "ln2_b_2"]


def kernel(**inputs):
    import concourse.bacc as bacc
    from concourse.bass_utils import run_bass_kernel_spmd

    arrays = {name: np.ascontiguousarray(inputs[name]) for name in _INS}
    distance = np.arange(P)[:, None] + (SEQ - P) - np.arange(SEQ)[None, :]
    table = np.asarray(inputs["rel_bias"])[0]
    arrays["rel_rows"] = np.ascontiguousarray(table[:, np.clip(distance, -REL, REL) + REL])
    arrays["inv_freq"] = (10000.0 ** (-np.arange(0, ROPE, 2, dtype=np.float32) / np.float32(ROPE))).astype(np.float32)

    nc = bacc.Bacc("TRN2", target_bir_lowering=False, num_devices=1)
    A = {name: nc.dram_tensor(f"in_{name}", a.shape, mybir.dt.from_np(a.dtype), kind="ExternalInput").ap()
         for name, a in arrays.items()}
    out = nc.dram_tensor("out", (1, SEQ, D), F32, kind="ExternalOutput").ap()
    hybrid_then_moe(nc, A, out)
    result = run_bass_kernel_spmd(nc, [{f"in_{name}": a for name, a in arrays.items()}], core_ids=[0])
    return result.results[0]["out"]
```
